# Optimizing a Trainium2 kernel written in Bass

```python
import jax, jax.numpy as jnp
from jax import lax
import numpy as np
import math
import jax
import jax.numpy as jnp

D_MODEL = 1024
BATCH = 1
SEQ = 256
DEPTH = 2

CHUNK = 64
SGU_GROUPS = 4
SGU_GROUP_DIM = 64
SGU_WIDTH = SGU_GROUPS * SGU_GROUP_DIM
SGU_BLOCK = 128
RET_HEADS = 4
RET_KDIM = 64
RET_VDIM = 64
POOL_WINDOWS = (2, 4, 8, 16)
POOL_GROUP_DIM = 64
POOL_WIDTH = 4 * POOL_GROUP_DIM
MLA_HEADS = 4
MLA_Q_RANK = 256
MLA_KV_RANK = 128
MLA_NOPE_DIM = 64
MLA_ROPE_DIM = 32
MLA_V_DIM = 64
Q_BLOCK = 128
ROPE_BASE = 10000.0
N_BRANCH = 4
BRANCH_WIDTH = 256
D_FF = 2816
PLE_DIM = 256
ALPHA = (2 * DEPTH) ** 0.25
BETA = (8 * DEPTH) ** -0.25
LN_EPS = 1e-5
RMS_EPS = 1e-6
GN_EPS = 1e-5
IN_SIZES = (SGU_WIDTH, SGU_WIDTH,
            RET_HEADS * RET_KDIM, RET_HEADS * RET_KDIM, RET_HEADS * RET_VDIM, RET_HEADS * RET_VDIM,
            POOL_WIDTH,
            MLA_Q_RANK, MLA_KV_RANK, MLA_ROPE_DIM,
            N_BRANCH * D_MODEL)
IN_COLS = sum(IN_SIZES)


def _split(h, sizes):
    parts, start = [], 0
    for size in sizes:
        parts.append(h[..., start:start + size])
        start += size
    return parts

def layer_norm(x, g, b):
    xf = x.astype(jnp.float32)
    mu = jnp.mean(xf, axis=-1, keepdims=True)
    var = jnp.mean(jnp.square(xf - mu), axis=-1, keepdims=True)
    y = (xf - mu) * lax.rsqrt(var + LN_EPS) * g.astype(jnp.float32) + b.astype(jnp.float32)
    return y.astype(x.dtype)

def rms_norm(x, g):
    xf = x.astype(jnp.float32)
    y = xf * lax.rsqrt(jnp.mean(jnp.square(xf), axis=-1, keepdims=True) + RMS_EPS) * g.astype(jnp.float32)
    return y.astype(x.dtype)

def rope_tables(positions, dim):
    inv_freq = ROPE_BASE ** (-jnp.arange(0, dim, 2, dtype=jnp.float32) / dim)
    ang = positions.astype(jnp.float32)[..., None] * inv_freq
    return jnp.cos(ang), jnp.sin(ang)

def apply_rope(x, cos, sin):
    half = x.shape[-1] // 2
    xf = x.astype(jnp.float32)
    x1, x2 = xf[..., :half], xf[..., half:]
    c, s = cos[:, :, None, :], sin[:, :, None, :]
    return jnp.concatenate([x1 * c - x2 * s, x1 * s + x2 * c], axis=-1).astype(x.dtype)

def swiglu(x, w_up, w_down):
    a, b = jnp.split(x @ w_up, 2, axis=-1)
    return (jax.nn.silu(a) * b) @ w_down

def sgu_mixer(u, v, ln_g, ln_b, w_s, b_s):
    bsz, seq, _ = u.shape
    u = jax.nn.gelu(u)
    v = layer_norm(jax.nn.gelu(v), ln_g, ln_b)
    vb = v.reshape(bsz, seq // SGU_BLOCK, SGU_BLOCK, SGU_GROUPS, SGU_GROUP_DIM)
    causal = jnp.tril(jnp.ones((SGU_BLOCK, SGU_BLOCK), dtype=bool))
    w = jnp.where(causal[None], w_s, jnp.zeros_like(w_s))
    mixed = jnp.einsum('gts,bnsgc->bntgc', w, vb) + b_s.T[None, None, :, :, None]
    return u * mixed.reshape(bsz, seq, SGU_WIDTH)

def retention_mixer(q, k, v, g, cos, sin):
    bsz, seq, _ = q.shape
    n_chunks = seq // CHUNK
    f32 = jnp.float32
    q = apply_rope(q.reshape(bsz, seq, RET_HEADS, RET_KDIM), cos, sin).astype(f32)
    k = apply_rope(k.reshape(bsz, seq, RET_HEADS, RET_KDIM), cos, sin).astype(f32) * RET_KDIM ** -0.5
    v = v.reshape(bsz, seq, RET_HEADS, RET_VDIM).astype(f32)
    log_gamma = jnp.log1p(-jnp.exp2(-5.0 - jnp.arange(RET_HEADS, dtype=f32)))
    pos = jnp.arange(CHUNK, dtype=f32)
    intra_decay = jnp.exp(log_gamma[:, None, None] * jnp.abs(pos[:, None] - pos[None, :]))
    key_to_end = jnp.exp(log_gamma[:, None] * (CHUNK - 1 - pos)[None, :])
    start_to_query = jnp.exp(log_gamma[:, None] * (pos + 1)[None, :])
    chunk_decay = jnp.exp(log_gamma * CHUNK)
    qc = q.reshape(bsz, n_chunks, CHUNK, RET_HEADS, RET_KDIM)
    kc = k.reshape(bsz, n_chunks, CHUNK, RET_HEADS, RET_KDIM)
    vc = v.reshape(bsz, n_chunks, CHUNK, RET_HEADS, RET_VDIM)
    scores = jnp.einsum('bnihd,bnjhd->bnhij', qc, kc) * intra_decay
    y = jnp.einsum('bnhij,bnjhe->bnihe', scores, vc)
    kv = jnp.einsum('bnjhd,hj,bnjhe->nbhde', kc, key_to_end, vc)

    def step(state, kv_chunk):
        return state * chunk_decay[None, :, None, None] + kv_chunk, state

    _, prev = lax.scan(step, jnp.zeros((bsz, RET_HEADS, RET_KDIM, RET_VDIM), f32), kv)
    y = y + jnp.einsum('bnihd,nbhde,hi->bnihe', qc, prev, start_to_query)
    y = y.reshape(bsz, seq, RET_HEADS, RET_VDIM)
    mu = jnp.mean(y, axis=-1, keepdims=True)
    var = jnp.mean(jnp.square(y - mu), axis=-1, keepdims=True)
    y = (y - mu) * lax.rsqrt(var + GN_EPS)
    return (jax.nn.silu(g.astype(f32)) * y.reshape(bsz, seq, RET_HEADS * RET_VDIM)).astype(g.dtype)

def pool_mixer(z, w_pool, scale):
    bsz, seq, _ = z.shape
    zf = z.astype(jnp.float32)
    csum = jnp.concatenate([jnp.zeros((bsz, 1, POOL_WIDTH), jnp.float32), jnp.cumsum(zf, axis=1)], axis=1)
    t = jnp.arange(seq)
    groups = []
    for gi, window in enumerate(POOL_WINDOWS):
        ch = slice(gi * POOL_GROUP_DIM, (gi + 1) * POOL_GROUP_DIM)
        lo = jnp.maximum(t + 1 - window, 0)
        count = (t + 1 - lo).astype(jnp.float32)[None, :, None]
        mean = (csum[:, 1:, ch] - csum[:, lo, ch]) / count
        groups.append(mean - zf[:, :, ch])
    pooled = jnp.stack(groups, axis=2).astype(z.dtype)
    y = jnp.einsum('bsgc,gcd->bsgd', pooled, w_pool).reshape(bsz, seq, POOL_WIDTH)
    return y * scale

def mla_mixer(c_q, c_kv, k_rope, q_norm_g, kv_norm_g, w_uq, w_ukv, cos, sin):
    bsz, seq, _ = c_q.shape
    qk_dim = MLA_NOPE_DIM + MLA_ROPE_DIM
    q = (rms_norm(c_q, q_norm_g) @ w_uq).reshape(bsz, seq, MLA_HEADS, qk_dim)
    kv = (rms_norm(c_kv, kv_norm_g) @ w_ukv).reshape(bsz, seq, MLA_HEADS, MLA_NOPE_DIM + MLA_V_DIM)
    k_nope, v = kv[..., :MLA_NOPE_DIM], kv[..., MLA_NOPE_DIM:]
    q = jnp.concatenate([q[..., :MLA_NOPE_DIM], apply_rope(q[..., MLA_NOPE_DIM:], cos, sin)], axis=-1) * qk_dim ** -0.5
    k_pe = apply_rope(k_rope[:, :, None, :], cos, sin)
    k = jnp.concatenate([k_nope, jnp.broadcast_to(k_pe, (bsz, seq, MLA_HEADS, MLA_ROPE_DIM))], axis=-1)
    n_blocks = seq // Q_BLOCK
    q_blocks = jnp.moveaxis(q.reshape(bsz, n_blocks, Q_BLOCK, MLA_HEADS, qk_dim), 1, 0)
    key_chunk = jnp.arange(seq) // CHUNK

    def attend(args):
        q_blk, blk = args
        query_chunk = (blk * Q_BLOCK + jnp.arange(Q_BLOCK)) // CHUNK
        s = jnp.einsum('bqhd,bkhd->bhqk', q_blk, k).astype(jnp.float32)
        s = jnp.where(key_chunk[None, :] <= query_chunk[:, None], s, -jnp.inf)
        probs = jax.nn.softmax(s, axis=-1).astype(v.dtype)
        return jnp.einsum('bhqk,bkhe->bqhe', probs, v)

    out = lax.map(attend, (q_blocks, jnp.arange(n_blocks)))
    return jnp.moveaxis(out, 0, 1).reshape(bsz, seq, MLA_HEADS * MLA_V_DIM)

def token_mix(x, w_in, sgu_ln_g, sgu_ln_b, sgu_w, sgu_b, pool_w, pool_scale,
              mla_q_norm, mla_kv_norm, mla_w_uq, mla_w_ukv, w_branch, w_out,
              ret_cos, ret_sin, mla_cos, mla_sin):
    bsz, seq, dm = x.shape
    (sgu_u, sgu_v, ret_q, ret_k, ret_v, ret_g, pool_in,
     c_q, c_kv, k_rope, gate_logits) = _split(x @ w_in, IN_SIZES)
    ys = (sgu_mixer(sgu_u, sgu_v, sgu_ln_g, sgu_ln_b, sgu_w, sgu_b).astype(x.dtype),
          retention_mixer(ret_q, ret_k, ret_v, ret_g, ret_cos, ret_sin).astype(x.dtype),
          pool_mixer(pool_in, pool_w, pool_scale).astype(x.dtype),
          mla_mixer(c_q, c_kv, k_rope, mla_q_norm, mla_kv_norm, mla_w_uq, mla_w_ukv, mla_cos, mla_sin).astype(x.dtype))
    gates = jax.nn.sigmoid(gate_logits).reshape(bsz, seq, N_BRANCH, dm)
    merged = gates[:, :, 0] * (ys[0] @ w_branch[0])
    for n in range(1, N_BRANCH):
        merged = merged + gates[:, :, n] * (ys[n] @ w_branch[n])
    return merged @ w_out

def first_inputs(seed: int = 0) -> dict:
    key = jax.random.key(seed)
    ks = jax.random.split(key, 32)

    def nrm(k, shape, scale):
        return jax.random.normal(k, shape, jnp.float32) * scale

    def gain(k, shape):
        return 1.0 + 0.05 * jax.random.normal(k, shape, jnp.float32)

    def bias(k, shape):
        return 0.02 * jax.random.normal(k, shape, jnp.float32)

    offset = jax.random.randint(ks[2], (BATCH, 1), 0, 64, dtype=jnp.int32) * CHUNK
    positions = (offset + jnp.arange(SEQ, dtype=jnp.int32)[None, :]).astype(jnp.int32)
    L, D = DEPTH, D_MODEL
    return {
        'x': nrm(ks[0], (BATCH, SEQ, D), 1.0),
        'p': nrm(ks[1], (DEPTH, BATCH, SEQ, PLE_DIM), 1.0),
        'positions': positions,
        'ffn1_up': nrm(ks[3], (L, D, 2 * D_FF), D ** -0.5),
        'ffn1_down': nrm(ks[4], (L, D_FF, D), BETA * D_FF ** -0.5),
        'ln1_g': gain(ks[5], (L, D)),
        'ln1_b': bias(ks[6], (L, D)),
        'w_in': nrm(ks[7], (L, D, IN_COLS), D ** -0.5),
        'sgu_ln_g': gain(ks[8], (L, SGU_WIDTH)),
        'sgu_ln_b': bias(ks[9], (L, SGU_WIDTH)),
        'sgu_w': nrm(ks[10], (L, SGU_GROUPS, SGU_BLOCK, SGU_BLOCK), SGU_BLOCK ** -0.5),
        'sgu_b': 1.0 + 0.1 * jax.random.normal(ks[11], (L, SGU_GROUPS, SGU_BLOCK), jnp.float32),
        'pool_w': nrm(ks[12], (L, 4, POOL_GROUP_DIM, POOL_GROUP_DIM), POOL_GROUP_DIM ** -0.5),
        'pool_scale': gain(ks[13], (L, POOL_WIDTH)),
        'mla_q_norm': gain(ks[14], (L, MLA_Q_RANK)),
        'mla_kv_norm': gain(ks[15], (L, MLA_KV_RANK)),
        'mla_w_uq': nrm(ks[16], (L, MLA_Q_RANK, MLA_HEADS * (MLA_NOPE_DIM + MLA_ROPE_DIM)), MLA_Q_RANK ** -0.5),
        'mla_w_ukv': nrm(ks[17], (L, MLA_KV_RANK, MLA_HEADS * (MLA_NOPE_DIM + MLA_V_DIM)), MLA_KV_RANK ** -0.5),
        'w_branch': nrm(ks[18], (L, N_BRANCH, BRANCH_WIDTH, D), BRANCH_WIDTH ** -0.5),
        'w_out': nrm(ks[19], (L, D, D), BETA * D ** -0.5),
        'ln2_g': gain(ks[20], (L, D)),
        'ln2_b': bias(ks[21], (L, D)),
        'ffn2_up': nrm(ks[22], (L, D, 2 * D_FF), D ** -0.5),
        'ffn2_down': nrm(ks[23], (L, D_FF, D), BETA * D_FF ** -0.5),
        'w_ple_gate': nrm(ks[24], (L, D, D), D ** -0.5),
        'w_ple': nrm(ks[25], (L, PLE_DIM, D), PLE_DIM ** -0.5),
        'ln3_g': gain(ks[26], (L, D)),
        'ln3_b': bias(ks[27], (L, D)),
    }

def first_block(x, p, positions, ffn1_up, ffn1_down, ln1_g, ln1_b, w_in, sgu_ln_g, sgu_ln_b,
              sgu_w, sgu_b, pool_w, pool_scale, mla_q_norm, mla_kv_norm, mla_w_uq, mla_w_ukv,
              w_branch, w_out, ln2_g, ln2_b, ffn2_up, ffn2_down, w_ple_gate, w_ple, ln3_g, ln3_b):
    ret_cos, ret_sin = rope_tables(positions, RET_KDIM)
    mla_cos, mla_sin = rope_tables(positions, MLA_ROPE_DIM)
    for i in range(DEPTH):
        x = layer_norm(ALPHA * x + 0.5 * swiglu(x, ffn1_up[i], ffn1_down[i]), ln1_g[i], ln1_b[i])
        mix = token_mix(x, w_in[i], sgu_ln_g[i], sgu_ln_b[i], sgu_w[i], sgu_b[i], pool_w[i], pool_scale[i],
                        mla_q_norm[i], mla_kv_norm[i], mla_w_uq[i], mla_w_ukv[i], w_branch[i], w_out[i],
                        ret_cos, ret_sin, mla_cos, mla_sin)
        x = layer_norm(ALPHA * x + mix, ln2_g[i], ln2_b[i])
        ple = jax.nn.sigmoid(x @ w_ple_gate[i]) * (p[i] @ w_ple[i])
        x = layer_norm(ALPHA * x + 0.5 * swiglu(x, ffn2_up[i], ffn2_down[i]) + ple, ln3_g[i], ln3_b[i])
    return x


DEPTH_2 = 1

LRU_WIDTH = 512
LRU_BLOCKS = 8
LRU_BD = LRU_WIDTH // LRU_BLOCKS
LRU_C = 8.0
CONV_W = 4
DIFF_HEADS = 4
DIFF_HD = 64
DIFF_QBLK = 128
SWA_HEADS = 8
SWA_KV_HEADS = 2
SWA_GROUP = SWA_HEADS // SWA_KV_HEADS
SWA_HD = 64
WINDOW = 128
SWA_BLK = WINDOW
N_BRANCHES = 3
BRANCH_WIDTH_2 = 512
REL_BUCKETS = 32
REL_MAX_DIST = 128
N_ATTN_HEADS = DIFF_HEADS + SWA_HEADS
N_EXPERTS = 32
TOP_K = 4
D_FF_2 = 1024
SWIGLU_LIMIT = 7.0
SWIGLU_ALPHA = 1.702
MOE_BLK = 128
NORM_EPS = 1e-6
NEG_INF = -1e30

IN_SPLITS = (LRU_WIDTH, LRU_WIDTH,
             DIFF_HEADS * 2 * DIFF_HD, DIFF_HEADS * 2 * DIFF_HD, DIFF_HEADS * 2 * DIFF_HD,
             SWA_HEADS * SWA_HD, SWA_KV_HEADS * SWA_HD, SWA_KV_HEADS * SWA_HD,
             N_BRANCHES * D_MODEL)
IN_WIDTH = sum(IN_SPLITS)


def rms_norm_2(x, gain):
    xf = x.astype(jnp.float32)
    y = xf * lax.rsqrt(jnp.mean(xf * xf, axis=-1, keepdims=True) + NORM_EPS)
    return (y * gain.astype(jnp.float32)).astype(x.dtype)

def t5_bucket(dist):
    exact = REL_BUCKETS // 2
    is_small = dist < exact
    log_ratio = jnp.log(jnp.maximum(dist, 1).astype(jnp.float32) / exact) / math.log(REL_MAX_DIST / exact)
    large = exact + (log_ratio * (REL_BUCKETS - exact)).astype(jnp.int32)
    return jnp.where(is_small, dist, jnp.minimum(large, REL_BUCKETS - 1))

def rglru_branch(xr, gr, conv_w, conv_b, wa, ba, wx, bx, lam):
    B, S, C = xr.shape
    xp = jnp.pad(xr, ((0, 0), (CONV_W - 1, 0), (0, 0)))
    xc = conv_b + sum(xp[:, tap:tap + S] * conv_w[tap] for tap in range(CONV_W))
    xh = xc.reshape(B, S, LRU_BLOCKS, LRU_BD)
    gate_a = jnp.einsum('bshi,hij->bshj', xh, wa).reshape(B, S, C) + ba
    gate_x = jnp.einsum('bshi,hij->bshj', xh, wx).reshape(B, S, C) + bx
    r = jax.nn.sigmoid(gate_a.astype(jnp.float32))
    i = jax.nn.sigmoid(gate_x.astype(jnp.float32))
    log_a = -LRU_C * r * jax.nn.softplus(-lam.astype(jnp.float32))
    a = jnp.exp(log_a)
    mult = jnp.sqrt(-jnp.expm1(2.0 * log_a))
    b = xc.astype(jnp.float32) * i * mult

    def combine(left, right):
        a1, b1 = left
        a2, b2 = right
        return a1 * a2, a2 * b1 + b2

    _, h = lax.associative_scan(combine, (a, b), axis=1)
    return (h * jax.nn.gelu(gr.astype(jnp.float32), approximate=True)).astype(xr.dtype)

def diff_attention(q, k, v, q_gain, k_gain, lam_vecs, subln_gain, bias_table, lambda_init):
    B, S = q.shape[:2]
    nb = S // DIFF_QBLK
    q = rms_norm_2(q, q_gain)
    k = rms_norm_2(k, k_gain)
    lv = lam_vecs.astype(jnp.float32)
    lam = jnp.exp(jnp.sum(lv[0] * lv[1])) - jnp.exp(jnp.sum(lv[2] * lv[3])) + lambda_init
    bias_by_dist = bias_table[t5_bucket(jnp.arange(S))][:, :DIFF_HEADS].astype(jnp.float32)
    k_pos = jnp.arange(S)
    q_blocks = jnp.moveaxis(q.reshape(B, nb, DIFF_QBLK, DIFF_HEADS, 2, DIFF_HD), 1, 0)

    def attend_block(args):
        q_blk, blk = args
        dist = (blk * DIFF_QBLK + jnp.arange(DIFF_QBLK))[:, None] - k_pos[None, :]
        bias = jnp.moveaxis(bias_by_dist[jnp.maximum(dist, 0)], -1, 0)
        s = jnp.einsum('bqhmd,bkhmd->bhmqk', q_blk, k).astype(jnp.float32) * DIFF_HD ** -0.5
        s = jnp.where(dist >= 0, s + bias[None, :, None], NEG_INF)
        p = jax.nn.softmax(s, axis=-1)
        attn = (p[:, :, 0] - lam * p[:, :, 1]).astype(v.dtype)
        return jnp.einsum('bhqk,bkhe->bqhe', attn, v)

    o = lax.map(attend_block, (q_blocks, jnp.arange(nb)))
    o = jnp.moveaxis(o, 0, 1).reshape(B, S, DIFF_HEADS, 2 * DIFF_HD)
    o = rms_norm_2(o, subln_gain) * (1.0 - lambda_init)
    return o.reshape(B, S, DIFF_HEADS * 2 * DIFF_HD)

def swa_attention(q, k, v, q_gain, k_gain, sinks, bias_table):
    B, S = q.shape[:2]
    nb = S // SWA_BLK
    q = rms_norm_2(q, q_gain).reshape(B, nb, SWA_BLK, SWA_KV_HEADS, SWA_GROUP, SWA_HD)
    k = rms_norm_2(k, k_gain).reshape(B, nb, SWA_BLK, SWA_KV_HEADS, SWA_HD)
    v = v.reshape(B, nb, SWA_BLK, SWA_KV_HEADS, SWA_HD)

    def band(t):
        prev = jnp.pad(t, ((0, 0), (1, 0), (0, 0), (0, 0), (0, 0)))[:, :-1]
        return jnp.concatenate([prev, t], axis=2)

    k_band, v_band = band(k), band(v)
    qi = jnp.arange(SWA_BLK)[:, None]
    kj = jnp.arange(2 * SWA_BLK)[None, :]
    dist = SWA_BLK + qi - kj
    in_window = (dist >= 0) & (dist < WINDOW)
    has_prev = (jnp.arange(nb) > 0)[:, None, None] | (kj >= SWA_BLK)[None]
    mask = in_window[None] & has_prev
    bias = bias_table[t5_bucket(jnp.clip(dist, 0, WINDOW - 1))][..., DIFF_HEADS:].astype(jnp.float32)
    bias = bias.reshape(SWA_BLK, 2 * SWA_BLK, SWA_KV_HEADS, SWA_GROUP).transpose(2, 3, 0, 1)
    s = jnp.einsum('bnqhgd,bnkhd->bnhgqk', q, k_band).astype(jnp.float32) * SWA_HD ** -0.5 + bias
    s = jnp.where(mask[None, :, None, None], s, NEG_INF)
    sink = jnp.broadcast_to(sinks.astype(jnp.float32).reshape(SWA_KV_HEADS, SWA_GROUP, 1, 1),
                            s.shape[:-1] + (1,))
    p = jax.nn.softmax(jnp.concatenate([s, sink], axis=-1), axis=-1)[..., :-1]
    o = jnp.einsum('bnhgqk,bnkhd->bnqhgd', p.astype(v.dtype), v_band)
    return o.reshape(B, S, SWA_HEADS * SWA_HD)

def hybrid_mixer(h, w_in, conv_w, conv_b, lru_wa, lru_ba, lru_wx, lru_bx, lru_lambda,
                 diff_qnorm, diff_knorm, diff_lambda, diff_subln,
                 swa_qnorm, swa_knorm, swa_sinks, rel_bias, w_branch, w_out, lambda_init):
    B, S, D = h.shape
    proj = h @ w_in
    offsets = []
    acc = 0
    for width in IN_SPLITS[:-1]:
        acc += width
        offsets.append(acc)
    xr, gr, dq, dk, dv, sq, sk, sv, gl = jnp.split(proj, offsets, axis=-1)
    o_lru = rglru_branch(xr, gr, conv_w, conv_b, lru_wa, lru_ba, lru_wx, lru_bx, lru_lambda)
    o_diff = diff_attention(dq.reshape(B, S, DIFF_HEADS, 2, DIFF_HD),
                            dk.reshape(B, S, DIFF_HEADS, 2, DIFF_HD),
                            dv.reshape(B, S, DIFF_HEADS, 2 * DIFF_HD),
                            diff_qnorm, diff_knorm, diff_lambda, diff_subln, rel_bias, lambda_init)
    o_swa = swa_attention(sq.reshape(B, S, SWA_HEADS, SWA_HD),
                          sk.reshape(B, S, SWA_KV_HEADS, SWA_HD),
                          sv.reshape(B, S, SWA_KV_HEADS, SWA_HD),
                          swa_qnorm, swa_knorm, swa_sinks, rel_bias)
    branches = jnp.stack([o_lru, o_diff, o_swa], axis=2)
    branch_proj = jnp.einsum('bsnc,ncd->bsnd', branches, w_branch)
    gates = jax.nn.sigmoid(gl).reshape(B, S, N_BRANCHES, D)
    merged = jnp.einsum('bsnd,bsnd->bsd', gates, branch_proj)
    return merged @ w_out

def moe_ffn(h, w_router, b_router, w1, b1, w2, b2):
    B, S, D = h.shape
    T = B * S
    xt = h.reshape(T, D)
    logits = xt.astype(jnp.float32) @ w_router.astype(jnp.float32) + b_router.astype(jnp.float32)
    top_v, top_e = lax.top_k(logits, TOP_K)
    weights = jax.nn.softmax(top_v, axis=-1).astype(xt.dtype)
    n_pairs = T * TOP_K
    flat_e = top_e.reshape(-1)
    order = jnp.argsort(flat_e)
    sorted_e = flat_e[order]
    counts = jnp.bincount(flat_e, length=N_EXPERTS)
    starts = jnp.cumsum(counts) - counts
    padded = (counts + MOE_BLK - 1) // MOE_BLK * MOE_BLK
    pad_ends = jnp.cumsum(padded)
    pad_starts = pad_ends - padded
    dest_sorted = pad_starts[sorted_e] + (jnp.arange(n_pairs) - starts[sorted_e])
    n_rows = (n_pairs + MOE_BLK - 1) // MOE_BLK * MOE_BLK + N_EXPERTS * MOE_BLK
    n_blocks = n_rows // MOE_BLK
    row_token = jnp.full((n_rows,), T, jnp.int32).at[dest_sorted].set((order // TOP_K).astype(jnp.int32))
    dest = jnp.zeros_like(order).at[order].set(dest_sorted)
    block_expert = jnp.minimum(jnp.searchsorted(pad_ends, jnp.arange(n_blocks) * MOE_BLK, side='right'),
                               N_EXPERTS - 1)
    x_pad = jnp.concatenate([xt, jnp.zeros((1, D), xt.dtype)], axis=0)

    def expert_block(args):
        tok, e = args
        hcat = x_pad[tok] @ w1[e] + b1[e]
        x_glu = jnp.minimum(hcat[:, ::2], SWIGLU_LIMIT)
        x_lin = jnp.clip(hcat[:, 1::2], -SWIGLU_LIMIT, SWIGLU_LIMIT)
        act = x_glu * jax.nn.sigmoid(SWIGLU_ALPHA * x_glu) * (x_lin + 1.0)
        return act @ w2[e] + b2[e]

    y = lax.map(expert_block, (row_token.reshape(n_blocks, MOE_BLK), block_expert)).reshape(n_rows, D)
    out = jnp.sum(y[dest].reshape(T, TOP_K, D) * weights[..., None], axis=1)
    return out.reshape(B, S, D)

def second_inputs(seed: int = 0) -> dict:
    key = jax.random.key(seed)
    keys = jax.random.split(key, 40)
    counter = [0]

    def next_key():
        k = keys[counter[0]]
        counter[0] += 1
        return k

    def nrm(shape, scale):
        return jax.random.normal(next_key(), shape, jnp.float32) * scale

    L = DEPTH_2
    D = D_MODEL
    x = nrm((BATCH, SEQ, D), 1.0)
    c = nrm((BATCH, D), 1.0)
    w_ada = nrm((L, D, 6 * D), 0.5 * D ** -0.5)
    b_ada = nrm((L, 6 * D), 0.02)
    norm_mix = 1.0 + nrm((L, D), 0.02)
    norm_ffn = 1.0 + nrm((L, D), 0.02)
    w_in = nrm((L, D, IN_WIDTH), D ** -0.5)
    conv_w = nrm((L, CONV_W, LRU_WIDTH), CONV_W ** -0.5)
    conv_b = nrm((L, LRU_WIDTH), 0.02)
    lru_wa = nrm((L, LRU_BLOCKS, LRU_BD, LRU_BD), LRU_BD ** -0.5)
    lru_ba = nrm((L, LRU_WIDTH), 0.02)
    lru_wx = nrm((L, LRU_BLOCKS, LRU_BD, LRU_BD), LRU_BD ** -0.5)
    lru_bx = nrm((L, LRU_WIDTH), 0.02)
    radius = jax.random.uniform(next_key(), (L, LRU_WIDTH), jnp.float32, 0.9, 0.999)
    lru_lambda = -jnp.log(jnp.expm1(-jnp.log(radius) / LRU_C))
    diff_qnorm = 1.0 + nrm((L, DIFF_HD), 0.02)
    diff_knorm = 1.0 + nrm((L, DIFF_HD), 0.02)
    diff_lambda = nrm((L, 4, DIFF_HD), 0.1)
    diff_subln = 1.0 + nrm((L, 2 * DIFF_HD), 0.02)
    swa_qnorm = 1.0 + nrm((L, SWA_HD), 0.02)
    swa_knorm = 1.0 + nrm((L, SWA_HD), 0.02)
    swa_sinks = nrm((L, SWA_HEADS), 0.5)
    rel_bias = nrm((REL_BUCKETS, N_ATTN_HEADS), 0.5)
    w_branch = nrm((L, N_BRANCHES, BRANCH_WIDTH_2, D), BRANCH_WIDTH_2 ** -0.5)
    w_out = nrm((L, D, D), D ** -0.5)
    w_router = nrm((L, D, N_EXPERTS), D ** -0.5)
    b_router = nrm((L, N_EXPERTS), 0.01)
    w1 = nrm((L, N_EXPERTS, D, 2 * D_FF_2), D ** -0.5)
    b1 = nrm((L, N_EXPERTS, 2 * D_FF_2), 0.02)
    w2 = nrm((L, N_EXPERTS, D_FF_2, D), D_FF_2 ** -0.5)
    b2 = nrm((L, N_EXPERTS, D), 0.02)
    return {'x': x, 'c': c, 'w_ada': w_ada, 'b_ada': b_ada, 'norm_mix': norm_mix, 'norm_ffn': norm_ffn,
            'w_in': w_in, 'conv_w': conv_w, 'conv_b': conv_b, 'lru_wa': lru_wa, 'lru_ba': lru_ba,
            'lru_wx': lru_wx, 'lru_bx': lru_bx, 'lru_lambda': lru_lambda, 'diff_qnorm': diff_qnorm,
            'diff_knorm': diff_knorm, 'diff_lambda': diff_lambda, 'diff_subln': diff_subln,
            'swa_qnorm': swa_qnorm, 'swa_knorm': swa_knorm, 'swa_sinks': swa_sinks, 'rel_bias': rel_bias,
            'w_branch': w_branch, 'w_out': w_out, 'w_router': w_router, 'b_router': b_router,
            'w1': w1, 'b1': b1, 'w2': w2, 'b2': b2}

def second_block(x, c, w_ada, b_ada, norm_mix, norm_ffn, w_in, conv_w, conv_b, lru_wa, lru_ba,
              lru_wx, lru_bx, lru_lambda, diff_qnorm, diff_knorm, diff_lambda, diff_subln,
              swa_qnorm, swa_knorm, swa_sinks, rel_bias, w_branch, w_out, w_router, b_router,
              w1, b1, w2, b2):
    cond = jax.nn.silu(c)
    for layer in range(DEPTH_2):
        mod = cond @ w_ada[layer] + b_ada[layer]
        sh_m, sc_m, g_m, sh_f, sc_f, g_f = [m[:, None, :] for m in jnp.split(mod, 6, axis=-1)]
        lambda_init = 0.8 - 0.6 * math.exp(-0.3 * layer)
        h = rms_norm_2(x, norm_mix[layer]) * (1.0 + sc_m) + sh_m
        x = x + g_m * hybrid_mixer(h, w_in[layer], conv_w[layer], conv_b[layer], lru_wa[layer],
                                   lru_ba[layer], lru_wx[layer], lru_bx[layer], lru_lambda[layer],
                                   diff_qnorm[layer], diff_knorm[layer], diff_lambda[layer],
                                   diff_subln[layer], swa_qnorm[layer], swa_knorm[layer],
                                   swa_sinks[layer], rel_bias, w_branch[layer], w_out[layer],
                                   lambda_init)
        h = rms_norm_2(x, norm_ffn[layer]) * (1.0 + sc_f) + sh_f
        x = x + g_f * moe_ffn(h, w_router[layer], b_router[layer], w1[layer], b1[layer],
                              w2[layer], b2[layer])
    return x


def setup_inputs(seed=0):
    out = dict(first_inputs(seed))
    for name, value in second_inputs(seed + 1).items():
        if name != "x":
            out[name + "_2"] = value
    return out


def reference(
    x, p, positions, ffn1_up, ffn1_down, ln1_g, ln1_b, w_in, sgu_ln_g, sgu_ln_b, sgu_w, sgu_b,
    pool_w, pool_scale, mla_q_norm, mla_kv_norm, mla_w_uq, mla_w_ukv, w_branch, w_out, ln2_g,
    ln2_b, ffn2_up, ffn2_down, w_ple_gate, w_ple, ln3_g, ln3_b, c_2, w_ada_2, b_ada_2,
    norm_mix_2, norm_ffn_2, w_in_2, conv_w_2, conv_b_2, lru_wa_2, lru_ba_2, lru_wx_2, lru_bx_2,
    lru_lambda_2, diff_qnorm_2, diff_knorm_2, diff_lambda_2, diff_subln_2, swa_qnorm_2,
    swa_knorm_2, swa_sinks_2, rel_bias_2, w_branch_2, w_out_2, w_router_2, b_router_2, w1_2,
    b1_2, w2_2, b2_2,
):
    x = first_block(
        x, p, positions, ffn1_up, ffn1_down, ln1_g, ln1_b, w_in, sgu_ln_g, sgu_ln_b, sgu_w,
        sgu_b, pool_w, pool_scale, mla_q_norm, mla_kv_norm, mla_w_uq, mla_w_ukv, w_branch,
        w_out, ln2_g, ln2_b, ffn2_up, ffn2_down, w_ple_gate, w_ple, ln3_g, ln3_b,
    )
    return second_block(
        x, c_2, w_ada_2, b_ada_2, norm_mix_2, norm_ffn_2, w_in_2, conv_w_2, conv_b_2, lru_wa_2,
        lru_ba_2, lru_wx_2, lru_bx_2, lru_lambda_2, diff_qnorm_2, diff_knorm_2, diff_lambda_2,
        diff_subln_2, swa_qnorm_2, swa_knorm_2, swa_sinks_2, rel_bias_2, w_branch_2, w_out_2,
        w_router_2, b_router_2, w1_2, b1_2, w2_2, b2_2,
    )


_drawn_inputs = setup_inputs


def setup_inputs(seed=0):
    import zlib

    import numpy as np

    out = dict(_drawn_inputs(seed))
    spreads = {}
    factors = {'sgu_ln_g': 4.91,
     'sgu_ln_b': 8.0,
     'pool_scale': 3.217,
     'mla_q_norm': 8.0,
     'mla_kv_norm': 8.0,
     'norm_mix_2': 5.173,
     'norm_ffn_2': 10.808,
     'conv_b_2': 3.763,
     'lru_ba_2': 34.001,
     'lru_bx_2': 24.08,
     'diff_qnorm_2': 8.0,
     'diff_knorm_2': 8.0,
     'diff_lambda_2': 8.0,
     'diff_subln_2': 30.295,
     'swa_qnorm_2': 8.0,
     'swa_knorm_2': 8.0,
     'swa_sinks_2': 200.0,
     'b_router_2': 19.659,
     'b1_2': 23.426,
     'b2_2': 53.341}
    for name, (base, spread) in spreads.items():
        noise = np.random.default_rng([zlib.crc32(name.encode()), seed]).standard_normal(out[name].shape)
        drawn = base * np.exp(spread * noise) if base else spread * noise
        out[name] = jnp.asarray(drawn.astype(out[name].dtype))
    for name, factor in factors.items():
        out[name] = (out[name] * factor).astype(out[name].dtype)
    return out
```

```python
import math
from contextlib import ExitStack

import numpy as np

import concourse.bass as bass
import concourse.mybir as mybir

ACT = mybir.ActivationFunctionType
ALU = mybir.AluOpType
AX = mybir.AxisListType
F32 = mybir.dt.float32
F32R = mybir.dt.float32r
I32 = mybir.dt.int32
U32 = mybir.dt.uint32

D = 1024
KD = D // 128
SEQ = 256
NT = SEQ // 128
DEPTH = 2
D_FF = 2816
NG = D_FF // 256
ALPHA = (2 * DEPTH) ** 0.25
LN_EPS = 1e-5
RMS_EPS = 1e-6
GN_EPS = 1e-5
MLA_SCALE = 96.0 ** -0.5
MASKED = -1e30
RMS_EPS = 1e-6
N_EXP = 32
N_EXTRA = 15
LIMIT = 7.0
SWIGLU = 1.702
NRAW = 3
NSPLIT = 3
AHEAD = 1


class Queue:

    def __init__(self, sem):
        self.items, self.sem, self.count, self.cost = [], sem, 0, 0.0
        self.regs, self.outer = {}, []

    def read(self, name, src, low, high, *after):
        def emit(e):
            self.regs[name] = e.value_load(src, min_val=low, max_val=high)

        self.items.append((after, emit, None, 0))

    def only_if_more(self, name, than):
        self.items.append(("if", name, than, 0))

    def end(self):
        self.items.append(("end", None, None, 0))

    def enter(self, sem):
        self.outer.append((self.sem, self.count))
        self.sem, self.count = sem, 0

    def leave(self):
        self.sem, self.count = self.outer.pop()

    def put(self, emit, *after):
        self.count += 1
        self.items.append((after, emit, self.sem, 1))
        return (self.sem, self.count)

    def replay(self, engine):
        reached, inside = {}, []
        for after, emit, sem, by in self.items:
            if after == "if":
                guard = engine.If(self.regs[emit] > sem)
                guard.__enter__()
                inside.append((guard, dict(reached)))
                continue
            if after == "end":
                guard, reached = inside.pop()
                guard.__exit__(None, None, None)
                continue
            for mark in after:
                if mark is None:
                    continue
                key = id(mark[0])
                if reached.get(key, 0) < mark[1]:
                    engine.wait_ge(mark[0], mark[1])
                    reached[key] = mark[1]
            if by:
                emit(engine).then_inc(sem, by)
            elif emit is not None:
                emit(engine)


class Vector(Queue):
    def tt(self, out, a, b, op, *after):
        return self.put(lambda e: e.tensor_tensor(out, a, b, op=op), *after)

    def ts(self, out, a, s1, s2, op0, op1, *after):
        if op1 is None:
            return self.put(lambda e: e.tensor_scalar(out, a, s1, None, op0=op0), *after)
        return self.put(lambda e: e.tensor_scalar(out, a, s1, s2, op0=op0, op1=op1), *after)

    def stt(self, out, a, s, b, op0, op1, *after):
        return self.put(lambda e: e.scalar_tensor_tensor(out, a, s, b, op0=op0, op1=op1), *after)

    def copy(self, out, a, *after):
        return self.put(lambda e: e.tensor_copy(out, a), *after)

    def memset(self, out, value, *after):
        return self.put(lambda e: e.memset(out, value), *after)

    def reduce(self, out, a, op, *after):
        return self.put(lambda e: e.tensor_reduce(out, a, axis=AX.X, op=op), *after)

    def recip(self, out, a, *after):
        return self.put(lambda e: e.reciprocal(out, a), *after)

    def stats(self, out, a, *after):
        return self.put(lambda e: e.bn_stats(out, a), *after)

    def aggr(self, out, a, *after):
        return self.put(lambda e: e.bn_aggr(out, a), *after)


class Scalar(Queue):
    def copy(self, out, a, *after):
        return self.put(lambda e: e.copy(out, a), *after)

    def act(self, out, a, func, *after, **more):
        return self.put(lambda e: e.activation(out, a, func, **more), *after)


class Tensor(Queue):
    def mms(self, products, *after):
        self.cost += sum(max(64, p[2].shape[-1]) * 4 / 2400 for p in products)

        def emit(e):
            for out, lhs, rhs, start, stop in products:
                last = e.matmul(out, lhs, rhs, start=start, stop=stop)
            return last

        return self.put(emit, *after)

    def split(self, products, *after):
        self.cost += sum(p[0].shape[-1] * 3 / 2400 + 0.008 for p in products)

        def emit(e):
            for out, (xh, xl), (wh, wl), start, stop in products:
                e.matmul(out, xh, wh, start=start, stop=False)
                e.matmul(out, xh, wl, start=False, stop=False)
                last = e.matmul(out, xl, wh, start=False, stop=stop)
            return last

        return self.put(emit, *after)

    def turn(self, pairs, ident, *after):
        self.cost += 0.065 * len(pairs)

        def emit(e):
            for out, a in pairs:
                last = e.transpose(out, a, ident)
            return last

        return self.put(emit, *after)


class Loads(Queue):

    def load(self, slot, out, src, *after):
        slot[1] += 16
        self.items.append((after, lambda e: e.dma_start(out, src() if callable(src) else src), slot[0], 16))
        return (slot[0], slot[1])


class Pool(Vector, Loads):
    pass


def rows(ap, n=128):
    return ap.unsqueeze(0).to_broadcast([n] + list(ap.shape))


def program(nc, a):
    top = ExitStack()

    def sem(name):
        return top.enter_context(nc.semaphore(name))

    def sb(name, cols, dt=F32, ctx=top):
        return ctx.enter_context(nc.sbuf_tensor("s_" + name, [128, cols], dt))

    bank = [top.enter_context(nc.psum_tensor(f"bank{i}", [128, 512], F32)) for i in range(8)]
    ACC = [[bank[0], bank[1]], [bank[2], bank[3]]]

    V, A, P = Vector(sem("dve_a")), Scalar(sem("act_a")), Tensor(sem("pe_a"))
    G, S = Pool(sem("pool_a")), Loads(None)

    ident = sb("ident", 128)
    X = [sb(f"x{t}", D) for t in range(NT)]
    MERGED = [sb(f"merged{t}", D) for t in range(NT)]
    GAIN, BIAS = sb("gain_row", D), sb("bias_row", D)
    ST = [sb(f"st{t}", 176) for t in range(NT)]
    RT = [sb(f"route{t}", 376) for t in range(NT)]
    RI = [top.enter_context(nc.sbuf_tensor(f"s_best{t}", [128, 8], U32)) for t in range(NT)]
    ones, cond_t, iota = sb("ones", 1), sb("cond", KD), sb("iota", 128)
    dense = ExitStack()
    RAW = [sb(f"raw{i}", 2048, ctx=dense) for i in range(NRAW)]
    WH = [sb(f"wh{i}", 2048, F32R, dense) for i in range(NSPLIT)]
    WL = [sb(f"wl{i}", 2048, F32R, dense) for i in range(NSPLIT)]
    XTH = [sb(f"xth{t}", D, F32R, dense) for t in range(NT)]
    XTL = [sb(f"xtl{t}", D, F32R, dense) for t in range(NT)]
    YTH = [sb(f"yth{t}", 512, F32R, dense) for t in range(NT)]
    YTL = [sb(f"ytl{t}", 512, F32R, dense) for t in range(NT)]
    GATE = [sb(f"gate{t}", D, ctx=dense) for t in range(NT)]

    first = ExitStack()
    sizes = dict(pr=1024, a2=1024, a3=512, a4=512, a5=256, kcat=384, q=384, ct=384, plt=256,
                 rqt=256, z=256, rv=256, rkt=256, mkt=512, mv=256)
    B = [{k: sb(f"{k}{t}", n, ctx=first) for k, n in sizes.items()} for t in range(NT)]
    RT1, RT2 = sb("rope1", 512, ctx=first), sb("rope2", 512, ctx=first)
    sgu_w, sgu_b = sb("sgu_w_t", 512, ctx=first), sb("sgu_b_t", 4, ctx=first)
    sgu_g, sgu_bb = sb("sgu_gain", 256, ctx=first), sb("sgu_bias", 256, ctx=first)
    pool_w, pool_s = sb("pool_w_t", 256, ctx=first), sb("pool_s", 256, ctx=first)
    q_gain, kv_gain = sb("q_gain", 256, ctx=first), sb("kv_gain", 128, ctx=first)
    w_uq, w_ukv = sb("w_uq_t", 768, ctx=first), sb("w_ukv_t", 512, ctx=first)
    decay = sb("decay", 1024, ctx=first)
    band = sb("band", 512 + 512 + 64, ctx=first)
    tril = sb("tril", 128, ctx=first)
    freq = sb("freq", 48, ctx=first)
    pos_i = first.enter_context(nc.sbuf_tensor("pos_i", [128, NT], I32))
    pos_f = sb("pos_f", NT, ctx=first)
    cos, sin = (sb(n, NT * 48, ctx=first) for n in ("cos_t", "sin_t"))
    ang, turns = RT1[:, :NT * 48], RT2[:, :NT * 48]

    first.close()
    second = ExitStack()
    sizes2 = dict(dq=512, dk=512, sq=512, sk=128, dv=512, sv=128, kt=512, skt=128, xrt=524, big=2048, aa=512, hl=4)
    room = sum(sizes.values()) - sum(sizes2.values())
    C = []
    for t in range(NT):
        C.append({k: sb(f"{k}_{t}", n, ctx=second) for k, n in sizes2.items()})
        sb(f"room{t}", room, ctx=second)
    bm = sb("bm", 12 * 256, ctx=second)
    gains = [sb(f"gain{i}", 64, ctx=second) for i in range(4)]
    subln, sinks, lamv, lam = (sb(n, w, ctx=second) for n, w in (("subln", 128), ("sinks", 8), ("lamv", 256), ("lam", 4)))
    conv_w, conv_b, sp, sp4, lt = (sb(n, w, ctx=second) for n, w in
                                   (("conv_w2", 16), ("conv_b2", 4), ("sp", 4), ("sp4", 8), ("lt", 12)))
    lru_a, lru_x, ba, bx = (sb(n, w, ctx=second) for n, w in (("lru_a2", 512), ("lru_x2", 512), ("ba", 4), ("bx", 4)))
    w_router, b_router = sb("w_router2", 256, ctx=second), sb("b_router2", N_EXP, ctx=second)
    rel, buckets, future = (sb(n, w, ctx=second) for n, w in (("rel", 12), ("buckets2", 384), ("future2", 384)))
    before = sb("before2", 128, ctx=second)
    second.close()
    dense.close()

    moe = ExitStack()
    NRING = 16
    RING = [sb(f"ring{i}", 2048, ctx=moe) for i in range(NRING)]
    XE = [sb(f"xe{i}", 512, ctx=moe) for i in range(2)]
    SEL = [sb(f"sel{i}", 128, ctx=moe) for i in range(2)]
    SELT = [sb(f"selt{i}", 256, ctx=moe) for i in range(2)]
    Y = [sb(f"y{i}", 512, ctx=moe) for i in range(2)]
    SELW = sb("selw", 256, ctx=moe)
    GLU, TH, LIN, ACTT = (sb(n, 512, ctx=moe) for n in ("glu", "th", "lin", "actt"))
    TMP = sb("tmp", D, ctx=moe)
    GT = sb("gt", 256, ctx=moe)
    b1s, b2s = sb("b1s", 2048, ctx=moe), sb("b2s", 1024, ctx=moe)
    EX = sb("extra", 256, ctx=moe)
    EXI = moe.enter_context(nc.sbuf_tensor("s_extra_n", [128, 1 + N_EXTRA], I32))
    moe.close()
    ring_slot = [[sem(f"ring_in{i}"), 0] for i in range(NRING)]
    b_slot = [sem("b_in"), 0]
    small2 = [sem("small2_in"), 0]
    toeplitz = nc.dram_tensor("toeplitz", [128, 12, 384], F32, kind="Internal").ap()
    IOTA, RING_AFTER, B_AFTER = [None], [()] * NRING, []

    spare = [(bank[i], None) for i in range(4, 8)]

    def take():
        return spare.pop(0)

    def give(b, mark):
        spare.append((b, mark))

    chunks, stream, place, extra = [], [], [], {}
    raw_slot = [[sem(f"raw_in{i}"), 0] for i in range(NRAW)]
    loaded, hi_done, lo_done, used, raw_free = {}, {}, {}, {}, {}
    at = [0, 0]

    def chunk_add(*srcs):
        for src in srcs:
            place.append(len(stream))
            chunks.append(src)
            stream.append(src)

    def chunk_extra(src):
        extra.setdefault(len(chunks), []).append(len(stream))
        stream.append(src)

    def chunk_load(i):
        if i < len(stream) and i not in loaded:
            src = stream[i]
            after = [raw_free[i - NRAW]] if i >= NRAW else []
            loaded[i] = S.load(raw_slot[i % NRAW], RAW[i % NRAW][:, :src.shape[-1]], src, *after)

    def chunk_split(i, part):
        if i >= len(chunks) or (i, part) in hi_done:
            return
        for j in extra.pop(i, []):
            chunk_load(j)
            raw_free[j] = ada_chunk(j)
            chunk_load(j + NRAW)
        j = place[i]
        chunk_load(j)
        w = chunks[i].shape[-1] // 2
        c = slice(part * w, (part + 1) * w)
        raw, hi, lo = RAW[j % NRAW][:, c], WH[i % NSPLIT][:, c], WL[i % NSPLIT][:, c]
        after = [used[(i - NSPLIT, t)] for t in range(NT)] if i >= NSPLIT else []
        hi_done[i, part] = A.copy(hi, raw, loaded[j], *after)
        lo_done[i, part] = V.tt(lo, raw, hi.bitcast(F32), ALU.subtract, hi_done[i, part])
        if part == 1:
            raw_free[j] = lo_done[i, 1]
            chunk_load(j + NRAW)

    def may_use(t):
        if t == 0:
            return at[0] + AHEAD - NSPLIT < at[1]
        return at[1] < at[0]

    def chunk_use(t, products, *after):
        i = at[t]
        at[t] += 1
        if t == 0:
            for part in range(2):
                chunk_split(i, part)
        hi, lo = WH[i % NSPLIT], WL[i % NSPLIT]
        halves = products(hi, lo)
        for part in range(2):
            if halves[part]:
                mark = P.split(halves[part], lo_done[i, part], *after)
            if t == 0:
                chunk_split(i + AHEAD, part)
        used[i, t] = mark
        return mark

    def rsqrt(x, y, u, v, mark, between=()):
        between = list(between)

        def other():
            if between:
                between.pop(0)()

        m = V.ts(u.bitcast(I32), x.bitcast(I32), 1, None, ALU.logical_shift_right, None, mark)
        other()
        m = V.ts(y.bitcast(I32), u.bitcast(I32), -1.0, float(0x5F3759DF), ALU.mult, ALU.add, m)
        other()
        for _ in range(3):
            m = V.tt(u, y, y, ALU.mult, m)
            other()
            m = V.stt(v, u, -0.5, x, ALU.mult, ALU.mult, m)
            other()
            m = V.stt(y, v, 1.5, y, ALU.add, ALU.mult, m)
            other()
        while between:
            other()
        return m

    def xt_from(t, src, ready, xt_free):
        done = []
        turned = []
        for j in range(2):
            b, free = take()
            turned.append((b, P.turn([(b[:, 128 * k:128 * k + 128], src[:, 512 * j + 128 * k:512 * j + 128 * k + 128])
                                      for k in range(4)], ident[:, :], ready[j], free, SB_SMALL["const"])))
        for j, (b, m) in enumerate(turned):
            h = A.copy(XTH[t][:, 512 * j:512 * j + 512], b[:, :], m, xt_free)
            l = V.tt(XTL[t][:, 512 * j:512 * j + 512], b[:, :], XTH[t][:, 512 * j:512 * j + 512].bitcast(F32),
                     ALU.subtract, h)
            give(b, l)
            done.append(l)
        return done, turned[1][1]

    def xk(t, k):
        return XTH[t][:, 128 * k:128 * k + 128], XTL[t][:, 128 * k:128 * k + 128]

    def group_products(t, b, w, part, nk=8):
        def products(hi, lo):
            out = []
            for j in range(nk):
                k = part * nk + j
                c = slice(j * w, j * w + w)
                out.append((b[:, :w], xk(t, k), (hi[:, c], lo[:, c]), k == 0, k == KD - 1))
            return out[:nk // 2], out[nk // 2:]
        return products

    def wide_products(lhs, outs, first_k, last_k, k0):
        def products(hi, lo):
            out = []
            for j in range(2):
                k = k0 + j
                for h in range(2):
                    c = slice(1024 * j + 512 * h, 1024 * j + 512 * h + 512)
                    out.append((outs[h][:, :], lhs(k), (hi[:, c], lo[:, c]), k == first_k, k == last_k))
            return out[:2], out[2:]
        return products

    def layer_norm(t, scale, pe_mark, x_mark, rows_mark):
        x, st = X[t], ST[t]
        halves = [x[:, :512], x[:, 512:]]
        m = []
        for h in range(2):
            y = V.stt(halves[h], ACC[t][h][:, :], scale, halves[h], ALU.mult, ALU.add, pe_mark, x_mark)
            m.append(V.stats(st[:, 6 * h:6 * h + 6], halves[h], y))
        acc_free = y
        m = V.aggr(st[:, 12:14], st[:, 0:12], *m)
        e = V.ts(st[:, 14:15], st[:, 13:14], LN_EPS, None, ALU.add, None, m)
        z = [None, None]

        def centre(h):
            def f():
                c = slice(512 * h, 512 * h + 512)
                z[h] = V.stt(halves[h], halves[h], st[:, 12:13], GAIN[:, c], ALU.subtract, ALU.mult, m, rows_mark)
            return f

        r = rsqrt(st[:, 14:15], st[:, 15:16], st[:, 16:17], st[:, 17:18], e, [centre(0), centre(1)])
        out = []
        for h in range(2):
            c = slice(512 * h, 512 * h + 512)
            out.append(V.stt(halves[h], halves[h], st[:, 15:16], BIAS[:, c], ALU.mult, ALU.add, r, z[h]))
        return out, acc_free

    def scale_x(t, *after):
        return G.ts(X[t][:, :], X[t][:, :], ALPHA, 0.0, ALU.mult, ALU.add, *after)

    rows_slot = [sem("rows_in"), 0]
    rows_users = []

    def load_rows(g, b, *after):
        S.load(rows_slot, GAIN[:, :], rows(g), *rows_users, *after)
        return S.load(rows_slot, BIAS[:, :], rows(b), *rows_users, *after)

    state = [dict(xt_free=None, acc_free=None, act_free=[None, None], sil_free=None, yt_free=[None, None])
             for _ in range(NT)]

    def ffn(t, xt, x_mark):
        s, buf = state[t], B[t]
        sil = buf["kcat"][:, 0:256]
        pend = None
        for g in range(NG + 1):
            if g < NG:
                b, free = take()
                m = chunk_use(t, group_products(t, b, 512, 0, 4), free, xt[0])
                yield 0.0
            if pend is not None:
                pb, act, ready, slot, pg = pend
                tm = P.turn([(pb[:, 128 * k:128 * k + 128], act[:, 128 * k:128 * k + 128]) for k in range(2)],
                            ident[:, :], ready)
                s["act_free"][slot] = tm
                c = slice(256 * slot, 256 * slot + 256)
                h = A.copy(YTH[t][:, c], pb[:, :256], tm, s["yt_free"][slot])
                l = V.tt(YTL[t][:, c], pb[:, :256], YTH[t][:, c].bitcast(F32), ALU.subtract, h)
                give(pb, l)
                if g == NG:
                    yield 1.5
            if g < NG:
                m = chunk_use(t, group_products(t, b, 512, 1, 4), xt[1])
                if g == NG - 1:
                    s["xt_free"] = m
                silu = A.act(sil, b[:, 0:256], ACT.Silu, m, s["sil_free"])
                slot = g % 2
                act = buf["pr"][:, 0:256] if slot else buf["a2"][:, 0:256]
                ready = V.tt(act, sil, b[:, 256:512], ALU.mult, silu, s["act_free"][slot])
                s["sil_free"] = ready
                now = (b, act, ready, slot, g)
                yield 0.0
            if pend is not None:
                pb, act, ready, slot, pg = pend

                def lhs(k, slot=slot):
                    c = slice(256 * slot + 128 * (k % 2), 256 * slot + 128 * (k % 2) + 128)
                    return YTH[t][:, c], YTL[t][:, c]

                m = chunk_use(t, wide_products(lhs, ACC[t], 0, 2 * NG - 1, 2 * pg), l,
                              s["acc_free"] if pg == 0 else None)
                s["yt_free"][slot] = m
                yield 0.0
            pend = now if g < NG else None
        s["down"] = m

    SB_SMALL = {}

    def rope(src, dst, groups, half, c, s, done, *after):
        n = groups * 2 * half
        t1 = RT1[:, :n].rearrange("p (g w h) -> p g w h", g=groups, w=2)
        t2 = RT2[:, :n].rearrange("p (g w h) -> p g w h", g=groups, w=2)
        cb = c.unsqueeze(1).to_broadcast([128, groups, half])
        sb_ = s.unsqueeze(1).to_broadcast([128, groups, half])
        m = []
        for w in range(2):
            m.append(G.tt(t1[:, :, w], src[:, :, w], cb, ALU.mult, *after, *done))
            m.append(G.tt(t2[:, :, w], src[:, :, 1 - w], sb_, ALU.mult, *after, *done))
        lo = G.tt(dst[:, :, 0], t1[:, :, 0], t2[:, :, 0], ALU.subtract, *m)
        hi = G.tt(dst[:, :, 1], t1[:, :, 1], t2[:, :, 1], ALU.add, *m)
        return [lo, hi]

    rope_done = [[]]

    def branches(t, layer, ev, out):
        buf, st, s = B[t], ST[t], state[t]
        b0, b1 = ACC[t]
        bf = [s["acc_free"], s["acc_free"]]
        prev = B[0]
        small = SB_SMALL["mark"]
        cq = buf["a2"][:, 0:416]
        cn = buf["a2"][:, 416:800]
        c_ret, s_ret = cos[:, 48 * t:48 * t + 32], sin[:, 48 * t:48 * t + 32]
        c_mla, s_mla = cos[:, 48 * t + 32:48 * t + 48], sin[:, 48 * t + 32:48 * t + 48]

        e0 = V.ts(st[:, 22:23], st[:, 20:21], 1.0 / 256, RMS_EPS, ALU.mult, ALU.add, ev["ssq"])
        e1 = V.ts(st[:, 23:24], st[:, 21:22], 1.0 / 128, RMS_EPS, ALU.mult, ALU.add, ev["ssq"], e0)
        r = rsqrt(st[:, 22:24], st[:, 24:26], st[:, 26:28], st[:, 28:30], e1)
        n0 = V.stt(cn[:, 0:256], cq[:, 0:256], st[:, 24:25], q_gain[:, :], ALU.mult, ALU.mult, r, ev["cq"], small)
        n1 = V.stt(cn[:, 256:384], cq[:, 256:384], st[:, 25:26], kv_gain[:, :], ALU.mult, ALU.mult, r)
        kpe = st[:, 32:64].rearrange("p (g w h) -> p g w h", g=1, w=2)
        rope_done[0] = rope(cq[:, 384:416].rearrange("p (g w h) -> p g w h", g=1, w=2), kpe, 1, 16, c_mla, s_mla,
                            rope_done[0], ev["cq"], s.get("kpe_free"), SB_SMALL["rope"])
        kpe_done = rope_done[0]
        yield "qk"
        m = P.turn([(b0[:, 128 * k:128 * k + 128], cn[:, 128 * k:128 * k + 128]) for k in range(3)], ident[:, :],
                   n0, n1, bf[0])
        ct = A.copy(buf["ct"][:, :], b0[:, 0:384], m)
        bf[0] = ct
        rqk = buf["pr"][:, 0:512].rearrange("p (g w h) -> p g w h", g=8, w=2)
        roped = buf["a3"][:, :].rearrange("p (g w h) -> p g w h", g=8, w=2)
        rope_done[0] = rope(rqk, roped, 8, 32, c_ret, s_ret, rope_done[0], ev["qk"], ada["brow_free"], ada["row_free"])
        ret_roped = rope_done[0]
        yield "qk"
        m = P.mms([(b1[:, 0:384], buf["ct"][:, 128 * k:128 * k + 128], w_uq[:, 384 * k:384 * k + 384], k == 0, k == 1)
                   for k in range(2)], ct, bf[1], small)
        qc = A.copy(buf["q"][:, :], b1[:, 0:384], m, s.get("q_free"))
        bf[1] = qc
        q4 = buf["q"][:, :].rearrange("p (h w) -> p h w", h=4)[:, :, 64:96].rearrange("p h (w x) -> p h w x", w=2)
        rope_done[0] = rope(q4, q4, 4, 16, c_mla, s_mla, rope_done[0], qc)
        q_roped = rope_done[0]
        yield "vg"
        m = P.mms([(b0[:, :], buf["ct"][:, 256:384], w_ukv[:, :], True, True)], ct, bf[0])
        kv4 = b0[:, :].rearrange("p (h w) -> p h w", h=4)
        kc4 = buf["kcat"][:, :].rearrange("p (h w) -> p h w", h=4)
        k_nope = A.copy(kc4[:, :, 0:64], kv4[:, :, 0:64], m)
        mv = A.copy(buf["mv"][:, :].rearrange("p (h w) -> p h w", h=4), kv4[:, :, 64:128], m)
        bf[0] = mv
        k_pe = G.copy(kc4[:, :, 64:96], st[:, 32:64].unsqueeze(1).to_broadcast([128, 4, 32]), *kpe_done, k_nope)
        s["kpe_free"] = k_pe
        m = P.turn([(b1[:, 128 * k:128 * k + 128], buf["a3"][:, 128 * k:128 * k + 128]) for k in range(4)], ident[:, :],
                   *ret_roped, bf[1])
        rq = A.copy(buf["rqt"][:, :], b1[:, 0:256], m)
        rk = A.copy(buf["rkt"][:, :], b1[:, 256:512], m, s.get("rkt_free"))
        bf[1] = rk
        s["rkt"], s["mv"] = rk, mv
        yield "vg"
        sb_ = [b0, b1]
        m = []
        for par in range(2):
            ps = []
            for kt in range(t + 1):
                for h2 in range(2):
                    lo = 64 * par
                    c = (kt * 2 + h2) * 128
                    ps.append((sb_[par][:, c:c + 128], B[kt]["rkt"][lo:lo + 64, 128 * h2:128 * h2 + 128],
                               buf["rqt"][lo:lo + 64, 128 * h2:128 * h2 + 128], True, True))
            m.append(P.mms(ps, rq, rk, state[0]["rkt"], bf[par]))
        w = 256 * (t + 1)
        d4 = decay[:, :].rearrange("p (a b) -> p a b", a=2)
        rs4 = buf["a2"][:, :].rearrange("p (a b) -> p a b", a=2)
        rs = []
        for par in range(2):
            rs.append(V.tt(rs4[:, par, 0:w], sb_[par][:, 0:w], d4[:, par, 512 - w:512], ALU.mult, m[par], SB_SMALL["const"],
                           *kpe_done))
            bf[par] = rs[par]
        yield "uv"
        gv = buf["a4"][:, 256:512]
        s0 = V.stats(st[:, 0:6], gv, ev["uv"])
        s0 = V.aggr(st[:, 12:14], st[:, 0:6], s0)
        e = V.ts(st[:, 14:15], st[:, 13:14], LN_EPS, None, ALU.add, None, s0)
        zz = []
        r = rsqrt(st[:, 14:15], st[:, 15:16], st[:, 16:17], st[:, 17:18], e,
                  [lambda: zz.append(V.stt(gv, gv, st[:, 12:13], sgu_g[:, :], ALU.subtract, ALU.mult, s0, small))])
        gvn = V.stt(gv, gv, st[:, 15:16], sgu_bb[:, :], ALU.mult, ALU.add, r, zz[0])
        m = P.turn([(b0[0:96, 128 * h:128 * h + 128], buf["q"][:, 96 * h:96 * h + 96]) for h in range(4)], ident[:, :],
                   *q_roped, bf[0])
        s["q_free"] = m
        qt = A.copy(buf["a3"][0:96, :], b0[0:96, :], m)
        bf[0] = qt
        m = P.turn([(b1[0:96, 128 * h:128 * h + 128], buf["kcat"][:, 96 * h:96 * h + 96]) for h in range(4)], ident[:, :],
                   k_nope, k_pe, bf[1])
        kt_ = A.copy(buf["mkt"][0:96, :], b1[0:96, :], m, s.get("mkt_free"))
        s["mkt"] = kt_
        bf[1] = kt_
        yield "z"
        ps = []
        for g in range(4):
            o = b0[64 * (g % 2):64 * (g % 2) + 64, 128 * (g // 2):128 * (g // 2) + 128]
            ps.append((o, buf["z"][:, 64 * g:64 * g + 64], band[:, 512 * t + 128 * g:512 * t + 128 * g + 128], True, t == 0))
            if t:
                ps.append((o[:, 0:16], prev["z"][96:128, 64 * g:64 * g + 64],
                           band[96:128, 1024 + 16 * g:1024 + 16 * g + 16], False, True))
        mp = P.mms(ps, ev["z"], ev.get("z_prev"), bf[0], SB_SMALL["const"])
        ps = []
        for h in range(4):
            for kt in range(t + 1):
                c = (kt * 2 + h // 2) * 128
                ps.append((b1[:, 64 * h:64 * h + 64], rs4[:, h % 2, c:c + 128], B[kt]["rv"][:, 64 * h:64 * h + 64],
                           kt == 0, kt == t))
        for g in range(4):
            ps.append((b1[:, 256 + 64 * g:320 + 64 * g], sgu_w[:, 128 * g:128 * g + 128], gv[:, 64 * g:64 * g + 64],
                       True, True))
        mr = P.mms(ps, *rs, gvn, bf[1], ev["vg"], ev.get("vg_prev"), SB_SMALL["tril"])
        s["rkt_free"] = mr
        plt = A.copy(buf["plt"][:, :], b0[:, 0:256], mp)
        bf[0] = plt
        us = []
        for g in range(4):
            c = slice(64 * g, 64 * g + 64)
            us.append(V.stt(buf["a4"][:, c], b1[:, 256 + 64 * g:320 + 64 * g], sgu_b[:, g:g + 1], buf["a4"][:, c],
                            ALU.add, ALU.mult, mr, ev["uv"]))
        ss = [V.stats(st[:, 6 * h:6 * h + 6], b1[:, 64 * h:64 * h + 64], mr, r) for h in range(4)]
        mv_ = [V.aggr(st[:, 24 + 2 * h:26 + 2 * h], st[:, 6 * h:6 * h + 6], *ss, n1) for h in range(4)]
        var = st[:, 24:32].rearrange("p (h w) -> p h w", w=2)
        e = V.ts(st[:, 0:4], var[:, :, 1], GN_EPS, None, ALU.add, None, *mv_)
        r = rsqrt(st[:, 0:4], st[:, 4:8], st[:, 8:12], st[:, 16:20], e)
        ry = []
        for h in range(4):
            ry.append(V.ts(buf["q"][:, 64 * h:64 * h + 64], b1[:, 64 * h:64 * h + 64], var[:, h, 0:1], st[:, 4 + h:5 + h],
                           ALU.subtract, ALU.mult, r, s["q_free"]))
        bf[1] = ry[3]
        yr = V.tt(buf["a5"][:, :], buf["a5"][:, :], buf["q"][:, 0:256], ALU.mult, *ry, ev["g"])
        s["q_free"] = yr
        yield "z"

        def turned(src, ready, n, free):
            b, f = take()
            c = slice(256 * (n % 2), 256 * (n % 2) + 256)
            m = P.turn([(b[:, 128 * k:128 * k + 128], src[:, 128 * k:128 * k + 128]) for k in range(2)], ident[:, :],
                       *ready, f)
            h = A.copy(YTH[t][:, c], b[:, 0:256], m, free)
            l = V.tt(YTL[t][:, c], b[:, 0:256], YTH[t][:, c].bitcast(F32), ALU.subtract, h)
            give(b, l)
            return l

        m = P.mms([(b0[:, 128 * g:128 * g + 128], buf["plt"][:, 128 * g:128 * g + 128], pool_w[:, 128 * g:128 * g + 128],
                    True, True) for g in range(2)], plt, bf[0], small)
        yp = V.tt(buf["plt"][:, :], b0[:, 0:256], pool_s[:, :], ALU.mult, m)
        bf[0] = yp
        out[0] = turned(buf["a4"], us, 0, s["yt_free"][0])
        yield "z"
        out[1] = turned(buf["plt"], [yp], 1, s["yt_free"][1])
        n_k = 128 * (t + 1)
        sc = [b0[:, :].rearrange("p (h k) -> p h k", k=n_k), b1[:, :].rearrange("p (h k) -> p h k", k=n_k)]
        per = 4 if t == 0 else 2
        m = []
        for j in range(4 // per):
            ps = []
            for h in range(per):
                for kt in range(t + 1):
                    hh = per * j + h
                    ps.append((sc[j][:, h, 128 * kt:128 * kt + 128], buf["a3"][0:96, 128 * hh:128 * hh + 128],
                               B[kt]["mkt"][0:96, 128 * hh:128 * hh + 128], True, True))
            m.append(P.mms(ps, qt, kt_, state[0]["mkt"], bf[j]))
        s["mkt_free"] = m[-1]
        mx = st[:, 0:4]
        pm = buf["pr"][:, 0:4 * n_k].rearrange("p (h k) -> p h k", k=n_k)
        exps = []
        for j in range(4 // per):
            cut = V.memset(sc[j][0:64, 0:per, n_k - 64:n_k], MASKED, m[j])
            top_ = V.reduce(mx[:, per * j:per * j + per], sc[j][:, 0:per, :], ALU.max, cut, *ry)
            neg = V.ts(st[:, 4 + per * j:4 + per * j + per], mx[:, per * j:per * j + per], -MLA_SCALE, None, ALU.mult, None, top_)
            for h in range(per):
                hh = per * j + h
                ex = A.act(pm[:, hh, :], sc[j][:, h, :], ACT.Exp, neg, *ret_roped, bias=st[:, 4 + hh:5 + hh],
                           scale=MLA_SCALE, accum_out=st[:, 8 + hh:9 + hh])
                exps.append(ex)
            bf[j] = ex
        rsum = V.recip(st[:, 16:20], st[:, 8:12], *exps)
        yield "z"
        out[2] = lambda: turned(buf["a5"], [yr], 0, s["yt_free"][0])
        pt = buf["a2"][:, 0:4 * n_k]
        ready = []
        for j in range(4 // per):
            tr = [(bank_[:, 128 * i:128 * i + 128], buf["pr"][:, 512 * j + 128 * i:512 * j + 128 * i + 128])
                  for bank_ in ([b0, b1][j],) for i in range(4)]
            m = P.turn(tr, ident[:, :], *exps, bf[j])
            cp = A.copy(pt[:, 512 * j:512 * j + 512], [b0, b1][j][:, :], m, mr)
            bf[j] = cp
            ready.append(cp)
        yield "z"
        ps = []
        for h in range(4):
            for kt in range(t + 1):
                c = h * n_k + kt * 128
                ps.append((b0[:, 64 * h:64 * h + 64], pt[:, c:c + 128], B[kt]["mv"][:, 64 * h:64 * h + 64], kt == 0, kt == t))
        m = P.mms(ps, *ready, mv, state[0]["mv"], bf[0])
        ym = V.tt(buf["q"][:, 0:256].rearrange("p (h e) -> p h e", h=4), b0[:, 0:256].rearrange("p (h e) -> p h e", h=4),
                  st[:, 16:20].unsqueeze(2).to_broadcast([128, 4, 64]), ALU.mult, m, rsum, s["q_free"])
        s["acc_free"] = ym
        s["b1_free"] = bf[1]
        out[3] = lambda: turned(buf["q"], [ym], 1, s["yt_free"][1])
        yield "z"

    def mix(t, layer, xt):
        s, buf, st = state[t], B[t], ST[t]
        ev, out, done = {}, {}, set()
        side = branches(t, layer, ev, out)
        need = ["cq"]

        def step():
            if need[0] in done:
                need[0] = next(side, "end")

        def group(w, nk, *parts):
            b, free = take()
            for i, part in enumerate(parts):
                m = chunk_use(t, group_products(t, b, w, part, nk), free if i == 0 else None, xt[0], xt[1])
                if i < len(parts) - 1:
                    step()
                    yield 0.0
            return b, m

        b, m = yield from group(416, 4, 0, 1)
        q0 = A.act(buf["kcat"][:, 0:256], b[:, 0:256], ACT.Square, m, accum_out=st[:, 20:21])
        q1 = A.act(buf["kcat"][:, 256:384], b[:, 256:384], ACT.Square, m, accum_out=st[:, 21:22])
        ev["ssq"] = q1
        ev["cq"] = A.copy(buf["a2"][:, 0:416], b[:, 0:416], m)
        give(b, ev["cq"])
        done.add("cq")
        yield 0.0
        b, m = yield from group(512, 4, 0, 1)
        ev["qk"] = A.copy(buf["pr"][:, 0:512], b[:, :], m)
        give(b, ev["qk"])
        done.add("qk")
        step()
        yield 0.0
        b, m = yield from group(512, 4, 0, 1)
        ev["g"] = A.act(buf["a5"][:, :], b[:, 256:512], ACT.Silu, m)
        ev["vg"] = A.copy(buf["rv"][:, :], b[:, 0:256], m, s.get("rv_free"))
        s["vg"] = ev["vg"]
        ev["vg_prev"] = state[0]["vg"]
        give(b, ev["vg"])
        done.add("vg")
        step()
        yield 0.0
        b, m = yield from group(512, 4, 0, 1)
        ev["uv"] = A.act(buf["a4"][:, :], b[:, :], ACT.Gelu_apprx_tanh, m, ada["brow_free"], ada["row_free"])
        give(b, ev["uv"])
        done.add("uv")
        step()
        yield 0.0
        b, m = yield from group(256, 8, 0)
        ev["z"] = A.copy(buf["z"][:, :], b[:, 0:256], m, s.get("z_free"))
        s["z"] = ev["z"]
        ev["z_prev"] = state[0]["z"]
        give(b, ev["z"])
        done.add("z")
        step()
        yield 0.0
        gate, merged = GATE[t], MERGED[t]
        gate_free = [s.get("gate_free")] * 2
        total = [None, None]
        for n in range(4):
            th = []
            for h in range(2):
                c = slice(512 * h, 512 * h + 512)
                b, m = yield from group(512, 4, 0, 1)
                th.append(A.act(gate[:, c], b[:, :], ACT.Tanh, m, gate_free[h], scale=0.5))
                give(b, th[h])
                step()
                if n == 3 and h == 1:
                    s["xt_free"] = m
                yield 0.0
            while n not in out:
                step()
            if not isinstance(out[n], tuple):
                out[n] = out[n]()
                yield 1.5

            def lhs(k, n=n):
                c = slice(256 * (n % 2) + 128 * k, 256 * (n % 2) + 128 * k + 128)
                return YTH[t][:, c], YTL[t][:, c]

            bs = [take(), take()]
            m = chunk_use(t, wide_products(lhs, [bs[0][0], bs[1][0]], 0, 1, 0), out[n], bs[0][1], bs[1][1])
            s["yt_free"][n % 2] = m
            for h in range(2):
                c = slice(512 * h, 512 * h + 512)
                if n == 0:
                    total[h] = V.stt(merged[:, c], gate[:, c], 1.0, bs[h][0][:, :], ALU.add, ALU.mult, m, th[h])
                    give(bs[h][0], total[h])
                    gate_free[h] = total[h]
                else:
                    pr = V.stt(gate[:, c], gate[:, c], 1.0, bs[h][0][:, :], ALU.add, ALU.mult, m, th[h])
                    give(bs[h][0], pr)
                    adder = V if n == 3 else G
                    total[h] = adder.tt(merged[:, c], merged[:, c], gate[:, c], ALU.add, pr, total[h])
                    gate_free[h] = total[h]
            yield 0.0
        s["gate_free"] = total[1]
        yield 1.5
        done_, turned_ = xt_from(t, merged, total, s["xt_free"])
        s["merged_free"] = turned_
        yield 1.5
        for c in range(4):
            m = chunk_use(t, wide_products(lambda k: xk(t, k), ACC[t], 0, KD - 1, 2 * c), done_[c // 2],
                          s["acc_free"], s["b1_free"])
            if c < 3:
                yield 0.0
        s["xt_free"] = m
        s["down"] = m

    def ple(t, xt):
        s, buf = state[t], B[t]
        kept, th = [], []
        for h in range(2):
            b, free = take()

            def products(hi, lo, b=b):
                out = []
                for k in range(2):
                    o, c = 256 * k + 128 * t, slice(512 + 512 * k, 1024 + 512 * k)
                    out.append((b[:, :], (hi[:, o:o + 128], lo[:, o:o + 128]), (hi[:, c], lo[:, c]), k == 0, k == 1))
                return [], out

            m = chunk_use(t, products, free)
            kept.append(A.copy(MERGED[t][:, 512 * h:512 * h + 512], b[:, :], m, s["merged_free"]))
            give(b, kept[h])
            yield 0.0
        x_done = yield from xt()
        for h in range(2):
            c = slice(512 * h, 512 * h + 512)
            b, free = take()
            for part in range(2):
                m = chunk_use(t, group_products(t, b, 512, part, 4), free, *x_done)
                if part == 0:
                    yield 0.0
            th = A.act(GATE[t][:, c], b[:, :], ACT.Tanh, m, s["gate_free"], scale=0.5)
            give(b, th)
            y = V.stt(MERGED[t][:, c], GATE[t][:, c], 1.0, MERGED[t][:, c], ALU.add, ALU.mult, th, kept[h])
            s["x"] = V.stt(X[t][:, c], MERGED[t][:, c], 0.5, X[t][:, c], ALU.mult, ALU.add, y, s["x"])
            s["gate_free"] = s["merged_free"] = s["x"]
            yield 0.0
        return x_done

    mods = nc.dram_tensor("mods", [6, D], F32, kind="Internal").ap()
    ada = dict(block=0, part=0, free=[None, None], rows=[], brow_free=None, row_free=None)
    brow_slot = [sem("b_ada_in"), 0]
    mod_slot = [[sem(f"mod_out{i}"), 0] for i in range(6)]

    def ada_chunk(i):
        j, part = ada["block"], ada["part"]
        acc = GATE[j % 2]
        raw = RAW[i % NRAW]
        m = ada.get("last")
        if part == 0:
            m = ada["free"][j % 2]
            brow = [G.load(brow_slot, B[0][n][0:1, :], a["b_ada"][j:j + 1, 512 * h:512 * h + 512], ada["brow_free"])
                    for h, n in enumerate(("a3", "a4"))]
            ada["brow"] = brow[1]
        for w in range(2):
            k = 2 * part + w
            cond = cond_t[:, k:k + 1]
            src = raw[:, 1024 * w:1024 * w + 1024]
            if k == 0:
                m = V.ts(acc[:, :], src, cond, None, ALU.mult, None, loaded[i], m, ada["cond"])
            else:
                m = V.stt(acc[:, :], src, cond, acc[:, :], ALU.mult, ALU.add, loaded[i], m)
        ada["last"] = m
        if part == 3:
            out = []
            for h, n in enumerate(("a3", "a4")):
                b, free = take()
                pm = P.mms([(b[0:1, :], ones[:, 0:1], acc[:, 512 * h:512 * h + 512], True, True)], m, free)
                y = V.tt(B[1][n][0:1, :], b[0:1, :], B[0][n][0:1, :], ALU.add, pm, ada["brow"], ada["row_free"])
                give(b, y)
                out.append(y)
            ada["free"][j % 2] = pm
            ada["brow_free"] = y
            for h, n in enumerate(("a3", "a4")):
                ada["row_free"] = G.load(mod_slot[j], mods[j:j + 1, 512 * h:512 * h + 512], B[1][n][0:1, :], out[h])
            ada["rows"].append(ada["row_free"])
            ada["block"], ada["part"] = j + 1, 0
        else:
            ada["part"] = part + 1
        return m

    TT = {}

    def setup_second():
        after = small_users
        for out, name in ((conv_w, "conv_w"), (conv_b, "conv_b"), (lru_a, "lru_a"), (lru_x, "lru_x"), (ba, "lru_ba"),
                          (bx, "lru_bx"), (sp, "lru_lambda"), (w_router, "w_router")):
            G.load(small2, out[:, :], a[name], *after)
        for out, name in ((gains[0], "diff_qnorm"), (gains[1], "diff_knorm"), (gains[2], "swa_qnorm"),
                          (gains[3], "swa_knorm"), (subln, "diff_subln"), (sinks, "swa_sinks"), (lamv, "diff_lambda"),
                          (b_router, "b_router")):
            G.load(small2, out[:, :], rows(a[name]), *after)
        G.load(small2, rel[0:32, :], a["rel_bias"], *after)
        G.load(small2, buckets[0:32, :], a["buckets"], *after)
        m = G.load(small2, future[0:12, :], a["future"], *after)
        b, free = take()
        pm = P.mms([(b[0:12, 0:384], rel[0:32, :], buckets[0:32, :], True, True)], m, free)
        y = V.tt(future[0:12, :], b[0:12, 0:384], future[0:12, :], ALU.add, pm)
        give(b, y)
        w = G.load([sem("toeplitz_out"), 0], toeplitz.rearrange("c h j -> h c j"),
                   future[0:12, :].unsqueeze(1).to_broadcast([12, 128, 384]), y)
        src = bass.AP(tensor=toeplitz.tensor, offset=127, ap=[[12 * 384 - 1, 128], [384, 12], [1, 256]])
        TT["bias"] = G.load([sem("toeplitz_in"), 0], bm[:, :].rearrange("p (h k) -> p h k", h=12), src, w)
        TT["dg"] = V.tt(gains[1][:, :], gains[0][:, :], gains[1][:, :], ALU.mult, m)
        TT["sg"] = V.tt(gains[3][:, :], gains[2][:, :], gains[3][:, :], ALU.mult, m)
        TT["sub"] = V.ts(subln[:, :], subln[:, :], 0.8, None, ALU.mult, None, m)
        l1 = V.tt(lamv[:, 0:64], lamv[:, 0:64], lamv[:, 64:128], ALU.mult, m)
        l2 = V.tt(lamv[:, 128:192], lamv[:, 128:192], lamv[:, 192:256], ALU.mult, m)
        l3 = V.reduce(lam[:, 0:2], lamv[:, :].rearrange("p (a b) -> p a b", a=2)[:, :, 0:64], ALU.add, l1, l2)
        l4 = A.act(lam[:, 0:2], lam[:, 0:2], ACT.Exp, l3)
        l5 = V.tt(lam[:, 2:3], lam[:, 1:2], lam[:, 0:1], ALU.subtract, l4)
        TT["lam"] = V.ts(lam[:, 2:3], lam[:, 2:3], -0.2, None, ALU.add, None, l5)
        n1 = V.stt(lt[:, 0:4], sp[:, :], -1.0, sp[:, :], ALU.mult, ALU.max, m)
        n2 = A.act(lt[:, 0:4], lt[:, 0:4], ACT.Exp, n1, scale=-1.0)
        n3 = V.ts(lt[:, 4:8], lt[:, 0:4], 2.0, None, ALU.add, None, n2)
        n3 = V.recip(lt[:, 4:8], lt[:, 4:8], n3)
        n3 = V.tt(lt[:, 0:4], lt[:, 0:4], lt[:, 4:8], ALU.mult, n3)
        n4 = V.tt(lt[:, 4:8], lt[:, 0:4], lt[:, 0:4], ALU.mult, n3)
        p = V.ts(lt[:, 8:12], lt[:, 4:8], 1.0 / 19, None, ALU.mult, None, n4)
        for k in range(8, 0, -1):
            p = V.stt(lt[:, 8:12], lt[:, 8:12], 1.0 / (2 * k + 1), lt[:, 4:8], ALU.add, ALU.mult, p)
        p = V.stt(lt[:, 8:12], lt[:, 8:12], 1.0, lt[:, 0:4], ALU.add, ALU.mult, p)
        q = V.ts(sp[:, :], sp[:, :], -4.0, 0.0, ALU.mult, ALU.max, p)
        q = V.stt(sp4[:, 0:4], lt[:, 8:12], 8.0, sp[:, :], ALU.mult, ALU.add, q)
        q = V.ts(sp4[:, 4:8], sp4[:, 0:4], -1.0, None, ALU.mult, None, q)
        q = V.ts(ba[:, :], ba[:, :], 0.5, None, ALU.mult, None, q)
        TT["lru"] = V.ts(bx[:, :], bx[:, :], 0.5, None, ALU.mult, None, q)
        TT["m"] = m

    def row_product(out, scale_row, base_row, *after):
        return V.stt(out[:, :], scale_row[:, :], 1.0, base_row[:, :], ALU.add, ALU.mult, *after)

    def rms(t, row, shift, dst, ready, *after):
        x, st = X[t], ST[t]
        m = [V.stats(st[:, 6 * h:6 * h + 6], x[:, 512 * h:512 * h + 512], *ready) for h in range(2)]
        m = V.aggr(st[:, 12:14], st[:, 0:12], *m)
        e = V.stt(st[:, 14:15], st[:, 12:13], st[:, 12:13], st[:, 13:14], ALU.mult, ALU.add, m)
        e = V.ts(st[:, 14:15], st[:, 14:15], RMS_EPS, None, ALU.add, None, e)
        z = [None, None]

        def gained(h):
            def f():
                c = slice(512 * h, 512 * h + 512)
                z[h] = V.tt(dst[:, c], x[:, c], row[:, c], ALU.mult, *ready, *after)
            return f

        r = rsqrt(st[:, 14:15], st[:, 15:16], st[:, 16:17], st[:, 17:18], e, [gained(0), gained(1)])
        out = []
        for h in range(2):
            c = slice(512 * h, 512 * h + 512)
            out.append(V.stt(dst[:, c], dst[:, c], st[:, 15:16], shift[:, c], ALU.mult, ALU.add, r, z[h]))
        return out

    def second_branches(t, ev, out):
        c, st, s = C[t], ST[t], state[t]
        b0, b1 = ACC[t]
        both = [b0, b1]
        bf = [s["acc_free"], s["acc_free"]]
        n_k = 128 * (t + 1)

        def cc4(ap):
            return ap.rearrange("p (c n) -> p c n", c=4)

        xrt = cc4(c["xrt"][:, :])
        big = c["big"]
        xc, grt, tp, ig = (big[:, 512 * i:512 * i + 512] for i in range(4))
        m = P.turn([(b0[:, 128 * k:128 * k + 128], tp[:, 128 * k:128 * k + 128]) for k in range(4)], ident[:, :], ev["xr"], bf[0])
        x1 = A.copy(xrt[:, :, 3:131], cc4(b0[:, :]), m)
        bf[0] = x1
        if t == 0:
            x0 = V.memset(xrt[:, :, 0:3], 0.0)
        else:
            x0 = V.copy(xrt[:, :, 0:3], cc4(C[0]["xrt"][:, :])[:, :, 128:131], TT["xrt0"])
        if t == 0:
            TT["xrt0"] = x1
        yield "gr"
        mg = P.turn([(b1[:, 128 * k:128 * k + 128], ig[:, 128 * k:128 * k + 128]) for k in range(4)], ident[:, :], ev["gr"], bf[1])
        gr = A.copy(grt, b1[:, :], mg)
        bf[1] = gr
        cw = conv_w[:, :].rearrange("p (c n) -> p c n", c=4)
        x4 = cc4(xc)
        m = [V.ts(x4[:, i, :], xrt[:, i, 0:128], cw[:, i, 0:1], conv_b[:, i:i + 1], ALU.mult, ALU.add, x0, x1, TT["m"])
             for i in range(4)]
        for tap in range(1, 4):
            m = [V.stt(x4[:, i, :], xrt[:, i, tap:tap + 128], cw[:, i, tap:tap + 1], x4[:, i, :], ALU.mult, ALU.add, m[i])
                 for i in range(4)]
        yield "gr"
        ga = P.mms([(b0[:, 128 * i:128 * i + 128], lru_a[:, 128 * i:128 * i + 128], x4[:, i, :], True, True) for i in range(4)],
                   *m, bf[0], TT["m"])
        gx = P.mms([(b1[:, 128 * i:128 * i + 128], lru_x[:, 128 * i:128 * i + 128], x4[:, i, :], True, True) for i in range(4)],
                   bf[1])
        ra = [A.act(cc4(tp)[:, i, :], b0[:, 128 * i:128 * i + 128], ACT.Tanh, ga, TT["lru"], bias=ba[:, i:i + 1], scale=0.5)
              for i in range(4)]
        bf[0] = ra[3]
        rx = [A.act(cc4(ig)[:, i, :], b1[:, 128 * i:128 * i + 128], ACT.Tanh, gx, mg, bias=bx[:, i:i + 1], scale=0.5)
              for i in range(4)]
        bf[1] = rx[3]
        aa = c["aa"]
        ea = [A.act(cc4(aa[:, :])[:, i, :], cc4(tp)[:, i, :], ACT.Exp, ra[i], bias=sp4[:, 4 + i:5 + i],
                    scale=sp4[:, 4 + i:5 + i]) for i in range(4)]
        ta = [A.act(cc4(tp)[:, i, :], cc4(tp)[:, i, :], ACT.Tanh, ea[i], bias=sp4[:, i:i + 1], scale=sp4[:, i:i + 1])
              for i in range(4)]
        bb = V.stt(ig, ig, 1.0, xc, ALU.add, ALU.mult, *rx)
        yield "gr"
        sq = xrt[:, :, 0:128]
        u = V.tt(sq, cc4(aa[:, :]), cc4(aa[:, :]), ALU.mult, *ea)
        u = V.stt(cc4(tp), sq, 1.0, cc4(tp), ALU.add, ALU.mult, u, *ta)
        rt = A.act(tp, tp, ACT.Sqrt, u, scale=0.25)
        yield "gr"
        bb = V.tt(ig, ig, tp, ALU.mult, rt, bb)
        hs = []
        for i in range(4):
            init = 0.0 if t == 0 else C[0]["hl"][:, i:i + 1]
            hs.append(V.put(lambda e, i=i, init=init: e.tensor_tensor_scan(
                x4[:, i, :], cc4(aa[:, :])[:, i, :], cc4(ig)[:, i, :], init, op0=ALU.mult, op1=ALU.add),
                bb, *ea, TT.get("hl") if t else None))
        if t == 0:
            TT["hl"] = V.copy(c["hl"][:, :].unsqueeze(2), x4[:, :, 127:128], *hs)
        o = V.tt(xc, xc, grt, ALU.mult, *hs, gr, TT["hl"])
        hi = A.copy(YTH[t][:, :], xc, o, *s["yt_free"])
        lo = V.tt(YTL[t][:, :], xc, YTH[t][:, :].bitcast(F32), ALU.subtract, hi)
        out[0] = lo
        big_free = lo
        yield "sq"
        def heads(ap):
            return ap.rearrange("p (h d) -> p h d", d=64)

        ms = V.ts(st[:, 64:90], st[:, 64:90], 1.0 / 64, RMS_EPS, ALU.mult, ALU.add, *ev["ss"])
        r = rsqrt(st[:, 64:90], st[:, 90:116], st[:, 116:142], st[:, 142:168], ms)

        def normed(buf, n, first):
            return V.tt(heads(buf), heads(buf), st[:, first:first + n].unsqueeze(2).to_broadcast([128, n, 64]), ALU.mult, r)

        dk = normed(c["dk"][:, :], 8, 98)
        sk = normed(c["sk"][:, :], 2, 114)
        dq = normed(c["dq"][:, :], 8, 90)
        sq_ = normed(c["sq"][:, :], 8, 106)
        dk = G.tt(heads(c["dk"][:, :]), heads(c["dk"][:, :]), gains[1][:, :].unsqueeze(1).to_broadcast([128, 8, 64]),
                  ALU.mult, dk, TT["dg"])
        sk = G.tt(heads(c["sk"][:, :]), heads(c["sk"][:, :]), gains[3][:, :].unsqueeze(1).to_broadcast([128, 2, 64]),
                  ALU.mult, sk, TT["sg"])
        yield "sq"

        def turn4(dst, src, b, n, *after):
            m = P.turn([(both[b][:, 128 * k:128 * k + 128], src[:, 128 * k:128 * k + 128]) for k in range(n)], ident[:, :],
                       *after, bf[b])
            bf[b] = A.copy(dst, both[b][:, 0:128 * n], m)
            return bf[b]

        qt = turn4(c["dq"][:, :], c["dq"], 0, 4, dq)
        kt = turn4(c["kt"][:, :], c["dk"], 1, 4, dk)
        yield "sq"
        sqt = turn4(c["sq"][:, :], c["sq"], 0, 4, sq_)
        skt = turn4(c["skt"][:, :], c["sk"], 1, 1, sk)
        if t == 0:
            TT["kt"], TT["skt"] = kt, skt
        S_, PT = big[:, 0:1024], big[:, 1024:2048]
        O = c["dk"]
        yield "dv"
        per = 4 if t == 0 else 2
        rounds = 4 // per
        o_free = kt
        s_free, pt_free = big_free, big_free
        for kind in range(2):
            q, k_, rowk = (c["dq"], "kt", TT["kt"]) if kind == 0 else (c["sq"], "skt", TT["skt"])
            kmark = kt if kind == 0 else skt
            qmark = qt if kind == 0 else sqt
            done = []
            for rd in range(rounds):
                sv = S_.rearrange("p (u j k) -> p u j k", u=2, j=per)
                bias = bm[:, :].rearrange("p (h k) -> p h k", h=12)[:, :, 256 - n_k:256]
                sm = []
                for u in range(2):
                    ps = []
                    for j in range(per):
                        blk = rd * per + j
                        for kk in range(t + 1):
                            col = 128 * blk if kind == 0 else 0
                            ps.append((both[u][:, j * n_k + 128 * kk:j * n_k + 128 * kk + 128],
                                       q[64 * u:64 * u + 64, 128 * blk:128 * blk + 128],
                                       C[kk][k_][64 * u:64 * u + 64, col:col + 128], True, True))
                    qt_used = m = P.mms(ps, qmark, kmark, rowk, bf[u])
                    if kind == 0:
                        bv = bias[:, rd * per:rd * per + per, :]
                    else:
                        bv = bias[:, 4:12, :].rearrange("p (g u) k -> p g u k", u=2)[:, rd * per:rd * per + per, u, :]
                    bf[u] = V.stt(sv[:, u], both[u][:, 0:per * n_k].rearrange("p (j k) -> p j k", j=per), 0.125, bv,
                                  ALU.mult, ALU.add, m, TT["bias"], s_free)
                    sm.append(bf[u])
                n = 2 * per
                mx = V.reduce(st[:, 0:n], S_[:, 0:n * n_k].rearrange("p (x k) -> p x k", k=n_k), ALU.max, *sm)
                if kind == 1:
                    sk_v = sinks[:, :].rearrange("p (u g) -> p u g", u=2)[:, :, rd * per:rd * per + per]
                    mx = V.tt(st[:, 0:n].rearrange("p (u j) -> p u j", u=2), st[:, 0:n].rearrange("p (u j) -> p u j", u=2),
                              sk_v, ALU.max, mx, TT["m"])
                neg = V.ts(st[:, 8:8 + n], st[:, 0:n], -1.0, None, ALU.mult, None, mx)
                ex = [A.act(S_[:, x * n_k:x * n_k + n_k], S_[:, x * n_k:x * n_k + n_k], ACT.Exp, neg,
                            bias=st[:, 8 + x:9 + x], accum_out=st[:, 16 + x:17 + x]) for x in range(n)]
                if kind == 1:
                    es = V.tt(st[:, 24:24 + n].rearrange("p (u j) -> p u j", u=2), sk_v,
                              st[:, 0:n].rearrange("p (u j) -> p u j", u=2), ALU.subtract, mx)
                    es = A.act(st[:, 24:24 + n], st[:, 24:24 + n], ACT.Exp, es)
                    su = V.tt(st[:, 16:16 + n], st[:, 16:16 + n], st[:, 24:24 + n], ALU.add, es, *ex)
                    rs = V.recip(st[:, 32:32 + n], st[:, 16:16 + n], su)
                    yield "dv"
                    pts = []
                    for u in range(2):
                        m = P.turn([(both[u][:, 128 * i:128 * i + 128], S_[:, 512 * u + 128 * i:512 * u + 128 * i + 128])
                                    for i in range(4)], ident[:, :], *ex, bf[u])
                        bf[u] = A.copy(PT[:, 512 * u:512 * u + 512], both[u][:, :], m, pt_free)
                        pts.append(bf[u])
                    s_free = m
                    yield "dv"
                    ps = []
                    for j in range(per):
                        for u in range(2):
                            for kk in range(t + 1):
                                i = 512 * u + j * n_k + 128 * kk
                                ps.append((b0[:, 64 * (2 * j + u):64 * (2 * j + u) + 64], PT[:, i:i + 128],
                                           C[kk]["sv"][:, 64 * u:64 * u + 64], kk == 0, kk == t))
                    m = P.mms(ps, *pts, ev["skv"], TT["sv"], bf[0])
                    pt_free = m
                    ov = O[:, 128 * per * rd:128 * per * rd + 128 * per].rearrange("p (j u e) -> p j u e", j=per, u=2)
                    rv = st[:, 32:32 + n].rearrange("p (u j) -> p j u", u=2).unsqueeze(3).to_broadcast([128, per, 2, 64])
                    bf[0] = V.tt(ov, b0[:, 0:128 * per].rearrange("p (j u e) -> p j u e", j=per, u=2), rv, ALU.mult, m, rs, o_free)
                    done.append(bf[0])
                else:
                    rs = V.recip(st[:, 32:32 + n], st[:, 16:16 + n], *ex)
                    rs = V.ts(st[:, 32 + per:32 + n], st[:, 32 + per:32 + n], lam[:, 2:3], None, ALU.mult, None, rs, TT["lam"])
                    at_ = []
                    for j in range(per):
                        p1 = A.act(sv[:, 1, j], sv[:, 1, j], ACT.Copy, rs, scale=st[:, 32 + per + j:33 + per + j])
                        at_.append(V.stt(sv[:, 0, j], sv[:, 0, j], st[:, 32 + j:33 + j], sv[:, 1, j], ALU.mult, ALU.add, p1))
                    yield "dv"
                    m = P.turn([(b0[:, 128 * i:128 * i + 128], S_[:, 128 * i:128 * i + 128]) for i in range(4)],
                               ident[:, :], *at_, bf[0])
                    s_free = m
                    bf[0] = A.copy(PT[:, 0:512], b0[:, :], m, pt_free)
                    yield "dv"
                    ps = []
                    for j in range(per):
                        for kk in range(t + 1):
                            i = j * n_k + 128 * kk
                            blk = rd * per + j
                            ps.append((b1[:, 128 * j:128 * j + 128], PT[:, i:i + 128],
                                       C[kk]["dv"][:, 128 * blk:128 * blk + 128], kk == 0, kk == t))
                    m = P.mms(ps, bf[0], ev["dv"], TT["dv"], bf[1])
                    pt_free = m
                    bf[1] = A.copy(O[:, 128 * per * rd:128 * per * rd + 128 * per], b1[:, 0:128 * per], m, o_free)
                    done.append(bf[1])
                yield "dv"
            if kind == 0:
                q2 = A.act(PT[:, 0:512], O[:, :], ACT.Square, *done, pt_free)
                pt_free = q2
                v = V.reduce(st[:, 0:4], PT[:, 0:512].rearrange("p (h e) -> p h e", h=4), ALU.add, q2)
                v = V.ts(st[:, 0:4], st[:, 0:4], 1.0 / 128, RMS_EPS, ALU.mult, ALU.add, v)
                r = rsqrt(st[:, 0:4], st[:, 4:8], st[:, 8:12], st[:, 12:16], v)
                o4 = O[:, :].rearrange("p (h e) -> p h e", h=4)
                y = V.tt(o4, o4, st[:, 4:8].unsqueeze(2).to_broadcast([128, 4, 128]), ALU.mult, r)
                y = G.tt(o4, o4, subln[:, :].unsqueeze(1).to_broadcast([128, 4, 128]), ALU.mult, y, TT["sub"])
                done = [y]
                pt_free = y

            def turned(done=done, b=kind, O=O):
                m = P.turn([(both[b][:, 128 * k:128 * k + 128], O[:, 128 * k:128 * k + 128]) for k in range(4)], ident[:, :],
                           *done, bf[b])
                h = A.copy(YTH[t][:, :], both[b][:, :], m, *s["yt_free"])
                l = V.tt(YTL[t][:, :], both[b][:, :], YTH[t][:, :].bitcast(F32), ALU.subtract, h)
                bf[b] = l
                s["acc_free"], s["b1_free"] = bf
                return l

            out[kind + 1] = turned
            if kind == 0:
                O, o_free = c["dq"], qt_used
            yield "dv"
        yield "end"

    def hybrid(t, xt):
        s, st, c = state[t], ST[t], C[t]
        ev, out, done = {}, {}, set()
        side = second_branches(t, ev, out)
        need = ["xr"]

        def step():
            if need[0] in done:
                need[0] = next(side)

        def group(w, nk, *parts):
            b, free = take()
            for i, part in enumerate(parts):
                m = chunk_use(t, group_products(t, b, w, part, nk), free if i == 0 else None, xt[0], xt[1])
                if i < len(parts) - 1:
                    step()
                    yield 0.0
            return b, m

        tmp = MERGED[t]
        sq_free = [s["h_turned"]] * 2
        ss = ev["ss"] = []
        big = c["big"]

        def squares(b, w, m, first, half):
            q = A.act(tmp[:, 512 * half:512 * half + w], b[:, 0:w], ACT.Square, m, sq_free[half])
            r = V.reduce(st[:, first:first + w // 64], tmp[:, 512 * half:512 * half + w].rearrange("p (h d) -> p h d", d=64),
                         ALU.add, q)
            sq_free[half] = r
            ss.append(r)
            return q

        b, m = yield from group(512, 4, 0, 1)
        ev["xr"] = A.copy(big[:, 1024:1536], b[:, :], m)
        give(b, ev["xr"])
        done.add("xr")
        yield 0.0
        b, m = yield from group(512, 4, 0, 1)
        ev["gr"] = A.act(big[:, 1536:2048], b[:, :], ACT.Gelu_apprx_tanh, m)
        give(b, ev["gr"])
        done.add("gr")
        step()
        yield 0.0
        for i, name in enumerate(("dq", "dk")):
            b, m = yield from group(512, 4, 0, 1)
            squares(b, 512, m, 64 + 8 * i, i)
            e = A.copy(c[name][:, :], b[:, :], m)
            give(b, e)
            step()
            yield 0.0
        b, m = yield from group(256, 8, 0)
        squares(b, 128, m, 88, 0)
        e = A.copy(c["sk"][:, :], b[:, 0:128], m)
        ev["skv"] = A.copy(c["sv"][:, :], b[:, 128:256], m)
        if t == 0:
            TT["sv"] = ev["skv"]
        give(b, ev["skv"])
        step()
        yield 0.0
        b, m = yield from group(512, 4, 0, 1)
        squares(b, 512, m, 80, 1)
        e = A.copy(c["sq"][:, :], b[:, :], m)
        ss.append(e)
        give(b, e)
        done.add("sq")
        step()
        yield 0.0
        b, m = yield from group(512, 4, 0, 1)
        ev["dv"] = A.copy(c["dv"][:, :], b[:, :], m)
        if t == 0:
            TT["dv"] = ev["dv"]
        give(b, ev["dv"])
        done.add("dv")
        step()
        yield 0.0
        gate, merged = GATE[t], MERGED[t]
        gate_free, total = [s["rows_free"]] * 2, [None, None]
        for n in range(3):
            th = []
            for h in range(2):
                cs = slice(512 * h, 512 * h + 512)
                b, m = yield from group(512, 4, 0, 1)
                th.append(A.act(gate[:, cs], b[:, :], ACT.Tanh, m, gate_free[h], scale=0.5))
                give(b, th[h])
                step()
                if n == 2 and h == 1:
                    s["xt_free"] = m
                yield 0.0
            while n not in out:
                step()
                yield 1.0
            ready = out[n]
            if n:
                ready = ready()
                yield 1.5

            def lhs(k):
                return YTH[t][:, 128 * k:128 * k + 128], YTL[t][:, 128 * k:128 * k + 128]

            bs = [take(), take()]
            for part in range(2):
                m = chunk_use(t, wide_products(lhs, [bs[0][0], bs[1][0]], 0, 3, 2 * part), ready, bs[0][1], bs[1][1])
                if part == 0:
                    step()
                    yield 0.0
            s["yt_free"] = [m, m]
            for h in range(2):
                cs = slice(512 * h, 512 * h + 512)
                if n == 0:
                    total[h] = V.stt(merged[:, cs], gate[:, cs], 1.0, bs[h][0][:, :], ALU.add, ALU.mult, m, th[h], *ss)
                    give(bs[h][0], total[h])
                else:
                    pr = V.stt(gate[:, cs], gate[:, cs], 1.0, bs[h][0][:, :], ALU.add, ALU.mult, m, th[h])
                    give(bs[h][0], pr)
                    adder = V if n == 2 else G
                    total[h] = adder.tt(merged[:, cs], merged[:, cs], gate[:, cs], ALU.add, pr, total[h])
                gate_free[h] = total[h]
            step()
            yield 0.0
        yield 1.5
        done_, turned_ = xt_from(t, merged, total, s["xt_free"])
        s["merged_free"] = turned_
        yield 1.5
        for i in range(4):
            m = chunk_use(t, wide_products(lambda k: xk(t, k), ACC[t], 0, KD - 1, 2 * i), done_[i // 2],
                          s["acc_free"], s["b1_free"])
            if i < 3:
                yield 0.0
        s["xt_free"] = m
        s["down"] = m

    def route(t, ready):
        s, c, r = state[t], C[t], RT[t]
        ht = [c["aa"], c["dk"]]
        turned = []
        for j in range(2):
            b, free = take()
            m = P.turn([(b[:, 128 * k:128 * k + 128], MERGED[t][:, 512 * j + 128 * k:512 * j + 128 * k + 128]) for k in range(4)],
                       ident[:, :], ready[j], free)
            h = A.copy(ht[j][:, :], b[:, :], m)
            give(b, h)
            turned.append(h)
        yield 1.2
        b, free = take()
        m = P.mms([(b[:, 0:32], ht[k // 4][:, 128 * (k % 4):128 * (k % 4) + 128], w_router[:, 32 * k:32 * k + 32], k == 0,
                    k == KD - 1) for k in range(KD)], *turned, free, TT["m"])
        lg, sel, pos, gp = r[:, 0:32], r[:, 32:64], r[:, 64:96], r[:, 248:376]
        m8, ex, su, rc, ng = r[:, 96:104], r[:, 104:108], r[:, 108:109], r[:, 109:110], r[:, 110:111]
        m = V.tt(lg, b[:, 0:32], b_router[:, :], ALU.add, m)
        give(b, m)
        mx = V.put(lambda e: e.max(m8, lg), m)
        ix = V.put(lambda e: e.max_index(RI[t][:, :], m8, lg), mx)
        ix = V.copy(r[:, 244:248], RI[t][:, 0:4], ix)
        ng_ = V.ts(ng, m8[:, 0:1], -1.0, None, ALU.mult, None, mx)
        e = A.act(ex, m8[:, 0:4], ACT.Exp, ng_, bias=ng, accum_out=su)
        z = V.memset(gp, 0.0)
        oh = [V.ts(r[:, 116 + 32 * k:148 + 32 * k], iota[:, 0:32], r[:, 244 + k:245 + k], None, ALU.is_equal, None, ix, IOTA[0])
              for k in range(4)]
        rc_ = V.recip(rc, su, e)
        w = V.ts(ex, ex, rc, None, ALU.mult, None, rc_)
        m, g = oh[0], z
        for k in range(4):
            one = r[:, 116 + 32 * k:148 + 32 * k]
            g = V.stt(gp[:, 0:32], one, ex[:, k:k + 1], gp[:, 0:32], ALU.mult, ALU.add, g, w, oh[k])
            if k == 1:
                m = V.tt(sel, r[:, 116:148], one, ALU.add, *oh)
            elif k > 1:
                m = V.tt(sel, sel, one, ALU.add, m)
        s["gp"], s["sel"] = g, m
        yield 4.0
        b, free = take()
        ps = [(b[:, 0:32], before[:, :], sel, True, t == 0)]
        if t:
            ps.append((b[:, 0:32], ones[:, 0:1].to_broadcast([128, 128]), RT[0][:, 32:64], False, True))
        pm = P.mms(ps, m, state[0]["sel"], free, SB_SMALL["const"], TT["m"])
        p = V.stt(pos, b[:, 0:32], -999.0, sel, ALU.add, ALU.mult, pm)
        give(b, p)
        s["pos"] = V.ts(pos, pos, 999.0, None, ALU.add, None, p)

    def experts():
        PA, PB, PC, PM = bank[4:8]
        free = {n: m for b, m in spare for n, x in (("A", PA), ("B", PB), ("C", PC), ("M", PM)) if b is x}
        acc_free = [state[t]["acc_free"] for t in range(NT)]
        ring_in, ring_used, extra_in, extra_used = {}, {}, {}, {}
        sel_free, selt_free, xe_free, y_free = [None, None], [None, None], [None, None], [None, None]
        last = dict(selw=None, act=None, actt=None, bias=None)
        sel, xe, selt, ymark = {}, {}, {}, {}

        def ring(e, k):
            if e < N_EXP:
                n = 12 * e + k
                return RING[n % NRING], ring_in[n]
            n = 12 * (e - N_EXP) + k
            return RING[n % 4], extra_in[n]

        def ring_load(n):
            if n < 12 * N_EXP:
                e, k = divmod(n, 12)
                after = [ring_used[n - NRING]] if n >= NRING else RING_AFTER[n]
                ring_in[n] = S.load(ring_slot[n % NRING], RING[n % NRING][:, :],
                                    a["w1"][e, k] if k < 8 else a["w2"][e, k - 8], *after)

        def extra_load(n):
            k = n % 12
            src = a["w1" if k < 8 else "w2"]
            extra_in[n] = S.load(extra_slot[n % 4], RING[n % 4][:, :],
                                 lambda: src[bass.ds(S.regs["e"], 1), k % 8].rearrange("a p c -> (a p) c"),
                                 extra_used[n - 4] if n >= 4 else ring_used[12 * (N_EXP - 1) - 4 + n])

        def ring_over(e, k, mark):
            if e < N_EXP:
                ring_used[12 * e + k] = mark
                ring_load(12 * e + k + NRING)
            else:
                extra_used[12 * (e - N_EXP) + k] = mark
                if k < 8:
                    extra_load(12 * (e - N_EXP) + k + 4)

        def selections(i, x, pos, weight, *after):
            m, w = [], []
            for t in range(NT):
                m.append(V.ts(SEL[x][:, 64 * t:64 * t + 64], iota[:, 0:64], pos(t), None, ALU.is_equal, None,
                              *after, IOTA[0], sel_free[x]))
                w.append(V.ts(SELW[:, 128 * t:128 * t + 128], iota[:, :], pos(t), weight(t), ALU.is_equal, ALU.mult,
                              *after, last["selw"]))
            sel[i] = m, w

        def gather(i, x):
            m = P.mms([(PM[:, 64 * k:64 * k + 64], MERGED[t][:, 128 * k:128 * k + 128], SEL[x][:, 64 * t:64 * t + 64],
                        t == 0, t == NT - 1) for k in range(KD) for t in range(NT)], *sel[i][0], free["M"])
            sel_free[x] = m
            free["M"] = xe[i] = A.copy(XE[x][:, :], PM[:, :], m, xe_free[x])

        def turn_weights(i, x):
            m = P.turn([(PM[:, 128 * t:128 * t + 128], SELW[:, 128 * t:128 * t + 128]) for t in range(NT)], ident[:, :],
                       *sel[i][1], free["M"])
            last["selw"] = m
            free["M"] = selt[i] = A.copy(SELT[x][:, :], PM[:, 0:256], m, selt_free[x])

        def scatter(i, x, stop):
            m = P.mms([(ACC[t][g][:, :], SELT[x][64 * g:64 * g + 64, 128 * t:128 * t + 128], Y[x][64 * g:64 * g + 64, :],
                        False, stop) for t in range(NT) for g in range(2)], selt[i], ymark[i])
            selt_free[x] = y_free[x] = m
            return m

        def first_layer(i, x, bias, bias_in):
            halves = [(pb[64 * g:64 * g + 64, :], slice(1024 * j + 512 * g, 1024 * j + 512 * g + 512))
                      for j, pb in enumerate((PA, PB)) for g in range(2)]
            last["bias"] = P.mms([(o, bias[0], bias[1][:, c], True, False) for o, c in halves], bias_in, free["A"], free["B"])
            for k in range(KD):
                w, w_in = ring(i, k)
                m = P.mms([(o, XE[x][:, 64 * k:64 * k + 64], w[:, c], False, k == KD - 1) for o, c in halves], w_in, xe[i])
                ring_over(i, k, m)
            xe_free[x] = m
            free["A"] = glu = V.ts(GLU[:, :], PA[:, :], LIMIT, None, ALU.min, None, m, last["act"])
            th = A.act(TH[:, :], GLU[:, :], ACT.Tanh, glu, last["act"], scale=0.5 * SWIGLU)
            free["B"] = lin = V.ts(LIN[:, :], PB[:, :], -LIMIT, LIMIT, ALU.max, ALU.min, m, last["act"])
            glu = V.stt(GLU[:, :], TH[:, :], 1.0, GLU[:, :], ALU.add, ALU.mult, th)
            return V.stt(GLU[:, :], LIN[:, :], 1.0, GLU[:, :], ALU.add, ALU.mult, glu, lin)

        def turn_act(glu):
            m = P.turn([(PC[:, 128 * j:128 * j + 128], GLU[:, 128 * j:128 * j + 128]) for j in range(4)], ident[:, :],
                       glu, free["C"])
            last["act"] = m
            return A.copy(ACTT[:, :], PC[:, :], m, last["actt"])

        def second_layer(i, x, act):
            for q in range(4):
                ps = []
                w, w_in = ring(i, 8 + q)
                for j in range(2):
                    c = 2 * q + j
                    lhs = ACTT[:, 128 * (c % 4) + 64 * (c // 4):128 * (c % 4) + 64 * (c // 4) + 64]
                    ps += [(PC[64 * g:64 * g + 64, :], lhs, w[:, 1024 * j + 512 * g:1024 * j + 512 * g + 512],
                            c == 0, c == KD - 1) for g in range(2)]
                m = P.mms(ps, w_in, act)
                ring_over(i, 8 + q, m)
            last["actt"] = m
            free["C"] = ymark[i] = A.act(Y[x][:, :], PC[:, :], ACT.Copy, m, y_free[x], scale=0.5)

        def select_expert(e):
            selections(e, e % 2, lambda t: RT[t][:, 64 + e:65 + e], lambda t: RT[t][:, 248 + e:249 + e],
                       state[0]["pos"], state[1]["pos"], state[0]["gp"], state[1]["gp"])

        for n in range(NRING):
            ring_load(n)
        G.load(b_slot, b1s[0:32, :], a["b1"], *B_AFTER)
        b_in = G.load(b_slot, b2s[0:32, :], a["b2"], *B_AFTER)
        gt = []
        for t in range(NT):
            m = P.turn([(PC[:, 128 * t:128 * t + 128], RT[t][:, 248:376])], ident[:, :], state[t]["gp"], free["C"])
            gt.append(A.copy(GT[0:32, 128 * t:128 * t + 128], PC[0:32, 128 * t:128 * t + 128], m, *B_AFTER))
            free["C"] = gt[t]
        select_expert(0)
        gather(0, 0)
        turn_weights(0, 0)
        P.mms([(ACC[t][g][:, :], GT[0:32, 128 * t:128 * t + 128], b2s[0:32, 512 * g:512 * g + 512], True, False)
               for t in range(NT) for g in range(2)], *gt, b_in, *acc_free)
        m = P.mms([(PM[:, 0:32], ones[:, 0:1].to_broadcast([128, 128]), RT[t][:, 32:64], t == 0, t == NT - 1)
                   for t in range(NT)], state[0]["sel"], state[1]["sel"], free["M"])
        own, before_, with_, one_ = (EX[:, 32 * i:32 * i + 32] for i in range(4))
        v = V.ts(own, PM[:, 0:32], 64.0, None, ALU.is_gt, None, m, *B_AFTER)
        for bound in (128.0, 192.0):
            v = V.stt(own, PM[:, 0:32], bound, own, ALU.is_gt, ALU.add, v)
        free["M"] = v
        o = V.memset(one_, 1.0)
        v = V.put(lambda e: e.tensor_tensor_scan(with_, one_, own, 0.0, op0=ALU.mult, op1=ALU.add), v, o)
        summed = V.tt(before_, with_, own, ALU.subtract, v)
        n_extra = V.copy(EXI[:, 0:1], with_[:, 31:32], v)
        def extra_items():
            engines = (S, V, A, P)
            kept = dict(free), dict(last), list(sel_free), list(selt_free), list(xe_free), list(y_free)
            for name, q in zip(("sp", "dve", "act", "pe"), engines):
                q.read("n", EXI[0:1, 0:1], 0, N_EXTRA, n_extra)
                q.only_if_more("n", 0)
                q.enter(sem(f"{name}_extra"))
            bias_slot = [sem("extra_b_in"), 0]
            num, pos, weight, tmp = EX[:, 128:129], EX[:, 129:131], EX[:, 131:133], EX[:, 224:256]
            pos_of = [EX[:, 160 + 32 * t:192 + 32 * t] for t in range(NT)]
            v = V.ts(tmp, before_, 64.0, -64.0, ALU.mult, ALU.add, summed)
            for t in range(NT):
                v = V.tt(pos_of[t], RT[t][:, 64:96], tmp, ALU.add, v)
            for i in range(N_EXTRA):
                e = N_EXP + i
                if i:
                    for q in engines:
                        q.only_if_more("n", i)
                v = V.ts(tmp, with_, float(i), None, ALU.is_le, None, v)
                v = V.reduce(num, tmp, ALU.add, v)
                number = V.copy(EXI[:, 1 + i:2 + i], num, v)
                v = V.stt(one_, before_, float(i), tmp, ALU.is_le, ALU.subtract, v)
                for t in range(NT):
                    for out, src in ((pos, pos_of[t]), (weight, RT[t][:, 248:280])):
                        v = V.tt(tmp, src, one_, ALU.mult, v)
                        v = V.reduce(out[:, t:t + 1], tmp, ALU.add, v)
                v = V.ts(pos, pos, -64.0 * i, None, ALU.add, None, v)
                S.read("e", EXI[0:1, 1 + i:2 + i], 0, N_EXP - 1, number)
                bias_in = S.load(bias_slot, b1s[32:33, :], lambda: a["b1"][bass.ds(S.regs["e"], 1)], last["bias"])
                for k in range(4):
                    extra_load(12 * i + k)
                selections(e, 0, lambda t: pos[:, t:t + 1], lambda t: weight[:, t:t + 1], v)
                v = sel[e][1][-1]
                gather(e, 0)
                turn_weights(e, 0)
                act = turn_act(first_layer(e, 0, (ones[32:33, 0:1].to_broadcast([1, 64]), b1s[32:33, :]), bias_in))
                second_layer(e, 0, act)
                scatter(e, 0, False)
            for q in engines:
                for i in range(N_EXTRA):
                    q.end()
                q.leave()
            free.update(kept[0])
            last.update(kept[1])
            for now, then in zip((sel_free, selt_free, xe_free, y_free), kept[2:]):
                now[:] = then

        extra_slot = [[sem(f"extra_in{i}"), 0] for i in range(4)]
        for e in range(N_EXP):
            x = e % 2
            if e == N_EXP - 1:
                scatter(e - 1, 1 - x, False)
                extra_items()
            glu = first_layer(e, x, (ident[0:32, e:e + 1].to_broadcast([32, 64]), b1s[0:32, :]), b_in)
            if 0 < e < N_EXP - 1:
                scatter(e - 1, 1 - x, False)
            if e + 1 < N_EXP:
                select_expert(e + 1)
                gather(e + 1, 1 - x)
            act = turn_act(glu)
            if e + 1 < N_EXP:
                turn_weights(e + 1, 1 - x)
            second_layer(e, x, act)
        m = scatter(N_EXP - 1, x, True)
        outs = []
        for t in range(NT):
            for g in range(2):
                c = slice(512 * g, 512 * g + 512)
                y = V.tt(TMP[:, c], ACC[t][g][:, :], BIAS[:, c], ALU.mult, m, TT["gf"], *outs)
                y = V.tt(X[t][:, c], X[t][:, c], TMP[:, c], ALU.add, y)
                outs.append(y)
        return outs

    for layer in range(DEPTH):
        def ffn_chunks(up, down, more=()):
            more = list(more)
            for g in range(NG + 1):
                if g < NG:
                    chunk_add(up[layer, 2 * g], up[layer, 2 * g + 1])
                if g:
                    chunk_add(down[layer, g - 1])
                for src in more[g:g + 1]:
                    chunk_extra(src)

        ffn_chunks(a["up1"], a["down1"], [a["w_ada"][12 * layer + i] for i in range(12)])
        chunk_add(*(a["w_in_a"][layer, i] for i in range(2)))
        chunk_add(*(a["w_in_b"][layer, i] for i in range(6)))
        chunk_add(a["w_in_c"][layer])
        for n in range(4):
            chunk_add(*(a["w_gate"][layer, 4 * n + i] for i in range(4)))
            chunk_add(a["w_branch"][layer, n])
        chunk_add(*(a["w_out"][layer, i] for i in range(4)))
        chunk_add(*(a["w_ple"][layer, i] for i in range(2)))
        chunk_add(*(a["w_ple_gate"][layer, i] for i in range(4)))
        ffn_chunks(a["up2"], a["down2"])
    chunk_add(*(a["w_in2"][i] for i in range(8)))
    chunk_add(a["w_in2_kv"])
    chunk_add(*(a["w_in2"][i] for i in range(8, 12)))
    for n in range(3):
        chunk_add(*(a["w_gate2"][4 * n + i] for i in range(4)))
        chunk_add(*(a["w_branch2"][2 * n + i] for i in range(2)))
    chunk_add(*(a["w_out2"][i] for i in range(4)))

    row2 = [sem("rows2_in"), 0]
    x_slot = [[sem(f"x_in{t}"), 0] for t in range(NT)]
    one = [sem("const_in"), 0]
    small_slot = [sem("small_in"), 0]
    small_users = []
    rows_mark = [None]

    def load_small(layer):
        for out, name in ((sgu_w, "sgu_w"), (sgu_b, "sgu_b"), (pool_w, "pool_w"), (w_uq, "w_uq"), (w_ukv, "w_ukv")):
            G.load(small_slot, out[:, :], a[name][layer], *small_users)
        for out, name in ((sgu_g, "sgu_ln_g"), (sgu_bb, "sgu_ln_b"), (pool_s, "pool_scale"), (q_gain, "mla_q_norm"),
                          (kv_gain, "mla_kv_norm")):
            m = G.load(small_slot, out[:, :], rows(a[name][layer]), *small_users)
        SB_SMALL["mark"] = m
        w = sgu_w[:, :].rearrange("p (g t) -> p g t", g=4)
        SB_SMALL["tril"] = V.tt(w, w, tril[:, :].unsqueeze(1).to_broadcast([128, 4, 128]), ALU.mult, m,
                                SB_SMALL["const"])

    def setup():
        for t in range(NT):
            state[t]["x_in"] = S.load(x_slot[t], X[t][:, :], a["x"][128 * t:128 * t + 128])
        G.load(one, ident[:, :], a["ident"])
        G.load(one, ones[:, :], a["ones"])
        IOTA[0] = G.load(one, iota[:, :], a["iota"])
        G.load(one, cond_t[:, :], a["cond"])
        for out, name in ((decay, "decay"), (band, "band"), (tril, "tril"), (freq, "freq"), (pos_i, "pos")):
            m = G.load(one, out[:, :], a[name])
        SB_SMALL["const"] = m
        ada["cond"] = A.act(cond_t[:, :], cond_t[:, :], ACT.Silu, m)
        rows_mark[0] = load_rows(a["ln1_g"][0], a["ln1_b"][0])

    def setup_rope():
        m = SB_SMALL["const"]
        m = V.copy(pos_f[:, :], pos_i[:, :], m)
        for t in range(NT):
            m = V.ts(ang[:, 48 * t:48 * t + 48], freq[:, :], pos_f[:, t:t + 1], None, ALU.mult, None, m)
        big = 12582912.0
        m = V.ts(turns, ang, float(np.float32(1 / (2 * math.pi))), big, ALU.mult, ALU.add, m)
        m = V.ts(turns, turns, big, None, ALU.subtract, None, m)
        rest = 2 * math.pi
        for bits in (9, 11, 24):
            part = float(np.float32(rest)) if bits == 24 else math.floor(rest * 2 ** (bits - 2 - math.floor(math.log2(rest)))) / 2 ** (bits - 2 - math.floor(math.log2(rest)))
            rest -= part
            m = V.stt(ang, turns, -part, ang, ALU.mult, ALU.add, m)
        lim = 3.1415925
        c0 = V.ts(sin[:, :], ang, -lim, lim, ALU.max, ALU.min, m)
        m = V.ts(cos[:, :], ang, math.pi / 2, None, ALU.add, None, m)
        m = V.ts(turns, cos[:, :], math.pi, -2 * math.pi, ALU.is_gt, ALU.mult, m)
        m = V.tt(cos[:, :], cos[:, :], turns, ALU.add, m)
        m = V.ts(cos[:, :], cos[:, :], -lim, lim, ALU.max, ALU.min, m)
        m0 = A.act(sin[:, :], sin[:, :], ACT.Sin, c0, m)
        SB_SMALL["rope"] = A.act(cos[:, :], cos[:, :], ACT.Sin, m)

    dumps = []

    def tile(t):
        s = state[t]
        ready = [s["x_in"]] * 2
        if t == 0:
            setup_rope()
        ln = 0
        order = [("ln1_g", "ln1_b"), ("ln2_g", "ln2_b"), ("ln3_g", "ln3_b")]

        def transposed():
            done, turned = xt_from(t, X[t], ready, s["xt_free"])
            s["x"] = scale_x(t, turned, *ready)
            yield 1.2
            return done

        def norm(scale, layer, i):
            nonlocal ready
            ready, free = layer_norm(t, scale, s["down"], s["x"], rows_mark[0])
            s["acc_free"] = free
            if t == 1:
                rows_users[:] = [ready[1]]
                i, layer = (i + 1, layer) if i < 2 else (0, layer + 1)
                if layer < DEPTH:
                    rows_mark[0] = load_rows(*(a[n][layer] for n in order[i]))
                else:
                    rows_mark[0] = load_rows(mods[2], a["norm_ffn"], ada["rows"][2])

        for layer in range(DEPTH):
            done = yield from transposed()
            if t == 0:
                if layer == 0:
                    load_small(0)
            yield from ffn(t, done, s["x"])
            norm(0.5, layer, 0)
            yield 5.0
            done = yield from transposed()
            yield from mix(t, layer, done)
            norm(0.5, layer, 1)
            if t == 1:
                small_users[:] = [s["acc_free"]]
                ada["brow_free"] = s["acc_free"]
                if layer + 1 < DEPTH:
                    load_small(layer + 1)
                else:
                    G.load(small2, before[:, :], a["before"], *small_users)
                    setup_second()
            yield 0.0

            def late():
                yield 2.0
                return (yield from transposed())

            done = yield from ple(t, late)
            yield from ffn(t, done, s["x"])
            norm(0.5, layer, 2)
            if t == 0 and layer + 1 == DEPTH:
                pass
            yield 5.0
        if t == 0:
            users = [state[u]["merged_free"] for u in range(NT)]
            G.load(row2, GATE[0][:, :], rows(mods[1]), ada["rows"][1], *users)
            G.load(row2, GATE[1][:, :], rows(mods[0]), ada["rows"][0], *users)
            m = G.load(row2, MERGED[1][:, :], rows(a["norm_mix"]), *users)
            TT["rows"] = V.stt(GATE[0][:, :], GATE[0][:, :], 1.0, MERGED[1][:, :], ALU.add, ALU.mult, m)
        h = rms(t, GATE[0], GATE[1], MERGED[t], ready, TT["rows"])
        state[0]["rows_free"] = s["rows_free"] = h[1]
        yield 4.0
        done, s["h_turned"] = xt_from(t, MERGED[t], h, s["xt_free"])
        yield 1.2
        yield from hybrid(t, done)
        out = []
        for i in range(2):
            c = slice(512 * i, 512 * i + 512)
            y = V.stt(MERGED[t][:, c], ACC[t][i][:, :], 0.5, GAIN[:, c], ALU.mult, ALU.mult, s["down"], rows_mark[0],
                      s["merged_free"])
            s["acc_free"] = y
            out.append(V.tt(X[t][:, c], X[t][:, c], MERGED[t][:, c], ALU.add, y, *ready))
        if t == 0:
            users = [s["merged_free"]]
            A_f, B_f = C[0]["big"][:, 0:1024], C[0]["big"][:, 1024:2048]
            G.load(row2, A_f, rows(mods[4]), ada["rows"][4], *users)
            m = G.load(row2, B_f, rows(mods[3]), ada["rows"][3], *users)
            TT["rows_f"] = V.stt(A_f, A_f, 1.0, BIAS[:, :], ALU.add, ALU.mult, m, rows_mark[0])
        h = rms(t, C[0]["big"][:, 0:1024], C[0]["big"][:, 1024:2048], MERGED[t], out, TT["rows_f"])
        if t == 1:
            TT["gf"] = G.load(row2, BIAS[:, :], rows(mods[5]), ada["rows"][5], TT["rows_f"])
        yield 4.0
        yield from route(t, h)
        s["end"] = [s["pos"], s["gp"]]

    setup()
    tiles = [tile(t) for t in range(NT)]
    clock, ready_at, over = 0.0, [0.0, 0.0], [False, False]
    while not all(over):
        can = [t for t in range(NT) if not over[t] and (over[0] or may_use(t))]
        now = [t for t in can if ready_at[t] <= clock]
        if not now:
            clock = min(ready_at[t] for t in can)
            continue
        t = now[0]
        spent = P.cost
        delay = next(tiles[t], "end")
        clock += P.cost - spent
        if delay == "end":
            over[t] = True
        else:
            ready_at[t] = clock + delay

    over_marks = [(q.sem, q.count) for q in (V, A, P, G)]
    RING_AFTER[:] = [over_marks] * NRING
    B_AFTER[:] = over_marks
    outs = experts()
    out_slot = [[sem(f"out_done{t}"), 0] for t in range(NT)]
    for t in range(NT):
        dumps.append(S.load(out_slot[t], a["out"][128 * t:128 * t + 128], X[t][:, :], *outs))
    S.items.append((tuple(dumps), None, None, 0))

    with nc.Block() as block:
        @block.sync
        def _(e):
            S.replay(e)

        @block.tensor
        def _(e):
            P.replay(e)

        @block.vector
        def _(e):
            V.replay(e)

        @block.scalar
        def _(e):
            A.replay(e)

        @block.gpsimd
        def _(e):
            G.replay(e)

    top.close()


def chunked(w, groups, width, per):
    n = w.shape[0] // (128 * per)
    return w.reshape(n, per, 128, groups, width).transpose(3, 0, 2, 1, 4).reshape(groups * n, 128, per * width)


def wide(w):
    return w.reshape(w.shape[0] // 256, 2, 128, w.shape[1]).transpose(0, 2, 1, 3).reshape(w.shape[0] // 256, 128, -1)


def layout_up(w):
    k = w.shape[0]
    return chunked(w.reshape(k, 2, NG, 256).transpose(0, 2, 1, 3).reshape(k, -1), NG, 512, 4)


ORDER = (0, 2, 1, 3)


def layout_first(v):
    each = range(DEPTH)
    out = {}

    def stack(f):
        return np.ascontiguousarray(np.stack([f(i) for i in each]))

    out["x"] = v["x"].reshape(SEQ, D)
    out["pos"] = np.ascontiguousarray(v["positions"].reshape(NT, 128).T)
    for n in ("1", "2"):
        out["up" + n] = stack(lambda i: layout_up(v[f"ffn{n}_up"][i]))
        out["down" + n] = stack(lambda i: wide(v[f"ffn{n}_down"][i]))
    w = v["w_in"]
    out["w_in_a"] = stack(lambda i: chunked(w[i][:, 1792:2208], 1, 416, 4))
    out["w_in_b"] = stack(lambda i: np.concatenate([chunked(w[i][:, 512:1536], 2, 512, 4), chunked(w[i][:, 0:512], 1, 512, 4)]))
    out["w_in_c"] = stack(lambda i: chunked(w[i][:, 1536:1792], 1, 256, 8)[0])
    out["w_gate"] = stack(lambda i: np.concatenate(
        [chunked(w[i][:, 2208 + 1024 * n:3232 + 1024 * n], 2, 512, 4) for n in ORDER]))
    out["w_branch"] = stack(lambda i: np.concatenate([wide(v["w_branch"][i, n]) for n in ORDER]))
    out["w_out"] = stack(lambda i: wide(v["w_out"][i]))

    def ple(i):
        p = v["p"][i, 0].T.reshape(2, 128, SEQ).transpose(1, 0, 2).reshape(128, 2 * SEQ)
        w = v["w_ple"][i].reshape(2, 128, 2, 512).transpose(2, 1, 0, 3).reshape(2, 128, 1024)
        return np.stack([np.concatenate([p, w[h]], axis=1) for h in range(2)])

    out["w_ple"] = stack(ple)
    out["w_ple_gate"] = stack(lambda i: chunked(v["w_ple_gate"][i], 2, 512, 4))
    out["sgu_w"] = stack(lambda i: v["sgu_w"][i].transpose(2, 0, 1).reshape(128, 512))
    out["sgu_b"] = stack(lambda i: v["sgu_b"][i].T)

    def pool(i):
        w = np.zeros((2, 2, 64, 2, 64), np.float32)
        for g in range(4):
            w[g // 2, g % 2, :, g % 2, :] = v["pool_w"][i, g]
        return w.reshape(2, 128, 128).transpose(1, 0, 2).reshape(128, 256)

    out["pool_w"] = stack(pool)
    out["w_uq"] = stack(lambda i: v["mla_w_uq"][i].reshape(2, 128, 384).transpose(1, 0, 2).reshape(128, 768))
    out["w_ukv"] = v["mla_w_ukv"]
    for n in ("ln1_g", "ln1_b", "ln2_g", "ln2_b", "ln3_g", "ln3_b", "sgu_ln_g", "sgu_ln_b", "pool_scale", "mla_q_norm",
              "mla_kv_norm"):
        out[n] = v[n]
    return out


def layout_second(v):
    out = {}
    w = v["w_in_2"][0]
    cut = np.cumsum([0, 512, 512, 512, 512, 512, 512, 128, 128])
    xr, gr, dq, dk, dv, sq, sk, sv = (w[:, cut[i]:cut[i + 1]] for i in range(8))
    sq = sq.reshape(D, 2, 4, 64).transpose(0, 2, 1, 3).reshape(D, 512)
    out["w_in2"] = np.concatenate([chunked(x, 1, 512, 4) for x in (xr, gr, dq, dk, sq, dv)])
    out["w_in2_kv"] = chunked(np.concatenate([sk, sv], axis=1), 1, 256, 8)[0]
    out["w_gate2"] = chunked(w[:, 3328:], 6, 512, 4)
    wb = v["w_branch_2"][0]
    swa = wb[2].reshape(2, 4, 64, D).transpose(1, 0, 2, 3).reshape(512, D)
    out["w_branch2"] = np.concatenate([wide(x) for x in (wb[0], wb[1], swa)])
    out["w_out2"] = wide(v["w_out_2"][0])
    out["w_ada"] = v["w_ada_2"][0].reshape(4, 2, 128, 6, D).transpose(3, 0, 2, 1, 4).reshape(24, 128, 2 * D)
    out["b_ada"] = v["b_ada_2"].reshape(6, D)
    out["cond"] = v["c_2"].reshape(KD, 128).T
    out["norm_mix"], out["norm_ffn"] = v["norm_mix_2"][0], v["norm_ffn_2"][0]
    out["conv_w"] = v["conv_w_2"][0].reshape(4, 4, 128).transpose(2, 1, 0).reshape(128, 16)
    for n in ("conv_b", "lru_ba", "lru_bx", "lru_lambda"):
        out[n] = v[n + "_2"].reshape(4, 128).T
    for n, name in (("lru_a", "lru_wa_2"), ("lru_x", "lru_wx_2")):
        w = np.zeros((2, 64, 4, 2, 64), np.float32)
        for h in range(8):
            w[h % 2, :, h // 2, h % 2, :] = v[name][0, h]
        out[n] = w.reshape(128, 512)
    for n in ("diff_qnorm", "diff_knorm", "swa_qnorm", "swa_knorm", "diff_subln", "swa_sinks"):
        out[n] = v[n + "_2"][0]
    out["diff_lambda"] = v["diff_lambda_2"].reshape(256)
    rb = v["rel_bias_2"]
    out["rel_bias"] = np.concatenate([rb[:, 0:4], rb[:, 4:].reshape(32, 2, 4).transpose(0, 2, 1).reshape(32, 8)], axis=1)
    out["w_router"] = v["w_router_2"][0].reshape(KD, 128, N_EXP).transpose(1, 0, 2).reshape(128, KD * N_EXP)
    out["b_router"] = v["b_router_2"][0]
    out["w1"] = v["w1_2"][0].reshape(N_EXP, KD, 128, D, 2).transpose(0, 1, 2, 4, 3).reshape(N_EXP, KD, 128, 2 * D)
    out["b1"] = v["b1_2"][0].reshape(N_EXP, D, 2).transpose(0, 2, 1).reshape(N_EXP, 2 * D)
    out["w2"] = v["w2_2"][0].reshape(N_EXP, 4, 2, 128, D).transpose(0, 1, 3, 2, 4).reshape(N_EXP, 4, 128, 2 * D)
    out["b2"] = v["b2_2"][0]
    return out


def constants_second():
    out = {"ones": np.ones((128, 1), np.float32)}
    dist = 255 - np.arange(384)
    near = np.maximum(dist, 0)
    ratio = np.log(np.maximum(near, 1).astype(np.float32) / np.float32(16)) / np.float32(math.log(128 / 16))
    bucket = np.where(near < 16, near, np.minimum(16 + (ratio * np.float32(16)).astype(np.int32), 31))
    out["buckets"] = (np.arange(32)[:, None] == bucket[None, :]).astype(np.float32)
    future = np.where(dist < 0, MASKED, 0.0)[None, :].repeat(12, axis=0)
    future[4:, dist >= 128] = MASKED
    out["future"] = future.astype(np.float32)
    out["before"] = np.triu(np.ones((128, 128), np.float32), 1)
    out["iota"] = np.tile(np.arange(64, dtype=np.float32), (128, 2))
    return out


def constants_first():
    out = {"ident": np.eye(128, dtype=np.float32), "tril": np.triu(np.ones((128, 128), np.float32))}
    j, i = np.arange(128)[:, None], np.arange(128)[None, :]
    decay = np.zeros((128, 2, 2, 2, 128))
    for h in range(4):
        log_gamma = math.log1p(-2.0 ** (-5 - h))
        decay[:, h % 2, 0, h // 2] = np.exp(log_gamma * (128 + i - j))
        decay[:, h % 2, 1, h // 2] = np.where(j // 64 <= i // 64, np.exp(log_gamma * abs(i - j)), 0.0)
    out["decay"] = (decay * 0.125).astype(np.float32).reshape(128, 1024)
    band = np.zeros((128, 1088), np.float64)
    for g, window in enumerate((2, 4, 8, 16)):
        near = (j <= i) & (j > i - window)
        own = np.where(near, 1.0 / np.minimum(i + 1, window), 0.0) - (i == j)
        band[:, 128 * g:128 * g + 128] = own
        band[:, 512 + 128 * g:640 + 128 * g] = np.where(near, 1.0 / window, 0.0) - (i == j)
        t = np.arange(16)[None, :]
        band[:, 1024 + 16 * g:1040 + 16 * g] = np.where(j > 128 + t - window, 1.0 / window, 0.0)
    out["band"] = band.astype(np.float32)
    freq = [10000.0 ** (-(np.arange(0, n, 2, dtype=np.float32) / np.float32(n)).astype(np.float64)) for n in (64, 32)]
    out["freq"] = np.repeat(np.concatenate(freq).astype(np.float32)[None], 128, axis=0)
    return out


def kernel(**inputs):
    import concourse.bacc as _bacc
    from concourse.bass_utils import run_bass_kernel_spmd as _run

    arrays = {**layout_first(inputs), **layout_second(inputs), **constants_first(), **constants_second()}
    arrays = {name + "_dram": np.ascontiguousarray(x) for name, x in arrays.items()}
    nc = _bacc.Bacc("TRN2", target_bir_lowering=False, num_devices=1, dynamic_dma_scratch_size=8192)
    aps = {name[:-5]: nc.dram_tensor(name, x.shape, mybir.dt.from_np(x.dtype), kind="ExternalInput").ap()
           for name, x in arrays.items()}
    aps["out"] = nc.dram_tensor("out_dram", (SEQ, D), F32, kind="ExternalOutput").ap()
    program(nc, aps)
    r = _run(nc, [arrays], core_ids=[0])
    return r.results[0]["out_dram"].reshape(1, SEQ, D)
```

```python
import math
from contextlib import ExitStack

import numpy as np

import concourse.bass as bass
import concourse.mybir as mybir

ACT = mybir.ActivationFunctionType
ALU = mybir.AluOpType
AX = mybir.AxisListType
F32 = mybir.dt.float32
F32R = mybir.dt.float32r
I32 = mybir.dt.int32
U32 = mybir.dt.uint32

D = 1024
KD = D // 128
SEQ = 256
NT = SEQ // 128
DEPTH = 2
D_FF = 2816
NG = D_FF // 256
ALPHA = (2 * DEPTH) ** 0.25
LN_EPS = 1e-5
RMS_EPS = 1e-6
GN_EPS = 1e-5
MLA_SCALE = 96.0 ** -0.5
MASKED = -1e30
N_EXP = 32
N_EXTRA = 15
LIMIT = 7.0
SWIGLU = 1.702

N_SLOT = 10
AHEAD = 2
PENDING = 2
LEAD = 4
SLACK = 0.8
EARLY = 0.15


class Mark:

    def __init__(self, sem, count, time):
        self.sem, self.count, self.time = sem, count, time


class Later:

    def __init__(self, plan):
        self.plan, self.over, self.value, self.waiting = plan, False, None, []

    def set(self, value):
        self.over, self.value = True, value
        for work, result in self.waiting:
            self.plan.push(self.plan.now, work, result, value)


class Plan:

    def __init__(self):
        self.now, self.line, self.n, self.dma = 0.0, [], 0, 0.0

    def push(self, when, work, result, value=None):
        self.n += 1
        self.line.append((when, self.n, work, result, value))

    def later(self):
        return Later(self)

    def start(self, work, *marks):
        result = self.later()
        self.push(max([self.now] + [m.time - EARLY for m in marks if m]), work, result)
        return result

    def after(self, emit, *marks):
        def work():
            return emit()
            yield

        return self.start(work(), *marks)

    def run(self):
        while self.line:
            first = min(self.line, key=lambda x: x[:2])
            self.line.remove(first)
            when, _, work, result, value = first
            self.now = max(self.now, when)
            try:
                wait = work.send(value)
            except StopIteration as end:
                result.set(end.value)
                continue
            if isinstance(wait, Later):
                if wait.over:
                    self.push(self.now, work, result, wait.value)
                else:
                    wait.waiting.append((work, result))
            elif isinstance(wait, float):
                self.push(self.now + wait, work, result)
            else:
                marks = wait if isinstance(wait, list) else [wait]
                self.push(max([self.now] + [m.time - EARLY for m in marks if m]), work, result)


def size(ap):
    return math.prod(ap.shape[1:])


class Queue:

    LATER = 0.15

    def __init__(self, sem, plan):
        self.items, self.sem, self.count, self.plan = [], sem, 0, plan
        self.free = 0.0
        self.regs, self.outer = {}, []

    def read(self, name, src, low, high, *after):
        def emit(e):
            self.regs[name] = e.value_load(src, min_val=low, max_val=high)

        self.items.append((after, emit, None, 0))

    def only_if_more(self, name, than):
        self.items.append(("if", name, than, 0))

    def end(self):
        self.items.append(("end", None, None, 0))

    def enter(self, sem):
        self.outer.append((self.sem, self.count))
        self.sem, self.count = sem, 0

    def leave(self):
        self.sem, self.count = self.outer.pop()

    def mark(self):
        return Mark(self.sem, self.count, self.free + self.LATER)

    def put(self, emit, *after, busy=0.1):
        self.free = max([self.free, self.plan.now] + [m.time for m in after if m]) + busy
        self.count += 1
        self.items.append((after, emit, self.sem, 1))
        return self.mark()

    def replay(self, engine):
        reached, inside = {}, []
        for after, emit, sem, by in self.items:
            if after == "if":
                guard = engine.If(self.regs[emit] > sem)
                guard.__enter__()
                inside.append((guard, dict(reached)))
                continue
            if after == "end":
                guard, reached = inside.pop()
                guard.__exit__(None, None, None)
                continue
            for mark in after:
                if mark is not None and reached.get(id(mark.sem), 0) < mark.count:
                    engine.wait_ge(mark.sem, mark.count)
                    reached[id(mark.sem)] = mark.count
            if by:
                emit(engine).then_inc(sem, by)
            elif emit is not None:
                emit(engine)


class Vector(Queue):
    def takes(self, n):
        return 0.07 + n / 960

    def tt(self, out, a, b, op, *after):
        return self.put(lambda e: e.tensor_tensor(out, a, b, op=op), *after, busy=self.takes(size(out)))

    def ts(self, out, a, s1, s2, op0, op1, *after):
        busy = self.takes(size(out))
        if op1 is None:
            return self.put(lambda e: e.tensor_scalar(out, a, s1, None, op0=op0), *after, busy=busy)
        return self.put(lambda e: e.tensor_scalar(out, a, s1, s2, op0=op0, op1=op1), *after, busy=busy)

    def stt(self, out, a, s, b, op0, op1, *after):
        return self.put(lambda e: e.scalar_tensor_tensor(out, a, s, b, op0=op0, op1=op1), *after, busy=self.takes(size(out)))

    def copy(self, out, a, *after):
        return self.put(lambda e: e.tensor_copy(out, a), *after, busy=self.takes(size(out)))

    def memset(self, out, value, *after):
        return self.put(lambda e: e.memset(out, value), *after, busy=self.takes(size(out)))

    def reduce(self, out, a, op, *after):
        return self.put(lambda e: e.tensor_reduce(out, a, axis=AX.X, op=op), *after, busy=self.takes(size(a)))

    def recip(self, out, a, *after):
        return self.put(lambda e: e.reciprocal(out, a), *after, busy=0.07 + size(out) / 155)

    def stats(self, out, a, *after):
        return self.put(lambda e: e.bn_stats(out, a), *after, busy=self.takes(size(a)))

    def aggr(self, out, a, *after):
        return self.put(lambda e: e.bn_aggr(out, a), *after)


class Scalar(Queue):
    LATER = 0.2

    def copy(self, out, a, *after):
        return self.put(lambda e: e.copy(out, a), *after, busy=0.22 + size(out) / 1400)

    def act(self, out, a, func, *after, **more):
        return self.put(lambda e: e.activation(out, a, func, **more), *after, busy=0.22 + size(out) / 1400)


class Tensor(Queue):
    LATER = 0.25

    def mms(self, products, *after):
        def emit(e):
            for out, lhs, rhs, start, stop in products:
                last = e.matmul(out, lhs, rhs, start=start, stop=stop)
            return last

        return self.put(emit, *after, busy=sum(max(64, size(p[2])) * 4 / 2400 for p in products))

    def split(self, products, *after):
        def emit(e):
            for out, (xh, xl), (wh, wl), start, stop in products:
                e.matmul(out, xh, wh, start=start, stop=False)
                e.matmul(out, xh, wl, start=False, stop=False)
                last = e.matmul(out, xl, wh, start=False, stop=stop)
            return last

        return self.put(emit, *after, busy=sum(3 * (size(p[0]) + 6) / 2400 for p in products))

    def turn(self, pairs, ident, *after):
        def emit(e):
            for out, a in pairs:
                last = e.transpose(out, a, ident)
            return last

        return self.put(emit, *after, busy=0.065 * len(pairs))


class Loads(Queue):

    ISSUE = 0.06

    def load(self, slot, out, src, *after):
        slot[1] += 16
        self.items.append((after, lambda e: e.dma_start(out, src() if callable(src) else src), slot[0], 16))
        plan = self.plan
        self.free = max([self.free, plan.now] + [m.time for m in after if m]) + self.ISSUE
        plan.dma = max(plan.dma, self.free + 1.3) + out.shape[0] * size(out) * 4 / 360e3
        return Mark(slot[0], slot[1], plan.dma + 0.5)


class Pool(Vector, Loads):
    ISSUE = 1.0

    def takes(self, n):
        return 0.1 + n / 440


def rows(ap, n=128):
    return ap.unsqueeze(0).to_broadcast([n] + list(ap.shape))


def program(nc, a):
    top = ExitStack()

    def sem(name):
        return top.enter_context(nc.semaphore(name))

    def sb(name, cols, dt=F32, ctx=top):
        return ctx.enter_context(nc.sbuf_tensor("s_" + name, [128, cols], dt))

    bank = [top.enter_context(nc.psum_tensor(f"bank{i}", [128, 512], F32)) for i in range(8)]
    ACC = [[bank[0], bank[1]], [bank[2], bank[3]]]

    plan = Plan()
    V, A, P = Vector(sem("dve_a"), plan), Scalar(sem("act_a"), plan), Tensor(sem("pe_a"), plan)
    G, S = Pool(sem("pool_a"), plan), Loads(None, plan)

    ident = sb("ident", 128)
    X = [sb(f"x{t}", D) for t in range(NT)]
    MERGED = [sb(f"merged{t}", D) for t in range(NT)]
    GAIN, BIAS = sb("gain_row", D), sb("bias_row", D)
    ST = [sb(f"st{t}", 176) for t in range(NT)]
    RT = [sb(f"route{t}", 376) for t in range(NT)]
    RI = [top.enter_context(nc.sbuf_tensor(f"s_best{t}", [128, 8], U32)) for t in range(NT)]
    ones, cond_t, iota = sb("ones", 1), sb("cond", KD), sb("iota", 128)
    dense = ExitStack()

    def slots(n, name, ctx):
        loads = ExitStack()
        raw = [sb(f"{name}_raw{i}", 2048, ctx=loads) for i in range(n)]
        loads.close()
        return [(raw[i], sb(f"{name}_part{i}", 2048, F32R, ctx)) for i in range(n)]

    SLOTS = [(pair, 2) for pair in slots(N_SLOT, "w", dense)]
    XTH = [sb(f"xth{t}", D, F32R, dense) for t in range(NT)]
    XTL = [sb(f"xtl{t}", D, F32R, dense) for t in range(NT)]
    YTH = [sb(f"yth{t}", 512, F32R, dense) for t in range(NT)]
    YTL = [sb(f"ytl{t}", 512, F32R, dense) for t in range(NT)]
    GATE = [sb(f"gate{t}", D, ctx=dense) for t in range(NT)]

    spread = ExitStack()
    for t in range(NT):
        SLOTS += [(pair, t) for pair in slots(3, f"v{t}", spread)]
        sb(f"unused{t}", 384, ctx=spread)
    spread.close()
    first = ExitStack()
    sizes = dict(pr=1024, a2=1024, a3=512, a4=512, a5=256, kcat=384, q=384, ct=384, plt=256,
                 rqt=256, z=256, rv=256, rkt=256, mkt=512, mv=256)
    B = [{k: sb(f"{k}{t}", n, ctx=first) for k, n in sizes.items()} for t in range(NT)]
    RT1, RT2 = sb("rope1", 512, ctx=first), sb("rope2", 512, ctx=first)
    sgu_w, sgu_b = sb("sgu_w_t", 512, ctx=first), sb("sgu_b_t", 4, ctx=first)
    sgu_g, sgu_bb = sb("sgu_gain", 256, ctx=first), sb("sgu_bias", 256, ctx=first)
    pool_w, pool_s = sb("pool_w_t", 256, ctx=first), sb("pool_s", 256, ctx=first)
    q_gain, kv_gain = sb("q_gain", 256, ctx=first), sb("kv_gain", 128, ctx=first)
    w_uq, w_ukv = sb("w_uq_t", 768, ctx=first), sb("w_ukv_t", 512, ctx=first)
    decay = sb("decay", 1024, ctx=first)
    band = sb("band", 512 + 512 + 64, ctx=first)
    tril = sb("tril", 128, ctx=first)
    freq = sb("freq", 48, ctx=first)
    pos_i = first.enter_context(nc.sbuf_tensor("pos_i", [128, NT], I32))
    pos_f = sb("pos_f", NT, ctx=first)
    cos, sin = (sb(n, NT * 48, ctx=first) for n in ("cos_t", "sin_t"))
    ang, turns = RT1[:, :NT * 48], RT2[:, :NT * 48]

    first.close()
    second = ExitStack()
    sizes2 = dict(dq=512, dk=512, sq=512, sk=128, dv=512, sv=128, kt=512, skt=128, xrt=524, big=2048, aa=512, hl=4)
    room = sum(sizes.values()) - sum(sizes2.values())
    C = []
    for t in range(NT):
        C.append({k: sb(f"{k}_{t}", n, ctx=second) for k, n in sizes2.items()})
        sb(f"room{t}", room, ctx=second)
    bm = sb("bm", 12 * 256, ctx=second)
    gains = [sb(f"gain{i}", 64, ctx=second) for i in range(4)]
    subln, sinks, lamv, lam = (sb(n, w, ctx=second) for n, w in (("subln", 128), ("sinks", 8), ("lamv", 256), ("lam", 4)))
    conv_w, conv_b, sp, sp4, lt = (sb(n, w, ctx=second) for n, w in
                                   (("conv_w2", 16), ("conv_b2", 4), ("sp", 4), ("sp4", 8), ("lt", 12)))
    lru_a, lru_x, ba, bx = (sb(n, w, ctx=second) for n, w in (("lru_a2", 512), ("lru_x2", 512), ("ba", 4), ("bx", 4)))
    w_router, b_router = sb("w_router2", 256, ctx=second), sb("b_router2", N_EXP, ctx=second)
    rel, buckets, future = (sb(n, w, ctx=second) for n, w in (("rel", 12), ("buckets2", 384), ("future2", 384)))
    before = sb("before2", 128, ctx=second)
    second.close()
    dense.close()

    moe = ExitStack()
    NRING = 16
    RING = [sb(f"ring{i}", 2048, ctx=moe) for i in range(NRING)]
    XE = [sb(f"xe{i}", 512, ctx=moe) for i in range(2)]
    SEL = [sb(f"sel{i}", 128, ctx=moe) for i in range(2)]
    SELT = [sb(f"selt{i}", 256, ctx=moe) for i in range(2)]
    Y = [sb(f"y{i}", 512, ctx=moe) for i in range(2)]
    SELW = sb("selw", 256, ctx=moe)
    GLU, TH, LIN, ACTT = (sb(n, 512, ctx=moe) for n in ("glu", "th", "lin", "actt"))
    TMP = sb("tmp", D, ctx=moe)
    GT = sb("gt", 256, ctx=moe)
    b1s, b2s = sb("b1s", 2048, ctx=moe), sb("b2s", 1024, ctx=moe)
    EX = sb("extra", 256, ctx=moe)
    EXI = moe.enter_context(nc.sbuf_tensor("s_extra_n", [128, 1 + N_EXTRA], I32))
    moe.close()
    ring_slot = [[sem(f"ring_in{i}"), 0] for i in range(NRING)]
    b_slot = [sem("b_in"), 0]
    small2 = [sem("small2_in"), 0]
    toeplitz = nc.dram_tensor("toeplitz", [128, 12, 384], F32, kind="Internal").ap()
    RING_AFTER, B_AFTER = [()] * NRING, []

    spare = [(bank[i], None) for i in range(4, 8)]

    def take():
        while not spare:
            yield 0.1
        return spare.pop(0)

    def give(b, mark):
        spare.append((b, mark))

    FOREVER = 1 << 30
    chunks, stream, extra, at_stream = [], [], {}, {}
    slot_sem = [[sem(f"w_in{i}"), 0] for i in range(len(SLOTS))]
    unused = [(i, []) for i in range(len(SLOTS)) if SLOTS[i][1] == 2]
    away = [i for i in range(len(SLOTS)) if SLOTS[i][1] < 2]
    limit = [0, 0, FOREVER]
    loaded, lo_done, raw_of, hi_of = {}, {}, {}, {}
    at, n_loaded, n_split = [0, 0], [0], [0]
    wants = [None, None]

    def chunk_add(*srcs):
        for src in srcs:
            at_stream[len(chunks)] = len(stream)
            stream.append((src, len(chunks)))
            chunks.append(src)

    def chunk_extra(src):
        extra.setdefault(len(chunks), []).append(len(stream))
        stream.append((src, len(chunks)))

    def open_to(i):
        return [x for x in unused if i < limit[SLOTS[x[0]][1]]]

    def slot_take(i):
        x = open_to(i)[0]
        unused.remove(x)
        return x

    def slot_give(i, mark):
        unused.append((i, [mark]))

    def region_open(region, until, *marks):
        limit[region] = until
        for i in list(away):
            if SLOTS[i][1] == region:
                away.remove(i)
                unused.append((i, list(marks)))

    def region_end(region):
        while True:
            for x in list(unused):
                if SLOTS[x[0]][1] == region:
                    unused.remove(x)
                    away.append(x[0])
            if sum(SLOTS[i][1] == region for i in away) == sum(r == region for _, r in SLOTS):
                return
            yield 0.3

    def load_ahead():
        while n_loaded[0] < len(stream):
            j = n_loaded[0]
            src, i = stream[j]
            pending = j - n_split[0]
            if pending >= PENDING or len(open_to(i)) < (2 if pending else 1):
                return
            n, marks = slot_take(i)
            raw_of[j] = n
            loaded[j] = S.load(slot_sem[n], SLOTS[n][0][0][:, :src.shape[-1]], src, *marks)
            n_loaded[0] += 1

    def splitter():
        for i in range(len(chunks)):
            for j in extra.get(i, []):
                while j >= n_loaded[0]:
                    yield 0.2
                yield loaded[j]
                slot_give(raw_of[j], (yield from ada_chunk(j)))
                n_split[0] = j + 1
                load_ahead()
            j = at_stream[i]
            while j >= n_loaded[0] or i > at[0] + AHEAD or not open_to(i):
                yield 0.2
                load_ahead()
            hi_of[i], marks = slot_take(i)
            yield [loaded[j], *marks]
            w = chunks[i].shape[-1] // 2
            for part in range(2):
                c = slice(part * w, (part + 1) * w)
                raw, lo = (x[:, c] for x in SLOTS[raw_of[j]][0])
                hi = SLOTS[hi_of[i]][0][1][:, c]
                m = A.copy(hi, raw, loaded[j], *marks)
                yield m
                lo_done[i, part] = V.tt(lo, raw, hi.bitcast(F32), ALU.subtract, m)
            n_split[0] = j + 1
            load_ahead()

    def may_lead(i):
        return i - at[1] < (sum(i < limit[r] for _, r in SLOTS) - PENDING) // 2 - 1

    def chunk_use(t, products, *after):
        i = at[t]
        marks = [m for m in after if m]

        def can(part):
            if (i, part) not in lo_done or (i >= at[0] if t else part == 0 and not may_lead(i)):
                return False
            return max([lo_done[i, part].time] + [m.time for m in marks]) <= plan.now + SLACK

        def turn(part):
            wants[t] = lambda: can(part)
            while P.free > plan.now + SLACK or not can(part) or t and wants[0] and wants[0]():
                yield 0.1
            wants[t] = None

        halves = None
        for part in range(2):
            yield from turn(part)
            if halves is None:
                j = at_stream[i]
                halves = products(SLOTS[hi_of[i]][0][1], SLOTS[raw_of[j]][0][1])
            if halves[part]:
                mark = P.split(halves[part], lo_done[i, part], *after)
        at[t] += 1
        if t == 1:
            slot_give(raw_of[j], mark)
            slot_give(hi_of[i], mark)
            load_ahead()
        return mark

    def rsqrt(x, y, u, v, mark, between=()):
        between = list(between)

        def other():
            if between:
                between.pop(0)()

        m = V.ts(u.bitcast(I32), x.bitcast(I32), 1, None, ALU.logical_shift_right, None, mark)
        other()
        yield m
        m = V.ts(y.bitcast(I32), u.bitcast(I32), -1.0, float(0x5F3759DF), ALU.mult, ALU.add, m)
        other()
        yield m
        for _ in range(3):
            m = V.tt(u, y, y, ALU.mult, m)
            yield m
            m = V.stt(v, u, -0.5, x, ALU.mult, ALU.mult, m)
            yield m
            m = V.stt(y, v, 1.5, y, ALU.add, ALU.mult, m)
            yield m
        return m

    def split_into(th, tl, src, give_back, m, *free):
        h = A.copy(th, src, m, *free)
        yield h
        l = V.tt(tl, src, th.bitcast(F32), ALU.subtract, h)
        give_back(l)
        return l

    def xt_from(t, src, ready, xt_free):
        done = []
        for j in range(2):
            b, free = yield from take()
            yield [ready[j], free]
            m = P.turn([(b[:, 128 * k:128 * k + 128], src[:, 512 * j + 128 * k:512 * j + 128 * k + 128]) for k in range(4)],
                       ident[:, :], ready[j], free, CONST["ident"])
            c = slice(512 * j, 512 * j + 512)
            done.append(plan.start(split_into(XTH[t][:, c], XTL[t][:, c], b[:, :], lambda l, b=b: give(b, l), m, xt_free), m))
        return done, m

    def xk(t, k):
        return XTH[t][:, 128 * k:128 * k + 128], XTL[t][:, 128 * k:128 * k + 128]

    def group_products(t, b, w, part, nk=8):
        def products(hi, lo):
            out = []
            for j in range(nk):
                k = part * nk + j
                c = slice(j * w, j * w + w)
                out.append((b[:, :w], xk(t, k), (hi[:, c], lo[:, c]), k == 0, k == KD - 1))
            return out[:nk // 2], out[nk // 2:]
        return products

    def wide_products(lhs, outs, first_k, last_k, k0):
        def products(hi, lo):
            out = []
            for j in range(2):
                k = k0 + j
                for h in range(2):
                    c = slice(1024 * j + 512 * h, 1024 * j + 512 * h + 512)
                    out.append((outs[h][:, :], lhs(k), (hi[:, c], lo[:, c]), k == first_k, k == last_k))
            return out[:2], out[2:]
        return products

    def layer_norm(t, scale, pe_mark, x_mark, rows_mark):
        x, st = X[t], ST[t]
        halves = [x[:, :512], x[:, 512:]]
        yield [pe_mark, x_mark]
        y = [V.stt(halves[h], ACC[t][h][:, :], scale, halves[h], ALU.mult, ALU.add, pe_mark, x_mark) for h in range(2)]
        m = [V.stats(st[:, 6 * h:6 * h + 6], halves[h], y[h]) for h in range(2)]
        yield m
        m = V.aggr(st[:, 12:14], st[:, 0:12], *m)
        yield m
        e = V.ts(st[:, 14:15], st[:, 13:14], LN_EPS, None, ALU.add, None, m)
        z = [None, None]

        def centre(h):
            def f():
                c = slice(512 * h, 512 * h + 512)
                z[h] = V.stt(halves[h], halves[h], st[:, 12:13], GAIN[:, c], ALU.subtract, ALU.mult, m, rows_mark)
            return f

        yield e
        r = yield from rsqrt(st[:, 14:15], st[:, 15:16], st[:, 16:17], st[:, 17:18], e, [centre(0), centre(1)])
        out = []
        for h in range(2):
            c = slice(512 * h, 512 * h + 512)
            out.append(V.stt(halves[h], halves[h], st[:, 15:16], BIAS[:, c], ALU.mult, ALU.add, r, z[h]))
        return out, y[1]

    def scale_x(t, *after):
        return G.ts(X[t][:, :], X[t][:, :], ALPHA, 0.0, ALU.mult, ALU.add, *after)

    rows_slot = [sem("rows_in"), 0]
    rows_users = []

    def load_rows(g, b, *after):
        S.load(rows_slot, GAIN[:, :], rows(g), *rows_users, *after)
        return S.load(rows_slot, BIAS[:, :], rows(b), *rows_users, *after)

    CONST = {}

    state = [dict(xt_free=None, acc_free=None, b1_free=None, merged_free=None, gate_free=None, yt_free=[None, None],
                  act_free=[None, None], sel_known=plan.later()) for _ in range(NT)]

    def ffn(t, xt, first=()):
        s = state[t]
        acts, sil = [MERGED[t][:, 0:256], MERGED[t][:, 256:512]], MERGED[t][:, 512:768]
        x = [None, None]

        def activate(b, m, slot):
            silu = A.act(sil, b[:, 0:256], ACT.Silu, m, s["sil_free"])
            yield silu
            s["sil_free"] = V.tt(acts[slot], sil, b[:, 256:512], ALU.mult, silu, s["act_free"][slot])
            return s["sil_free"]

        pend = None
        for g in range(NG + 1):
            if g < NG:
                b, free = yield from take()
                x[0] = yield xt[0]
                m = yield from chunk_use(t, group_products(t, b, 512, 0, 4), free, x[0])
            if pend:
                pb, ready, slot, pg = pend
                ready = yield ready
                yield ready
                m = P.turn([(pb[:, 128 * k:128 * k + 128], acts[slot][:, 128 * k:128 * k + 128]) for k in range(2)],
                           ident[:, :], ready)
                s["act_free"][slot] = m
                c = slice(256 * slot, 256 * slot + 256)
                yt = plan.start(split_into(YTH[t][:, c], YTL[t][:, c], pb[:, :256], lambda l, pb=pb: give(pb, l), m,
                                           s["yt_free"][slot]), m)
            if g < NG:
                x[1] = yield xt[1]
                m = yield from chunk_use(t, group_products(t, b, 512, 1, 4), x[1])
                if g == 0:
                    for f in first:
                        yield f
                    s["act_free"], s["sil_free"] = [s["merged_free"]] * 2, s["merged_free"]
                if g == NG - 1:
                    s["xt_free"] = m
                now = (b, plan.start(activate(b, m, g % 2), m), g % 2, g)
            if pend:
                def lhs(k, slot=slot):
                    c = slice(256 * slot + 128 * (k % 2), 256 * slot + 128 * (k % 2) + 128)
                    return YTH[t][:, c], YTL[t][:, c]

                y = yield yt
                m = yield from chunk_use(t, wide_products(lhs, ACC[t], 0, 2 * NG - 1, 2 * pg), y,
                                         s["acc_free"] if pg == 0 else None, s["b1_free"] if pg == 0 else None)
                s["yt_free"][slot] = m
            pend = now if g < NG else None
        s["down"] = m

    def rope(src, dst, groups, half, c, s, done, *after):
        n = groups * 2 * half
        t1 = RT1[:, :n].rearrange("p (g w h) -> p g w h", g=groups, w=2)
        t2 = RT2[:, :n].rearrange("p (g w h) -> p g w h", g=groups, w=2)
        cb = c.unsqueeze(1).to_broadcast([128, groups, half])
        sb_ = s.unsqueeze(1).to_broadcast([128, groups, half])
        m = []
        for w in range(2):
            m.append(G.tt(t1[:, :, w], src[:, :, w], cb, ALU.mult, *after, *done))
            m.append(G.tt(t2[:, :, w], src[:, :, 1 - w], sb_, ALU.mult, *after, *done))
        lo = G.tt(dst[:, :, 0], t1[:, :, 0], t2[:, :, 0], ALU.subtract, *m)
        hi = G.tt(dst[:, :, 1], t1[:, :, 1], t2[:, :, 1], ALU.add, *m)
        return [lo, hi]

    rope_done = [[]]

    def branches(t, layer, ev, out, yt_used, prev_ev):
        buf, st, s = B[t], ST[t], state[t]
        b0, b1 = ACC[t]
        bf = [s["acc_free"], s["acc_free"]]
        prev = B[0]
        small = CONST["small"]
        cq = buf["a2"][:, 0:416]
        cn = buf["a2"][:, 416:800]
        c_ret, s_ret = cos[:, 48 * t:48 * t + 32], sin[:, 48 * t:48 * t + 32]
        c_mla, s_mla = cos[:, 48 * t + 32:48 * t + 48], sin[:, 48 * t + 32:48 * t + 48]

        def turned(src, ready, n):
            yt_free = (yield yt_used[n - 2]) if n > 1 else s["yt_free"][n % 2]
            b, f = yield from take()
            yield [f, *ready]
            c = slice(256 * (n % 2), 256 * (n % 2) + 256)
            m = P.turn([(b[:, 128 * k:128 * k + 128], src[:, 128 * k:128 * k + 128]) for k in range(2)], ident[:, :],
                       *ready, f)
            yield m
            l = yield from split_into(YTH[t][:, c], YTL[t][:, c], b[:, 0:256], lambda l: give(b, l), m, yt_free)
            out[n].set(l)

        ssq, cq_in = yield ev["cq"]
        yield ssq
        e0 = V.ts(st[:, 22:23], st[:, 20:21], 1.0 / 256, RMS_EPS, ALU.mult, ALU.add, ssq)
        e1 = V.ts(st[:, 23:24], st[:, 21:22], 1.0 / 128, RMS_EPS, ALU.mult, ALU.add, ssq, e0)
        r = yield from rsqrt(st[:, 22:24], st[:, 24:26], st[:, 26:28], st[:, 28:30], e1)
        n0 = V.stt(cn[:, 0:256], cq[:, 0:256], st[:, 24:25], q_gain[:, :], ALU.mult, ALU.mult, r, cq_in, small)
        n1 = V.stt(cn[:, 256:384], cq[:, 256:384], st[:, 25:26], kv_gain[:, :], ALU.mult, ALU.mult, r)
        kpe = st[:, 32:64].rearrange("p (g w h) -> p g w h", g=1, w=2)
        rope_done[0] = rope(cq[:, 384:416].rearrange("p (g w h) -> p g w h", g=1, w=2), kpe, 1, 16, c_mla, s_mla,
                            rope_done[0] + ada["row_free"], cq_in, s.get("kpe_free"), CONST["rope"])
        kpe_done = rope_done[0]
        yield [n0, n1, bf[0]]
        m = P.turn([(b0[:, 128 * k:128 * k + 128], cn[:, 128 * k:128 * k + 128]) for k in range(3)], ident[:, :],
                   n0, n1, bf[0])
        yield m
        ct = A.copy(buf["ct"][:, :], b0[:, 0:384], m)
        bf[0] = ct
        rqk = buf["pr"][:, 0:512].rearrange("p (g w h) -> p g w h", g=8, w=2)
        roped = buf["a3"][:, :].rearrange("p (g w h) -> p g w h", g=8, w=2)
        qk_in = yield ev["qk"]
        yield [qk_in, ct]
        rope_done[0] = rope(rqk, roped, 8, 32, c_ret, s_ret, rope_done[0], qk_in)
        ret_roped = rope_done[0]
        m = P.mms([(b1[:, 0:384], buf["ct"][:, 128 * k:128 * k + 128], w_uq[:, 384 * k:384 * k + 384], k == 0, k == 1)
                   for k in range(2)], ct, bf[1], small)
        mk = P.mms([(b0[:, :], buf["ct"][:, 256:384], w_ukv[:, :], True, True)], ct, bf[0])
        yield m
        qc = A.copy(buf["q"][:, :], b1[:, 0:384], m, s.get("q_free"))
        bf[1] = qc
        yield mk
        kv4 = b0[:, :].rearrange("p (h w) -> p h w", h=4)
        kc4 = buf["kcat"][:, :].rearrange("p (h w) -> p h w", h=4)
        k_nope = A.copy(kc4[:, :, 0:64], kv4[:, :, 0:64], mk)
        mv = A.copy(buf["mv"][:, :].rearrange("p (h w) -> p h w", h=4), kv4[:, :, 64:128], mk)
        bf[0] = mv
        q4 = buf["q"][:, :].rearrange("p (h w) -> p h w", h=4)[:, :, 64:96].rearrange("p h (w x) -> p h w x", w=2)
        rope_done[0] = rope(q4, q4, 4, 16, c_mla, s_mla, rope_done[0], qc)
        q_roped = rope_done[0]
        k_pe = G.copy(kc4[:, :, 64:96], st[:, 32:64].unsqueeze(1).to_broadcast([128, 4, 32]), *kpe_done, k_nope)
        s["kpe_free"] = k_pe
        yield [*ret_roped, bf[1]]
        m = P.turn([(b1[:, 128 * k:128 * k + 128], buf["a3"][:, 128 * k:128 * k + 128]) for k in range(4)], ident[:, :],
                   *ret_roped, bf[1])
        yield m
        rq = A.copy(buf["rqt"][:, :], b1[:, 0:256], m)
        rk = A.copy(buf["rkt"][:, :], b1[:, 256:512], m, s.get("rkt_free"))
        bf[1] = rk
        ev["rkt"].set(rk)
        ev["mv"].set(mv)
        rk0, mv0 = (yield prev_ev["rkt"]), (yield prev_ev["mv"])
        yield [q_roped[1], k_pe, bf[0]]
        m = P.turn([(b0[0:96, 128 * h:128 * h + 128], buf["q"][:, 96 * h:96 * h + 96]) for h in range(4)], ident[:, :],
                   *q_roped, bf[0])
        s["q_free"] = m
        yield m
        qt = A.copy(buf["a3"][0:96, :], b0[0:96, :], m)
        bf[0] = qt
        yield [rk, rk0, qt]
        sb_ = [b0, b1]
        m = []
        for par in range(2):
            ps = []
            for kt in range(t + 1):
                for h2 in range(2):
                    lo = 64 * par
                    c = (kt * 2 + h2) * 128
                    ps.append((sb_[par][:, c:c + 128], B[kt]["rkt"][lo:lo + 64, 128 * h2:128 * h2 + 128],
                               buf["rqt"][lo:lo + 64, 128 * h2:128 * h2 + 128], True, True))
            m.append(P.mms(ps, rq, rk, rk0, bf[par]))
        yield m
        w = 256 * (t + 1)
        d4 = decay[:, :].rearrange("p (a b) -> p a b", a=2)
        rs4 = buf["a2"][:, :].rearrange("p (a b) -> p a b", a=2)
        rs = []
        for par in range(2):
            rs.append(V.tt(rs4[:, par, 0:w], sb_[par][:, 0:w], d4[:, par, 512 - w:512], ALU.mult, m[par], CONST["all"],
                           *kpe_done))
            bf[par] = rs[par]
        yield [bf[1], k_nope, k_pe]
        m = P.turn([(b1[0:96, 128 * h:128 * h + 128], buf["kcat"][:, 96 * h:96 * h + 96]) for h in range(4)], ident[:, :],
                   k_nope, k_pe, bf[1])
        yield m
        kt_ = A.copy(buf["mkt"][0:96, :], b1[0:96, :], m, s.get("mkt_free"))
        bf[1] = kt_
        ev["mkt"].set(kt_)
        uv_in = yield ev["uv"]
        yield uv_in
        gv = buf["a4"][:, 256:512]
        s0 = V.stats(st[:, 0:6], gv, uv_in)
        yield s0
        s0 = V.aggr(st[:, 12:14], st[:, 0:6], s0)
        yield s0
        e = V.ts(st[:, 14:15], st[:, 13:14], LN_EPS, None, ALU.add, None, s0)
        zz = []
        r = yield from rsqrt(st[:, 14:15], st[:, 15:16], st[:, 16:17], st[:, 17:18], e,
                             [lambda: zz.append(V.stt(gv, gv, st[:, 12:13], sgu_g[:, :], ALU.subtract, ALU.mult, s0, small))])
        gvn = V.stt(gv, gv, st[:, 15:16], sgu_bb[:, :], ALU.mult, ALU.add, r, zz[0])
        z_in, vg_in, z0, vg0 = (yield ev["z"]), (yield ev["vg"]), (yield prev_ev["z"]), (yield prev_ev["vg"])
        yield [z_in, bf[0]]
        ps = []
        for g in range(4):
            o = b0[64 * (g % 2):64 * (g % 2) + 64, 128 * (g // 2):128 * (g // 2) + 128]
            ps.append((o, buf["z"][:, 64 * g:64 * g + 64], band[:, 512 * t + 128 * g:512 * t + 128 * g + 128], True, t == 0))
            if t:
                ps.append((o[:, 0:16], prev["z"][96:128, 64 * g:64 * g + 64],
                           band[96:128, 1024 + 16 * g:1024 + 16 * g + 16], False, True))
        mp = P.mms(ps, z_in, z0, bf[0], CONST["all"])
        yield mp
        plt = A.copy(buf["plt"][:, :], b0[:, 0:256], mp)
        bf[0] = plt
        yield [*rs, gvn, bf[1], vg_in]
        ps = []
        for h in range(4):
            for kt in range(t + 1):
                c = (kt * 2 + h // 2) * 128
                ps.append((b1[:, 64 * h:64 * h + 64], rs4[:, h % 2, c:c + 128], B[kt]["rv"][:, 64 * h:64 * h + 64],
                           kt == 0, kt == t))
        for g in range(4):
            ps.append((b1[:, 256 + 64 * g:320 + 64 * g], sgu_w[:, 128 * g:128 * g + 128], gv[:, 64 * g:64 * g + 64],
                       True, True))
        mr = P.mms(ps, *rs, gvn, bf[1], vg_in, vg0, CONST["tril"])
        s["rkt_free"] = mr
        yield [mr]
        us = []
        for g in range(4):
            c = slice(64 * g, 64 * g + 64)
            us.append(V.stt(buf["a4"][:, c], b1[:, 256 + 64 * g:320 + 64 * g], sgu_b[:, g:g + 1], buf["a4"][:, c],
                            ALU.add, ALU.mult, mr, uv_in))
        plan.start(turned(buf["a4"], us, 0), *us)
        ss = [V.stats(st[:, 6 * h:6 * h + 6], b1[:, 64 * h:64 * h + 64], mr, r) for h in range(4)]
        yield ss
        mv_ = [V.aggr(st[:, 24 + 2 * h:26 + 2 * h], st[:, 6 * h:6 * h + 6], *ss, n1) for h in range(4)]
        yield mv_
        var = st[:, 24:32].rearrange("p (h w) -> p h w", w=2)
        e = V.ts(st[:, 0:4], var[:, :, 1], GN_EPS, None, ALU.add, None, *mv_)
        yield e
        r = yield from rsqrt(st[:, 0:4], st[:, 4:8], st[:, 8:12], st[:, 16:20], e)
        ry = []
        for h in range(4):
            ry.append(V.ts(buf["q"][:, 64 * h:64 * h + 64], b1[:, 64 * h:64 * h + 64], var[:, h, 0:1], st[:, 4 + h:5 + h],
                           ALU.subtract, ALU.mult, r, s["q_free"]))
        bf[1] = ry[3]
        g_in = yield ev["g"]
        yield ry
        yr = V.tt(buf["a5"][:, :], buf["a5"][:, :], buf["q"][:, 0:256], ALU.mult, *ry, g_in)
        s["q_free"] = yr
        plan.start(turned(buf["a5"], [yr], 2), yr)
        yield [plt, bf[0]]
        m = P.mms([(b0[:, 128 * g:128 * g + 128], buf["plt"][:, 128 * g:128 * g + 128], pool_w[:, 128 * g:128 * g + 128],
                    True, True) for g in range(2)], plt, bf[0], small)
        yield m
        yp = V.tt(buf["plt"][:, :], b0[:, 0:256], pool_s[:, :], ALU.mult, m)
        bf[0] = yp
        plan.start(turned(buf["plt"], [yp], 1), yp)
        kt0 = yield prev_ev["mkt"]
        yield [qt, kt_, kt0, *bf]
        n_k = 128 * (t + 1)
        sc = [b0[:, :].rearrange("p (h k) -> p h k", k=n_k), b1[:, :].rearrange("p (h k) -> p h k", k=n_k)]
        per = 4 if t == 0 else 2
        m = []
        for j in range(4 // per):
            ps = []
            for h in range(per):
                for kt in range(t + 1):
                    hh = per * j + h
                    ps.append((sc[j][:, h, 128 * kt:128 * kt + 128], buf["a3"][0:96, 128 * hh:128 * hh + 128],
                               B[kt]["mkt"][0:96, 128 * hh:128 * hh + 128], True, True))
            m.append(P.mms(ps, qt, kt_, kt0, bf[j]))
        s["mkt_free"] = m[-1]
        mx = st[:, 0:4]
        pm = buf["pr"][:, 0:4 * n_k].rearrange("p (h k) -> p h k", k=n_k)
        exps = []
        for j in range(4 // per):
            yield m[j]
            cut = V.memset(sc[j][0:64, 0:per, n_k - 64:n_k], MASKED, m[j])
            top_ = V.reduce(mx[:, per * j:per * j + per], sc[j][:, 0:per, :], ALU.max, cut, *ry)
            yield top_
            neg = V.ts(st[:, 4 + per * j:4 + per * j + per], mx[:, per * j:per * j + per], -MLA_SCALE, None, ALU.mult, None, top_)
            yield neg
            for h in range(per):
                hh = per * j + h
                ex = A.act(pm[:, hh, :], sc[j][:, h, :], ACT.Exp, neg, *ret_roped, bias=st[:, 4 + hh:5 + hh],
                           scale=MLA_SCALE, accum_out=st[:, 8 + hh:9 + hh])
                exps.append(ex)
            bf[j] = ex
        yield exps
        rsum = V.recip(st[:, 16:20], st[:, 8:12], *exps)
        pt = buf["a2"][:, 0:4 * n_k]
        ready = []
        for j in range(4 // per):
            m = P.turn([([b0, b1][j][:, 128 * i:128 * i + 128], buf["pr"][:, 512 * j + 128 * i:512 * j + 128 * i + 128])
                        for i in range(4)], ident[:, :], *exps, bf[j])
            ready.append(m)
        for j in range(4 // per):
            yield ready[j]
            ready[j] = bf[j] = A.copy(pt[:, 512 * j:512 * j + 512], [b0, b1][j][:, :], ready[j], mr)
        yield ready
        ps = []
        for h in range(4):
            for kt in range(t + 1):
                c = h * n_k + kt * 128
                ps.append((b0[:, 64 * h:64 * h + 64], pt[:, c:c + 128], B[kt]["mv"][:, 64 * h:64 * h + 64], kt == 0, kt == t))
        m = P.mms(ps, *ready, mv, mv0, bf[0])
        yield [m, rsum]
        ym = V.tt(buf["q"][:, 0:256].rearrange("p (h e) -> p h e", h=4), b0[:, 0:256].rearrange("p (h e) -> p h e", h=4),
                  st[:, 16:20].unsqueeze(2).to_broadcast([128, 4, 64]), ALU.mult, m, rsum, s["q_free"])
        s["acc_free"] = ym
        s["b1_free"] = bf[1]
        yield from turned(buf["q"], [ym], 3)
        if t == 1 and layer + 1 <= DEPTH:
            for r in range(2):
                region_open(r, region_until(r, layer + 1), *(q.mark() for q in (V, A, P, G)))
            load_ahead()

    def group_of(t, xt):
        s = state[t]

        def group(w, nk, *parts):
            b, free = yield from take()
            for i, part in enumerate(parts):
                x = [(yield xt[0])]
                if nk == 8 or part:
                    x.append((yield xt[1]))
                m = yield from chunk_use(t, group_products(t, b, w, part, nk), free if i == 0 else None, *x)
            s["xt_free"] = m
            return b, m

        return group

    def evacuate(b, m, ev, emit):
        def work():
            marks = emit()
            last = marks[-1] if isinstance(marks, tuple) else marks
            give(b, last)
            ev.set(marks)

        plan.after(work, m)

    def known(marks):
        out = []
        for m in marks:
            if isinstance(m, Later):
                m = yield m
            out.append(m[0] if isinstance(m, list) else m)
        return out

    def gated_sum(t, lhs_of, n_branch, n_chunk, out, yt_used, gate_free, merged_free):
        s = state[t]
        gate, merged = GATE[t], MERGED[t]
        group = s["group"]
        total = [None, None]
        for n in range(n_branch):
            th = [plan.later(), plan.later()]
            for h in range(2):
                c = slice(512 * h, 512 * h + 512)
                b, m = yield from group(512, 4, 0, 1)

                def squash(b=b, m=m, c=c, before=total[h], th=th[h]):
                    free = yield from known([before] if before else gate_free)
                    yield free
                    y = A.act(gate[:, c], b[:, :], ACT.Tanh, m, *free, scale=0.5)
                    give(b, y)
                    th.set(y)

                plan.start(squash(), m)
            ready = yield out[n]
            yield ready
            bs = []
            for h in range(2):
                bs.append((yield from take()))
            for i in range(n_chunk):
                m = yield from chunk_use(t, wide_products(lhs_of(n), [bs[0][0], bs[1][0]], 0, 2 * n_chunk - 1, 2 * i),
                                         ready, bs[0][1], bs[1][1])
            yt_used[n].set(m)

            def gather(h, m=m, n=n, bs=bs, th=th, before=total):
                c = slice(512 * h, 512 * h + 512)
                x = yield th[h]
                yield x
                if n == 0:
                    free = yield from known(merged_free)
                    y = V.stt(merged[:, c], gate[:, c], 1.0, bs[h][0][:, :], ALU.add, ALU.mult, m, x, *free)
                    give(bs[h][0], y)
                    return y
                y = V.stt(gate[:, c], gate[:, c], 1.0, bs[h][0][:, :], ALU.add, ALU.mult, m, x)
                give(bs[h][0], y)
                so_far = yield before[h]
                yield [y, so_far]
                return (V if n == n_branch - 1 else G).tt(merged[:, c], merged[:, c], gate[:, c], ALU.add, y, so_far)

            total = [plan.start(gather(h), m) for h in range(2)]
        total = yield from known(total)
        s["gate_free"] = total[1]
        done, s["merged_free"] = yield from xt_from(t, merged, total, s["xt_free"])
        return done

    def through_w_out(t, done):
        s = state[t]
        for i in range(4):
            x = yield done[i // 2]
            m = yield from chunk_use(t, wide_products(lambda k: xk(t, k), ACC[t], 0, KD - 1, 2 * i), x, s["acc_free"], s["b1_free"])
        s["xt_free"] = s["down"] = m

    mix_ev = {}

    def mix(t, layer, xt):
        s, buf, st = state[t], B[t], ST[t]
        ev = mix_ev[t, layer] = {n: plan.later() for n in ("cq", "qk", "vg", "g", "uv", "z", "rkt", "mkt", "mv")}
        out, yt_used = [plan.later() for _ in range(4)], [plan.later() for _ in range(4)]
        group = s["group"] = group_of(t, xt)
        side = plan.start(branches(t, layer, ev, out, yt_used, mix_ev[0, layer]))
        act_free = s["act_free"]

        b, m = yield from group(416, 4, 0, 1)
        yield from region_end(t)

        def evacuated(b, m, name, emit):
            evacuate(b, m, ev[name], lambda: emit(b, m))

        def cq(b, m):
            A.act(buf["kcat"][:, 0:256], b[:, 0:256], ACT.Square, m, accum_out=st[:, 20:21])
            q = A.act(buf["kcat"][:, 256:384], b[:, 256:384], ACT.Square, m, accum_out=st[:, 21:22])
            return q, A.copy(buf["a2"][:, 0:416], b[:, 0:416], m)

        evacuated(b, m, "cq", cq)
        b, m = yield from group(512, 4, 0, 1)
        evacuated(b, m, "qk", lambda b, m: A.copy(buf["pr"][:, 0:512], b[:, :], m))
        b, m = yield from group(512, 4, 0, 1)

        def vg(b, m):
            ev["g"].set(A.act(buf["a5"][:, :], b[:, 256:512], ACT.Silu, m))
            return A.copy(buf["rv"][:, :], b[:, 0:256], m, s.get("rv_free"))

        evacuated(b, m, "vg", vg)
        b, m = yield from group(512, 4, 0, 1)
        evacuated(b, m, "uv", lambda b, m: A.act(buf["a4"][:, :], b[:, :], ACT.Gelu_apprx_tanh, m))
        b, m = yield from group(256, 8, 0)
        evacuated(b, m, "z", lambda b, m: A.copy(buf["z"][:, :], b[:, 0:256], m, s.get("z_free")))

        def lhs_of(n):
            def lhs(k):
                c = slice(256 * (n % 2) + 128 * k, 256 * (n % 2) + 128 * k + 128)
                return YTH[t][:, c], YTL[t][:, c]
            return lhs

        done = yield from gated_sum(t, lhs_of, 4, 1, out, yt_used, [s["gate_free"]], act_free)
        s["yt_free"] = [(yield yt_used[2]), (yield yt_used[3])]
        yield side
        yield from through_w_out(t, done)

    def ple(t, xt):
        s = state[t]
        kept = []
        for h in range(2):
            b, free = yield from take()

            def products(hi, lo, b=b):
                out = []
                for k in range(2):
                    o, c = 256 * k + 128 * t, slice(512 + 512 * k, 1024 + 512 * k)
                    out.append((b[:, :], (hi[:, o:o + 128], lo[:, o:o + 128]), (hi[:, c], lo[:, c]), k == 0, k == 1))
                return [], out

            m = yield from chunk_use(t, products, free)
            kept.append(plan.later())
            evacuate(b, m, kept[h], lambda h=h, b=b, m=m: A.copy(MERGED[t][:, 512 * h:512 * h + 512], b[:, :], m,
                                                                s["merged_free"]))
        xt = yield from xt()
        group = group_of(t, xt)
        added = []
        for h in range(2):
            b, m = yield from group(512, 4, 0, 1)

            def add(h=h, b=b, m=m):
                c = slice(512 * h, 512 * h + 512)
                th = A.act(GATE[t][:, c], b[:, :], ACT.Tanh, m, s["gate_free"], scale=0.5)
                give(b, th)
                k = yield kept[h]
                yield [th, k]
                y = V.stt(MERGED[t][:, c], GATE[t][:, c], 1.0, MERGED[t][:, c], ALU.add, ALU.mult, th, k)
                yield y
                s["gate_free"] = s["merged_free"] = s["x"] = V.stt(X[t][:, c], MERGED[t][:, c], 0.5, X[t][:, c], ALU.mult, ALU.add, y, s["x"])

            added.append(plan.start(add(), m))
        return xt, added

    mods = nc.dram_tensor("mods", [6, D], F32, kind="Internal").ap()
    ada = dict(block=0, part=0, free=[None, None], rows=[], row_free=[None, None], last=None)
    brow_slot = [[sem(f"b_ada_in{h}"), 0] for h in range(2)]
    mod_slot = [[sem(f"mod_out{i}"), 0] for i in range(6)]

    def ada_row(j, m):
        acc = GATE[j % 2]
        for h, out in enumerate((RT1, RT2)):
            c = slice(512 * h, 512 * h + 512)
            row = out[0:1, :]
            brow = G.load(brow_slot[h], row, a["b_ada"][j:j + 1, c], ada["row_free"][h], *rope_done[0])
            b, free = yield from take()
            yield [m, free]
            pm = P.mms([(b[0:1, :], ones[:, 0:1], acc[:, c], True, True)], m, free)
            yield [pm, brow]
            y = V.tt(row, b[0:1, :], row, ALU.add, pm, brow)
            give(b, y)
            ada["row_free"][h] = G.load(mod_slot[j], mods[j:j + 1, c], row, y)
        ada["free"][j % 2] = pm
        ada["rows"].append(ada["row_free"][1])

    def ada_chunk(i):
        j, part = ada["block"], ada["part"]
        acc = GATE[j % 2]
        raw = SLOTS[raw_of[i]][0][0]
        m = ada["last"]
        for w in range(2):
            k = 2 * part + w
            cond = cond_t[:, k:k + 1]
            src = raw[:, 1024 * w:1024 * w + 1024]
            if k == 0:
                m = V.ts(acc[:, :], src, cond, None, ALU.mult, None, loaded[i], ada["free"][j % 2], ada["cond"])
            else:
                m = V.stt(acc[:, :], src, cond, acc[:, :], ALU.mult, ALU.add, loaded[i], m)
            yield m
        ada["last"] = m
        ada["part"] = part + 1
        if part == 3:
            ada["block"], ada["part"] = j + 1, 0
            plan.start(ada_row(j, m), m)
        return m

    TT = {}

    def load_second():
        after = small_users
        for out, name in ((before, "before"), (conv_w, "conv_w"), (conv_b, "conv_b"), (lru_a, "lru_a"), (lru_x, "lru_x"),
                          (ba, "lru_ba"), (bx, "lru_bx"), (sp, "lru_lambda"), (w_router, "w_router")):
            G.load(small2, out[:, :], a[name], *after)
        for out, name in ((gains[0], "diff_qnorm"), (gains[1], "diff_knorm"), (gains[2], "swa_qnorm"),
                          (gains[3], "swa_knorm"), (subln, "diff_subln"), (sinks, "swa_sinks"), (lamv, "diff_lambda"),
                          (b_router, "b_router")):
            G.load(small2, out[:, :], rows(a[name]), *after)
        G.load(small2, rel[0:32, :], a["rel_bias"], *after)
        G.load(small2, buckets[0:32, :], a["buckets"], *after)
        m = TT["m"] = G.load(small2, future[0:12, :], a["future"], *after)
        plan.start(parameters(m), m)

    def parameters(m):
        yield 20.0
        b, free = yield from take()
        pm = P.mms([(b[0:12, 0:384], rel[0:32, :], buckets[0:32, :], True, True)], m, free)
        yield pm
        y = V.tt(future[0:12, :], b[0:12, 0:384], future[0:12, :], ALU.add, pm)
        give(b, y)
        w = G.load([sem("toeplitz_out"), 0], toeplitz.rearrange("c h j -> h c j"),
                   future[0:12, :].unsqueeze(1).to_broadcast([12, 128, 384]), y)
        src = bass.AP(tensor=toeplitz.tensor, offset=127, ap=[[12 * 384 - 1, 128], [384, 12], [1, 256]])
        TT["bias"] = G.load([sem("toeplitz_in"), 0], bm[:, :].rearrange("p (h k) -> p h k", h=12), src, w)
        TT["dg"] = V.tt(gains[1][:, :], gains[0][:, :], gains[1][:, :], ALU.mult, m)
        TT["sg"] = V.tt(gains[3][:, :], gains[2][:, :], gains[3][:, :], ALU.mult, m)
        TT["sub"] = V.ts(subln[:, :], subln[:, :], 0.8, None, ALU.mult, None, m)
        l1 = V.tt(lamv[:, 0:64], lamv[:, 0:64], lamv[:, 64:128], ALU.mult, m)
        l2 = V.tt(lamv[:, 128:192], lamv[:, 128:192], lamv[:, 192:256], ALU.mult, m)
        yield [l1, l2]
        l3 = V.reduce(lam[:, 0:2], lamv[:, :].rearrange("p (a b) -> p a b", a=2)[:, :, 0:64], ALU.add, l1, l2)
        yield l3
        l4 = A.act(lam[:, 0:2], lam[:, 0:2], ACT.Exp, l3)
        yield l4
        l5 = V.tt(lam[:, 2:3], lam[:, 1:2], lam[:, 0:1], ALU.subtract, l4)
        yield l5
        TT["lam"] = V.ts(lam[:, 2:3], lam[:, 2:3], -0.2, None, ALU.add, None, l5)
        n1 = V.stt(lt[:, 0:4], sp[:, :], -1.0, sp[:, :], ALU.mult, ALU.max, m)
        yield n1
        n2 = A.act(lt[:, 0:4], lt[:, 0:4], ACT.Exp, n1, scale=-1.0)
        yield n2
        n3 = V.ts(lt[:, 4:8], lt[:, 0:4], 2.0, None, ALU.add, None, n2)
        yield n3
        n3 = V.recip(lt[:, 4:8], lt[:, 4:8], n3)
        yield n3
        n3 = V.tt(lt[:, 0:4], lt[:, 0:4], lt[:, 4:8], ALU.mult, n3)
        yield n3
        n4 = V.tt(lt[:, 4:8], lt[:, 0:4], lt[:, 0:4], ALU.mult, n3)
        yield n4
        p = V.ts(lt[:, 8:12], lt[:, 4:8], 1.0 / 19, None, ALU.mult, None, n4)
        for k in range(8, 0, -1):
            yield p
            p = V.stt(lt[:, 8:12], lt[:, 8:12], 1.0 / (2 * k + 1), lt[:, 4:8], ALU.add, ALU.mult, p)
        yield p
        p = V.stt(lt[:, 8:12], lt[:, 8:12], 1.0, lt[:, 0:4], ALU.add, ALU.mult, p)
        yield p
        q = V.ts(sp[:, :], sp[:, :], -4.0, 0.0, ALU.mult, ALU.max, p)
        yield q
        q = V.stt(sp4[:, 0:4], lt[:, 8:12], 8.0, sp[:, :], ALU.mult, ALU.add, q)
        yield q
        q = V.ts(sp4[:, 4:8], sp4[:, 0:4], -1.0, None, ALU.mult, None, q)
        q = V.ts(ba[:, :], ba[:, :], 0.5, None, ALU.mult, None, q)
        TT["lru"] = V.ts(bx[:, :], bx[:, :], 0.5, None, ALU.mult, None, q)

    def rms(t, row, shift, dst, ready, *after):
        x, st = X[t], ST[t]
        yield ready
        m = [V.stats(st[:, 6 * h:6 * h + 6], x[:, 512 * h:512 * h + 512], *ready) for h in range(2)]
        yield m
        m = V.aggr(st[:, 12:14], st[:, 0:12], *m)
        yield m
        e = V.stt(st[:, 14:15], st[:, 12:13], st[:, 12:13], st[:, 13:14], ALU.mult, ALU.add, m)
        yield e
        e = V.ts(st[:, 14:15], st[:, 14:15], RMS_EPS, None, ALU.add, None, e)
        z = [None, None]

        def gained(h):
            def f():
                c = slice(512 * h, 512 * h + 512)
                z[h] = V.tt(dst[:, c], x[:, c], row[:, c], ALU.mult, *ready, *after)
            return f

        yield [e, *after]
        r = yield from rsqrt(st[:, 14:15], st[:, 15:16], st[:, 16:17], st[:, 17:18], e, [gained(0), gained(1)])
        out = []
        for h in range(2):
            c = slice(512 * h, 512 * h + 512)
            out.append(V.stt(dst[:, c], dst[:, c], st[:, 15:16], shift[:, c], ALU.mult, ALU.add, r, z[h]))
        return out

    def second_branches(t, ev, out, yt_used, prev):
        c, st, s = C[t], ST[t], state[t]
        b0, b1 = ACC[t]
        both = [b0, b1]
        bf = [s["acc_free"], s["acc_free"]]
        n_k = 128 * (t + 1)

        def cc4(ap):
            return ap.rearrange("p (c n) -> p c n", c=4)

        xrt = cc4(c["xrt"][:, :])
        big = c["big"]
        xc, grt, tp, ig = (big[:, 512 * i:512 * i + 512] for i in range(4))
        xr_in = yield ev["xr"]
        yield [xr_in, bf[0]]
        m = P.turn([(b0[:, 128 * k:128 * k + 128], tp[:, 128 * k:128 * k + 128]) for k in range(4)], ident[:, :], xr_in, bf[0])
        yield m
        x1 = A.copy(xrt[:, :, 3:131], cc4(b0[:, :]), m)
        bf[0] = x1
        if t == 0:
            x0 = V.memset(xrt[:, :, 0:3], 0.0, x1)
        else:
            x0 = yield prev["xrt"]
            yield x0
            x0 = V.copy(xrt[:, :, 0:3], cc4(C[0]["xrt"][:, :])[:, :, 128:131], x0, x1)
        ev["xrt"].set(x1)
        gr_in = yield ev["gr"]
        yield [gr_in, bf[1]]
        mg = P.turn([(b1[:, 128 * k:128 * k + 128], ig[:, 128 * k:128 * k + 128]) for k in range(4)], ident[:, :], gr_in, bf[1])
        yield mg
        gr = A.copy(grt, b1[:, :], mg)
        bf[1] = gr
        cw = conv_w[:, :].rearrange("p (c n) -> p c n", c=4)
        x4 = cc4(xc)
        yield [x0, x1]
        m = [V.ts(x4[:, i, :], xrt[:, i, 0:128], cw[:, i, 0:1], conv_b[:, i:i + 1], ALU.mult, ALU.add, x0, x1, TT["m"])
             for i in range(4)]
        for tap in range(1, 4):
            yield m
            m = [V.stt(x4[:, i, :], xrt[:, i, tap:tap + 128], cw[:, i, tap:tap + 1], x4[:, i, :], ALU.mult, ALU.add, m[i])
                 for i in range(4)]
        yield [*m, *bf]
        ga = P.mms([(b0[:, 128 * i:128 * i + 128], lru_a[:, 128 * i:128 * i + 128], x4[:, i, :], True, True) for i in range(4)],
                   *m, bf[0], TT["m"])
        gx = P.mms([(b1[:, 128 * i:128 * i + 128], lru_x[:, 128 * i:128 * i + 128], x4[:, i, :], True, True) for i in range(4)],
                   bf[1])
        yield ga
        ra = [A.act(cc4(tp)[:, i, :], b0[:, 128 * i:128 * i + 128], ACT.Tanh, ga, TT["lru"], bias=ba[:, i:i + 1], scale=0.5)
              for i in range(4)]
        bf[0] = ra[3]
        yield [gx, ra[0]]
        rx = [A.act(cc4(ig)[:, i, :], b1[:, 128 * i:128 * i + 128], ACT.Tanh, gx, mg, bias=bx[:, i:i + 1], scale=0.5)
              for i in range(4)]
        bf[1] = rx[3]
        aa = c["aa"]
        yield [ra[3], rx[0]]
        ea = [A.act(cc4(aa[:, :])[:, i, :], cc4(tp)[:, i, :], ACT.Exp, ra[i], bias=sp4[:, 4 + i:5 + i],
                    scale=sp4[:, 4 + i:5 + i]) for i in range(4)]
        yield [rx[3], ea[0]]
        ta = [A.act(cc4(tp)[:, i, :], cc4(tp)[:, i, :], ACT.Tanh, ea[i], bias=sp4[:, i:i + 1], scale=sp4[:, i:i + 1])
              for i in range(4)]
        bb = V.stt(ig, ig, 1.0, xc, ALU.add, ALU.mult, *rx)
        yield ea
        sq = xrt[:, :, 0:128]
        u = V.tt(sq, cc4(aa[:, :]), cc4(aa[:, :]), ALU.mult, *ea)
        yield [u, *ta]
        u = V.stt(cc4(tp), sq, 1.0, cc4(tp), ALU.add, ALU.mult, u, *ta)
        yield u
        rt = A.act(tp, tp, ACT.Sqrt, u, scale=0.25)
        yield [rt, bb]
        bb = V.tt(ig, ig, tp, ALU.mult, rt, bb)
        init_in = None if t == 0 else (yield prev["hl"])
        yield [bb, init_in]
        hs = []
        for i in range(4):
            init = 0.0 if t == 0 else C[0]["hl"][:, i:i + 1]
            hs.append(V.put(lambda e, i=i, init=init: e.tensor_tensor_scan(
                x4[:, i, :], cc4(aa[:, :])[:, i, :], cc4(ig)[:, i, :], init, op0=ALU.mult, op1=ALU.add),
                bb, *ea, init_in, busy=0.2))
        hl = V.copy(c["hl"][:, :].unsqueeze(2), x4[:, :, 127:128], *hs)
        ev["hl"].set(hl)
        o = V.tt(xc, xc, grt, ALU.mult, *hs, gr, hl)
        yield o
        hi = A.copy(YTH[t][:, :], xc, o, *s["yt_free"])
        yield hi
        lo = V.tt(YTL[t][:, :], xc, YTH[t][:, :].bitcast(F32), ALU.subtract, hi)
        out[0].set(lo)
        big_free = lo
        def heads(ap):
            return ap.rearrange("p (h d) -> p h d", d=64)

        in_ = []
        for n in ("dq", "dk", "sk", "sq"):
            in_ += yield ev[n]
        yield in_
        ms = V.ts(st[:, 64:90], st[:, 64:90], 1.0 / 64, RMS_EPS, ALU.mult, ALU.add, *in_)
        yield ms
        r = yield from rsqrt(st[:, 64:90], st[:, 90:116], st[:, 116:142], st[:, 142:168], ms)

        def normed(buf, n, first):
            return V.tt(heads(buf), heads(buf), st[:, first:first + n].unsqueeze(2).to_broadcast([128, n, 64]), ALU.mult, r)

        dk = normed(c["dk"][:, :], 8, 98)
        dq = normed(c["dq"][:, :], 8, 90)
        dk = G.tt(heads(c["dk"][:, :]), heads(c["dk"][:, :]), gains[1][:, :].unsqueeze(1).to_broadcast([128, 8, 64]),
                  ALU.mult, dk, TT["dg"])

        def turn4(dst, src, b, n, *after):
            yield [*after, bf[b]]
            m = P.turn([(both[b][:, 128 * k:128 * k + 128], src[:, 128 * k:128 * k + 128]) for k in range(n)], ident[:, :],
                       *after, bf[b])
            yield m
            bf[b] = A.copy(dst, both[b][:, 0:128 * n], m)
            return bf[b]

        qt = yield from turn4(c["dq"][:, :], c["dq"], 0, 4, dq)
        sk = normed(c["sk"][:, :], 2, 114)
        sk = G.tt(heads(c["sk"][:, :]), heads(c["sk"][:, :]), gains[3][:, :].unsqueeze(1).to_broadcast([128, 2, 64]),
                  ALU.mult, sk, TT["sg"])
        sq_ = normed(c["sq"][:, :], 8, 106)
        kt = yield from turn4(c["kt"][:, :], c["dk"], 1, 4, dk)
        ev["kt"].set(kt)
        sqt = yield from turn4(c["sq"][:, :], c["sq"], 0, 4, sq_)
        skt = yield from turn4(c["skt"][:, :], c["sk"], 1, 1, sk)
        ev["skt"].set(skt)
        S_, PT = big[:, 0:1024], big[:, 1024:2048]
        O = c["dk"]
        per = 4 if t == 0 else 2
        rounds = 4 // per
        o_free = kt
        s_free, pt_free = big_free, big_free
        kt0, skt0 = (yield prev["kt"]), (yield prev["skt"])
        sv_in, sv0 = (yield ev["skv"]), (yield prev["skv"])
        dv_in, dv0 = (yield ev["dv"]), (yield prev["dv"])
        for kind in range(2):
            q, k_, rowk = (c["dq"], "kt", kt0) if kind == 0 else (c["sq"], "skt", skt0)
            kmark = kt if kind == 0 else skt
            qmark = qt if kind == 0 else sqt
            done = []
            for rd in range(rounds):
                sv = S_.rearrange("p (u j k) -> p u j k", u=2, j=per)
                bias = bm[:, :].rearrange("p (h k) -> p h k", h=12)[:, :, 256 - n_k:256]
                yield [qmark, kmark, rowk, s_free, *bf]
                ms = []
                for u in range(2):
                    ps = []
                    for j in range(per):
                        blk = rd * per + j
                        for kk in range(t + 1):
                            col = 128 * blk if kind == 0 else 0
                            ps.append((both[u][:, j * n_k + 128 * kk:j * n_k + 128 * kk + 128],
                                       q[64 * u:64 * u + 64, 128 * blk:128 * blk + 128],
                                       C[kk][k_][64 * u:64 * u + 64, col:col + 128], True, True))
                    qt_used = m = P.mms(ps, qmark, kmark, rowk, bf[u])
                    ms.append(m)
                sm = []
                for u in range(2):
                    if kind == 0:
                        bv = bias[:, rd * per:rd * per + per, :]
                    else:
                        bv = bias[:, 4:12, :].rearrange("p (g u) k -> p g u k", u=2)[:, rd * per:rd * per + per, u, :]
                    yield ms[u]
                    bf[u] = V.stt(sv[:, u], both[u][:, 0:per * n_k].rearrange("p (j k) -> p j k", j=per), 0.125, bv,
                                  ALU.mult, ALU.add, ms[u], TT["bias"], s_free)
                    sm.append(bf[u])
                n = 2 * per
                yield sm
                mx = V.reduce(st[:, 0:n], S_[:, 0:n * n_k].rearrange("p (x k) -> p x k", k=n_k), ALU.max, *sm)
                yield mx
                if kind == 1:
                    sk_v = sinks[:, :].rearrange("p (u g) -> p u g", u=2)[:, :, rd * per:rd * per + per]
                    mx = V.tt(st[:, 0:n].rearrange("p (u j) -> p u j", u=2), st[:, 0:n].rearrange("p (u j) -> p u j", u=2),
                              sk_v, ALU.max, mx, TT["m"])
                    yield mx
                neg = V.ts(st[:, 8:8 + n], st[:, 0:n], -1.0, None, ALU.mult, None, mx)
                yield neg
                ex = [A.act(S_[:, x * n_k:x * n_k + n_k], S_[:, x * n_k:x * n_k + n_k], ACT.Exp, neg,
                            bias=st[:, 8 + x:9 + x], accum_out=st[:, 16 + x:17 + x]) for x in range(n)]
                if kind == 1:
                    es = V.tt(st[:, 24:24 + n].rearrange("p (u j) -> p u j", u=2), sk_v,
                              st[:, 0:n].rearrange("p (u j) -> p u j", u=2), ALU.subtract, mx)
                    es = A.act(st[:, 24:24 + n], st[:, 24:24 + n], ACT.Exp, es)
                    yield [es, *ex]
                    su = V.tt(st[:, 16:16 + n], st[:, 16:16 + n], st[:, 24:24 + n], ALU.add, es, *ex)
                    yield su
                    rs = V.recip(st[:, 32:32 + n], st[:, 16:16 + n], su)
                    pts = []
                    for u in range(2):
                        pts.append(P.turn([(both[u][:, 128 * i:128 * i + 128], S_[:, 512 * u + 128 * i:512 * u + 128 * i + 128])
                                           for i in range(4)], ident[:, :], *ex, bf[u]))
                    s_free = pts[1]
                    for u in range(2):
                        yield pts[u]
                        pts[u] = bf[u] = A.copy(PT[:, 512 * u:512 * u + 512], both[u][:, :], pts[u], pt_free)
                    yield pts
                    ps = []
                    for j in range(per):
                        for u in range(2):
                            for kk in range(t + 1):
                                i = 512 * u + j * n_k + 128 * kk
                                ps.append((b0[:, 64 * (2 * j + u):64 * (2 * j + u) + 64], PT[:, i:i + 128],
                                           C[kk]["sv"][:, 64 * u:64 * u + 64], kk == 0, kk == t))
                    m = P.mms(ps, *pts, sv_in, sv0, bf[0])
                    pt_free = m
                    yield [m, rs, o_free]
                    ov = O[:, 128 * per * rd:128 * per * rd + 128 * per].rearrange("p (j u e) -> p j u e", j=per, u=2)
                    rv = st[:, 32:32 + n].rearrange("p (u j) -> p j u", u=2).unsqueeze(3).to_broadcast([128, per, 2, 64])
                    bf[0] = V.tt(ov, b0[:, 0:128 * per].rearrange("p (j u e) -> p j u e", j=per, u=2), rv, ALU.mult, m, rs, o_free)
                    done.append(bf[0])
                else:
                    yield ex
                    rs = V.recip(st[:, 32:32 + n], st[:, 16:16 + n], *ex)
                    yield rs
                    rs = V.ts(st[:, 32 + per:32 + n], st[:, 32 + per:32 + n], lam[:, 2:3], None, ALU.mult, None, rs, TT["lam"])
                    yield rs
                    p1 = [A.act(sv[:, 1, j], sv[:, 1, j], ACT.Copy, rs, scale=st[:, 32 + per + j:33 + per + j])
                          for j in range(per)]
                    at_ = []
                    for j in range(per):
                        yield p1[j]
                        at_.append(V.stt(sv[:, 0, j], sv[:, 0, j], st[:, 32 + j:33 + j], sv[:, 1, j], ALU.mult, ALU.add, p1[j]))
                    yield [*at_, bf[0]]
                    m = P.turn([(b0[:, 128 * i:128 * i + 128], S_[:, 128 * i:128 * i + 128]) for i in range(4)],
                               ident[:, :], *at_, bf[0])
                    s_free = m
                    yield m
                    bf[0] = A.copy(PT[:, 0:512], b0[:, :], m, pt_free)
                    yield [bf[0], bf[1]]
                    ps = []
                    for j in range(per):
                        for kk in range(t + 1):
                            i = j * n_k + 128 * kk
                            blk = rd * per + j
                            ps.append((b1[:, 128 * j:128 * j + 128], PT[:, i:i + 128],
                                       C[kk]["dv"][:, 128 * blk:128 * blk + 128], kk == 0, kk == t))
                    m = P.mms(ps, bf[0], dv_in, dv0, bf[1])
                    pt_free = m
                    yield m
                    bf[1] = A.copy(O[:, 128 * per * rd:128 * per * rd + 128 * per], b1[:, 0:128 * per], m, o_free)
                    done.append(bf[1])
            if kind == 0:
                yield done
                q2 = A.act(PT[:, 0:512], O[:, :], ACT.Square, *done, pt_free)
                yield q2
                v = V.reduce(st[:, 0:4], PT[:, 0:512].rearrange("p (h e) -> p h e", h=4), ALU.add, q2)
                pt_free = v
                yield v
                v = V.ts(st[:, 0:4], st[:, 0:4], 1.0 / 128, RMS_EPS, ALU.mult, ALU.add, v)
                yield v
                r = yield from rsqrt(st[:, 0:4], st[:, 4:8], st[:, 8:12], st[:, 12:16], v)
                o4 = O[:, :].rearrange("p (h e) -> p h e", h=4)
                y = V.tt(o4, o4, st[:, 4:8].unsqueeze(2).to_broadcast([128, 4, 128]), ALU.mult, r)
                yield y
                y = G.tt(o4, o4, subln[:, :].unsqueeze(1).to_broadcast([128, 4, 128]), ALU.mult, y, TT["sub"])
                done = [y]

            def turned(done, O, n):
                free = yield yt_used[n - 1]
                b, f = yield from take()
                yield [f, *done]
                m = P.turn([(b[:, 128 * k:128 * k + 128], O[:, 128 * k:128 * k + 128]) for k in range(4)], ident[:, :], *done, f)
                yield m
                l = yield from split_into(YTH[t][:, :], YTL[t][:, :], b[:, :], lambda l: give(b, l), m, free)
                out[n].set(l)

            if kind == 0:
                plan.start(turned(done, O, 1), *done)
                O, o_free = c["dq"], qt_used
            else:
                s["acc_free"], s["b1_free"] = bf
                yield from turned(done, O, 2)

    hybrid_ev = []

    def hybrid(t, xt):
        s, st, c = state[t], ST[t], C[t]
        names = ("xr", "gr", "dq", "dk", "sk", "skv", "sq", "dv", "xrt", "hl", "kt", "skt")
        ev = {n: plan.later() for n in names}
        hybrid_ev.append(ev)
        out, yt_used = [plan.later() for _ in range(3)], [plan.later() for _ in range(3)]
        group = s["group"] = group_of(t, xt)
        side = plan.start(second_branches(t, ev, out, yt_used, hybrid_ev[0]))
        tmp = MERGED[t]
        big = c["big"]

        def heads_of(name, b, m, w, first, half, before=None, more=None):
            def work():
                sq = tmp[:, 512 * half:512 * half + w]
                free = (yield ev[before])[0] if before else s["h_turned"]
                q = A.act(sq, b[:, 0:w], ACT.Square, m, free)
                e = A.copy(c[name][:, :], b[:, 0:w], m)
                last = e
                if more:
                    last = A.copy(c[more][:, :], b[:, w:2 * w], m)
                    ev["skv"].set(last)
                give(b, last)
                yield q
                r = V.reduce(st[:, first:first + w // 64], sq.rearrange("p (h d) -> p h d", d=64), ALU.add, q)
                ev[name].set([r, e])

            plan.start(work(), m)

        b, m = yield from group(512, 4, 0, 1)
        yield from region_end(t)
        evacuate(b, m, ev["xr"], lambda b=b, m=m: A.copy(big[:, 1024:1536], b[:, :], m))
        b, m = yield from group(512, 4, 0, 1)
        evacuate(b, m, ev["gr"], lambda b=b, m=m: A.act(big[:, 1536:2048], b[:, :], ACT.Gelu_apprx_tanh, m))
        b, m = yield from group(512, 4, 0, 1)
        heads_of("dq", b, m, 512, 64, 0)
        b, m = yield from group(512, 4, 0, 1)
        heads_of("dk", b, m, 512, 72, 1)
        b, m = yield from group(256, 8, 0)
        heads_of("sk", b, m, 128, 88, 0, "dq", "sv")
        b, m = yield from group(512, 4, 0, 1)
        heads_of("sq", b, m, 512, 80, 1, "dk")
        b, m = yield from group(512, 4, 0, 1)
        evacuate(b, m, ev["dv"], lambda b=b, m=m: A.copy(c["dv"][:, :], b[:, :], m))
        squares = [ev["sk"], ev["sq"]]

        def lhs_of(n):
            return lambda k: (YTH[t][:, 128 * k:128 * k + 128], YTL[t][:, 128 * k:128 * k + 128])

        done = yield from gated_sum(t, lhs_of, 3, 2, out, yt_used, rows_free, squares)
        yield side
        yield from through_w_out(t, done)

    def route(t, ready):
        s, c, r = state[t], C[t], RT[t]
        ht = [c["aa"], c["dk"]]
        lg, sel, pos, gp = r[:, 0:32], r[:, 32:64], r[:, 64:96], r[:, 248:376]
        m8, ex, su, rc, ng = r[:, 96:104], r[:, 104:108], r[:, 108:109], r[:, 109:110], r[:, 110:111]
        z = V.memset(gp, 0.0)
        turned = []
        for j in range(2):
            b, free = yield from take()
            yield [ready[j], free]
            m = P.turn([(b[:, 128 * k:128 * k + 128], MERGED[t][:, 512 * j + 128 * k:512 * j + 128 * k + 128]) for k in range(4)],
                       ident[:, :], ready[j], free)
            turned.append((b, m))
        for j, (b, m) in enumerate(turned):
            yield m
            turned[j] = A.copy(ht[j][:, :], b[:, :], m)
            give(b, turned[j])
        yield turned
        b, free = yield from take()
        m = P.mms([(b[:, 0:32], ht[k // 4][:, 128 * (k % 4):128 * (k % 4) + 128], w_router[:, 32 * k:32 * k + 32], k == 0,
                    k == KD - 1) for k in range(KD)], *turned, free, TT["m"])
        yield m
        m = V.tt(lg, b[:, 0:32], b_router[:, :], ALU.add, m)
        give(b, m)
        yield m
        mx = V.put(lambda e: e.max(m8, lg), m)
        yield mx
        ix = V.put(lambda e: e.max_index(RI[t][:, :], m8, lg), mx)
        ng_ = V.ts(ng, m8[:, 0:1], -1.0, None, ALU.mult, None, mx)
        yield [ix, ng_]
        ix = V.copy(r[:, 244:248], RI[t][:, 0:4], ix)
        e = A.act(ex, m8[:, 0:4], ACT.Exp, ng_, bias=ng, accum_out=su)
        yield ix
        oh = [V.ts(r[:, 116 + 32 * k:148 + 32 * k], iota[:, 0:32], r[:, 244 + k:245 + k], None, ALU.is_equal, None, ix, CONST["all"])
              for k in range(4)]
        yield e
        rc_ = V.recip(rc, su, e)
        m = oh[0]
        for k in range(1, 4):
            one = r[:, 116 + 32 * k:148 + 32 * k]
            yield m
            m = V.tt(sel, r[:, 116:148] if k == 1 else sel, one, ALU.add, m, *oh)
        s["sel"] = m
        s["sel_known"].set(m)
        yield [rc_, m]
        w = V.ts(ex, ex, rc, None, ALU.mult, None, rc_)
        sel0 = yield state[0]["sel_known"]
        yield [m, sel0]
        b, free = yield from take()
        ps = [(b[:, 0:32], before[:, :], sel, True, t == 0)]
        if t:
            ps.append((b[:, 0:32], ones[:, 0:1].to_broadcast([128, 128]), RT[0][:, 32:64], False, True))
        pm = P.mms(ps, m, sel0, free, CONST["all"], TT["m"])
        g = z
        for k in range(4):
            one = r[:, 116 + 32 * k:148 + 32 * k]
            yield [g, w]
            g = V.stt(gp[:, 0:32], one, ex[:, k:k + 1], gp[:, 0:32], ALU.mult, ALU.add, g, w, oh[k])
        s["gp"] = g
        yield pm
        p = V.stt(pos, b[:, 0:32], -999.0, sel, ALU.add, ALU.mult, pm)
        give(b, p)
        yield p
        s["pos"] = V.ts(pos, pos, 999.0, None, ALU.add, None, p)

    def experts():
        PA, PB, PC, PM = bank[4:8]
        free = {n: m for b, m in spare for n, x in (("A", PA), ("B", PB), ("C", PC), ("M", PM)) if b is x}
        acc_free = [state[t]["acc_free"] for t in range(NT)]
        ring_in, ring_used, extra_in, extra_used = {}, {}, {}, {}
        sel_free, selt_free, xe_free, y_free = [None, None], [None, None], [None, None], [None, None]
        last = dict(selw=None, act=None, actt=None, bias=None)
        sel, xe, selt, ymark = {}, {}, {}, {}

        def ring(e, k):
            if e < N_EXP:
                n = 12 * e + k
                return RING[n % NRING], ring_in[n]
            n = 12 * (e - N_EXP) + k
            return RING[n % 4], extra_in[n]

        def ring_load(n):
            if n < 12 * N_EXP:
                e, k = divmod(n, 12)
                after = [ring_used[n - NRING]] if n >= NRING else RING_AFTER[n]
                ring_in[n] = S.load(ring_slot[n % NRING], RING[n % NRING][:, :],
                                    a["w1"][e, k] if k < 8 else a["w2"][e, k - 8], *after)

        def extra_load(n):
            k = n % 12
            src = a["w1" if k < 8 else "w2"]
            extra_in[n] = S.load(extra_slot[n % 4], RING[n % 4][:, :],
                                 lambda: src[bass.ds(S.regs["e"], 1), k % 8].rearrange("a p c -> (a p) c"),
                                 extra_used[n - 4] if n >= 4 else ring_used[12 * (N_EXP - 1) - 4 + n])

        def ring_over(e, k, mark):
            if e < N_EXP:
                ring_used[12 * e + k] = mark
                ring_load(12 * e + k + NRING)
            else:
                extra_used[12 * (e - N_EXP) + k] = mark
                if k < 8:
                    extra_load(12 * (e - N_EXP) + k + 4)

        def selections(i, x, pos, weight, *after):
            m, w = [], []
            for t in range(NT):
                m.append(V.ts(SEL[x][:, 64 * t:64 * t + 64], iota[:, 0:64], pos(t), None, ALU.is_equal, None,
                              *after, CONST["all"], sel_free[x]))
                w.append(V.ts(SELW[:, 128 * t:128 * t + 128], iota[:, :], pos(t), weight(t), ALU.is_equal, ALU.mult,
                              *after, last["selw"]))
            sel[i] = m, w

        def gather(i, x):
            m = P.mms([(PM[:, 64 * k:64 * k + 64], MERGED[t][:, 128 * k:128 * k + 128], SEL[x][:, 64 * t:64 * t + 64],
                        t == 0, t == NT - 1) for k in range(KD) for t in range(NT)], *sel[i][0], free["M"])
            sel_free[x] = m
            free["M"] = xe[i] = A.copy(XE[x][:, :], PM[:, :], m, xe_free[x])

        def turn_weights(i, x):
            m = P.turn([(PM[:, 128 * t:128 * t + 128], SELW[:, 128 * t:128 * t + 128]) for t in range(NT)], ident[:, :],
                       *sel[i][1], free["M"])
            last["selw"] = m
            free["M"] = selt[i] = A.copy(SELT[x][:, :], PM[:, 0:256], m, selt_free[x])

        def scatter(i, x, stop):
            m = P.mms([(ACC[t][g][:, :], SELT[x][64 * g:64 * g + 64, 128 * t:128 * t + 128], Y[x][64 * g:64 * g + 64, :],
                        False, stop) for t in range(NT) for g in range(2)], selt[i], ymark[i])
            selt_free[x] = y_free[x] = m
            return m

        def first_layer(i, x, bias, bias_in):
            halves = [(pb[64 * g:64 * g + 64, :], slice(1024 * j + 512 * g, 1024 * j + 512 * g + 512))
                      for j, pb in enumerate((PA, PB)) for g in range(2)]
            last["bias"] = P.mms([(o, bias[0], bias[1][:, c], True, False) for o, c in halves], bias_in, free["A"], free["B"])
            for k in range(KD):
                w, w_in = ring(i, k)
                m = P.mms([(o, XE[x][:, 64 * k:64 * k + 64], w[:, c], False, k == KD - 1) for o, c in halves], w_in, xe[i])
                ring_over(i, k, m)
            xe_free[x] = m
            free["A"] = glu = V.ts(GLU[:, :], PA[:, :], LIMIT, None, ALU.min, None, m, last["act"])
            th = A.act(TH[:, :], GLU[:, :], ACT.Tanh, glu, last["act"], scale=0.5 * SWIGLU)
            free["B"] = lin = V.ts(LIN[:, :], PB[:, :], -LIMIT, LIMIT, ALU.max, ALU.min, m, last["act"])
            glu = V.stt(GLU[:, :], TH[:, :], 1.0, GLU[:, :], ALU.add, ALU.mult, th)
            return V.stt(GLU[:, :], LIN[:, :], 1.0, GLU[:, :], ALU.add, ALU.mult, glu, lin)

        def turn_act(glu):
            m = P.turn([(PC[:, 128 * j:128 * j + 128], GLU[:, 128 * j:128 * j + 128]) for j in range(4)], ident[:, :],
                       glu, free["C"])
            last["act"] = m
            return A.copy(ACTT[:, :], PC[:, :], m, last["actt"])

        def second_layer(i, x, act):
            for q in range(4):
                ps = []
                w, w_in = ring(i, 8 + q)
                for j in range(2):
                    c = 2 * q + j
                    lhs = ACTT[:, 128 * (c % 4) + 64 * (c // 4):128 * (c % 4) + 64 * (c // 4) + 64]
                    ps += [(PC[64 * g:64 * g + 64, :], lhs, w[:, 1024 * j + 512 * g:1024 * j + 512 * g + 512],
                            c == 0, c == KD - 1) for g in range(2)]
                m = P.mms(ps, w_in, act)
                ring_over(i, 8 + q, m)
            last["actt"] = m
            free["C"] = ymark[i] = A.act(Y[x][:, :], PC[:, :], ACT.Copy, m, y_free[x], scale=0.5)

        def select_expert(e):
            selections(e, e % 2, lambda t: RT[t][:, 64 + e:65 + e], lambda t: RT[t][:, 248 + e:249 + e],
                       state[0]["pos"], state[1]["pos"], state[0]["gp"], state[1]["gp"])

        for n in range(NRING):
            ring_load(n)
        G.load(b_slot, b1s[0:32, :], a["b1"], *B_AFTER)
        b_in = G.load(b_slot, b2s[0:32, :], a["b2"], *B_AFTER)
        gt = []
        for t in range(NT):
            m = P.turn([(PC[:, 128 * t:128 * t + 128], RT[t][:, 248:376])], ident[:, :], state[t]["gp"], free["C"])
            gt.append(A.copy(GT[0:32, 128 * t:128 * t + 128], PC[0:32, 128 * t:128 * t + 128], m, *B_AFTER))
            free["C"] = gt[t]
        select_expert(0)
        gather(0, 0)
        turn_weights(0, 0)
        P.mms([(ACC[t][g][:, :], GT[0:32, 128 * t:128 * t + 128], b2s[0:32, 512 * g:512 * g + 512], True, False)
               for t in range(NT) for g in range(2)], *gt, b_in, *acc_free)
        m = P.mms([(PM[:, 0:32], ones[:, 0:1].to_broadcast([128, 128]), RT[t][:, 32:64], t == 0, t == NT - 1)
                   for t in range(NT)], state[0]["sel"], state[1]["sel"], free["M"])
        own, before_, with_, one_ = (EX[:, 32 * i:32 * i + 32] for i in range(4))
        v = V.ts(own, PM[:, 0:32], 64.0, None, ALU.is_gt, None, m, *B_AFTER)
        for bound in (128.0, 192.0):
            v = V.stt(own, PM[:, 0:32], bound, own, ALU.is_gt, ALU.add, v)
        free["M"] = v
        o = V.memset(one_, 1.0)
        v = V.put(lambda e: e.tensor_tensor_scan(with_, one_, own, 0.0, op0=ALU.mult, op1=ALU.add), v, o)
        summed = V.tt(before_, with_, own, ALU.subtract, v)
        n_extra = V.copy(EXI[:, 0:1], with_[:, 31:32], v)
        def extra_items():
            engines = (S, V, A, P)
            kept = dict(free), dict(last), list(sel_free), list(selt_free), list(xe_free), list(y_free)
            for name, q in zip(("sp", "dve", "act", "pe"), engines):
                q.read("n", EXI[0:1, 0:1], 0, N_EXTRA, n_extra)
                q.only_if_more("n", 0)
                q.enter(sem(f"{name}_extra"))
            bias_slot = [sem("extra_b_in"), 0]
            num, pos, weight, tmp = EX[:, 128:129], EX[:, 129:131], EX[:, 131:133], EX[:, 224:256]
            pos_of = [EX[:, 160 + 32 * t:192 + 32 * t] for t in range(NT)]
            v = V.ts(tmp, before_, 64.0, -64.0, ALU.mult, ALU.add, summed)
            for t in range(NT):
                v = V.tt(pos_of[t], RT[t][:, 64:96], tmp, ALU.add, v)
            for i in range(N_EXTRA):
                e = N_EXP + i
                if i:
                    for q in engines:
                        q.only_if_more("n", i)
                v = V.ts(tmp, with_, float(i), None, ALU.is_le, None, v)
                v = V.reduce(num, tmp, ALU.add, v)
                number = V.copy(EXI[:, 1 + i:2 + i], num, v)
                v = V.stt(one_, before_, float(i), tmp, ALU.is_le, ALU.subtract, v)
                for t in range(NT):
                    for out, src in ((pos, pos_of[t]), (weight, RT[t][:, 248:280])):
                        v = V.tt(tmp, src, one_, ALU.mult, v)
                        v = V.reduce(out[:, t:t + 1], tmp, ALU.add, v)
                v = V.ts(pos, pos, -64.0 * i, None, ALU.add, None, v)
                S.read("e", EXI[0:1, 1 + i:2 + i], 0, N_EXP - 1, number)
                bias_in = S.load(bias_slot, b1s[32:33, :], lambda: a["b1"][bass.ds(S.regs["e"], 1)], last["bias"])
                for k in range(4):
                    extra_load(12 * i + k)
                selections(e, 0, lambda t: pos[:, t:t + 1], lambda t: weight[:, t:t + 1], v)
                v = sel[e][1][-1]
                gather(e, 0)
                turn_weights(e, 0)
                act = turn_act(first_layer(e, 0, (ones[32:33, 0:1].to_broadcast([1, 64]), b1s[32:33, :]), bias_in))
                second_layer(e, 0, act)
                scatter(e, 0, False)
            for q in engines:
                for i in range(N_EXTRA):
                    q.end()
                q.leave()
            free.update(kept[0])
            last.update(kept[1])
            for now, then in zip((sel_free, selt_free, xe_free, y_free), kept[2:]):
                now[:] = then

        extra_slot = [[sem(f"extra_in{i}"), 0] for i in range(4)]
        for e in range(N_EXP):
            x = e % 2
            if e == N_EXP - 1:
                scatter(e - 1, 1 - x, False)
                extra_items()
            glu = first_layer(e, x, (ident[0:32, e:e + 1].to_broadcast([32, 64]), b1s[0:32, :]), b_in)
            if 0 < e < N_EXP - 1:
                scatter(e - 1, 1 - x, False)
            if e + 1 < N_EXP:
                select_expert(e + 1)
                gather(e + 1, 1 - x)
            act = turn_act(glu)
            if e + 1 < N_EXP:
                turn_weights(e + 1, 1 - x)
            second_layer(e, x, act)
        m = scatter(N_EXP - 1, x, True)
        outs = []
        for t in range(NT):
            for g in range(2):
                c = slice(512 * g, 512 * g + 512)
                y = V.tt(TMP[:, c], ACC[t][g][:, :], BIAS[:, c], ALU.mult, m, TT["gf"], *outs)
                y = V.tt(X[t][:, c], X[t][:, c], TMP[:, c], ALU.add, y)
                outs.append(y)
        return outs

    mix_start = []

    def region_until(region, layer):
        return mix_start[layer] + (2 if region else -LEAD)

    for layer in range(DEPTH):
        def ffn_chunks(up, down, more=()):
            for g in range(NG + 1):
                if g < NG:
                    chunk_add(up[layer, 2 * g], up[layer, 2 * g + 1])
                if g:
                    chunk_add(down[layer, g - 1])
                for src in more[g - 1:g] if 0 < g < NG else more[NG - 1:] if g == NG else ():
                    chunk_extra(src)

        ffn_chunks(a["up1"], a["down1"], [a["w_ada"][12 * layer + i] for i in range(12)])
        mix_start.append(len(chunks))
        chunk_add(*(a["w_in_a"][layer, i] for i in range(2)))
        chunk_add(*(a["w_in_b"][layer, i] for i in range(6)))
        chunk_add(a["w_in_c"][layer])
        for n in range(4):
            chunk_add(*(a["w_gate"][layer, 4 * n + i] for i in range(4)))
            chunk_add(a["w_branch"][layer, n])
        chunk_add(*(a["w_out"][layer, i] for i in range(4)))
        chunk_add(*(a["w_ple"][layer, i] for i in range(2)))
        chunk_add(*(a["w_ple_gate"][layer, i] for i in range(4)))
        ffn_chunks(a["up2"], a["down2"])
    mix_start.append(len(chunks))
    chunk_add(*(a["w_in2"][i] for i in range(8)))
    chunk_add(a["w_in2_kv"])
    chunk_add(*(a["w_in2"][i] for i in range(8, 12)))
    for n in range(3):
        chunk_add(*(a["w_gate2"][4 * n + i] for i in range(4)))
        chunk_add(*(a["w_branch2"][2 * n + i] for i in range(2)))
    chunk_add(*(a["w_out2"][i] for i in range(4)))

    row2 = [sem("rows2_in"), 0]
    x_slot = [[sem(f"x_in{t}"), 0] for t in range(NT)]
    one = [sem("const_in"), 0]
    small_slot = [sem("small_in"), 0]
    small_users = []
    rows_mark = [None]
    rows_free = [plan.later() for _ in range(NT)]

    def load_small(layer):
        for out, name in ((sgu_w, "sgu_w"), (sgu_b, "sgu_b"), (pool_w, "pool_w"), (w_uq, "w_uq"), (w_ukv, "w_ukv")):
            G.load(small_slot, out[:, :], a[name][layer], *small_users)
        for out, name in ((sgu_g, "sgu_ln_g"), (sgu_bb, "sgu_ln_b"), (pool_s, "pool_scale"), (q_gain, "mla_q_norm"),
                          (kv_gain, "mla_kv_norm")):
            m = G.load(small_slot, out[:, :], rows(a[name][layer]), *small_users)
        CONST["small"] = m

        def mask():
            w = sgu_w[:, :].rearrange("p (g t) -> p g t", g=4)
            CONST["tril"] = V.tt(w, w, tril[:, :].unsqueeze(1).to_broadcast([128, 4, 128]), ALU.mult, m, CONST["all"])

        plan.after(mask, m)

    def setup():
        CONST["ident"] = S.load([sem("ident_in"), 0], ident[:, :], a["ident"])
        state[0]["x_in"] = S.load(x_slot[0], X[0][:, :], a["x"][0:128])
        for r in range(2):
            region_open(r, region_until(r, 0))
        load_ahead()
        state[1]["x_in"] = S.load(x_slot[1], X[1][:, :], a["x"][128:256])
        G.load(one, cond_t[:, :], a["cond"])
        G.load(one, ones[:, :], a["ones"])
        for out, name in ((iota, "iota"), (freq, "freq"), (pos_i, "pos"), (tril, "tril"), (decay, "decay"), (band, "band")):
            m = G.load(one, out[:, :], a[name], loaded[1])
        CONST["all"] = m

    def setup_late():
        while at[0] < 2:
            yield 0.5
        yield CONST["all"]
        ada["cond"] = A.act(cond_t[:, :], cond_t[:, :], ACT.Silu, CONST["all"])
        rows_mark[0] = load_rows(a["ln1_g"][0], a["ln1_b"][0])
        load_small(0)
        while at[0] < 8:
            yield 0.5
        yield from setup_rope()

    def setup_rope():
        m = CONST["all"]
        m = V.copy(pos_f[:, :], pos_i[:, :], m)
        for t in range(NT):
            yield m
            m = V.ts(ang[:, 48 * t:48 * t + 48], freq[:, :], pos_f[:, t:t + 1], None, ALU.mult, None, m)
        big = 12582912.0
        yield m
        m = V.ts(turns, ang, float(np.float32(1 / (2 * math.pi))), big, ALU.mult, ALU.add, m)
        yield m
        m = V.ts(turns, turns, big, None, ALU.subtract, None, m)
        rest = 2 * math.pi
        for bits in (9, 11, 24):
            unit = 2.0 ** (bits - 2 - math.floor(math.log2(rest)))
            part = float(np.float32(rest)) if bits == 24 else math.floor(rest * unit) / unit
            rest -= part
            yield m
            m = V.stt(ang, turns, -part, ang, ALU.mult, ALU.add, m)
        lim = 3.1415925
        yield m
        c0 = V.ts(sin[:, :], ang, -lim, lim, ALU.max, ALU.min, m)
        m = V.ts(cos[:, :], ang, math.pi / 2, None, ALU.add, None, m)
        yield m
        m = V.ts(turns, cos[:, :], math.pi, -2 * math.pi, ALU.is_gt, ALU.mult, m)
        yield m
        m = V.tt(cos[:, :], cos[:, :], turns, ALU.add, m)
        yield m
        m = V.ts(cos[:, :], cos[:, :], -lim, lim, ALU.max, ALU.min, m)
        yield m
        A.act(sin[:, :], sin[:, :], ACT.Sin, c0, m)
        CONST["rope"] = A.act(cos[:, :], cos[:, :], ACT.Sin, m)
        ada["row_free"] = [CONST["rope"]] * 2

    def tile(t):
        s = state[t]
        ready = [s["x_in"]] * 2
        order = [("ln1_g", "ln1_b"), ("ln2_g", "ln2_b"), ("ln3_g", "ln3_b")]

        def transposed():
            done, m = yield from xt_from(t, X[t], ready, s["xt_free"])
            s["x"] = scale_x(t, m, *ready)
            return done

        def norm(layer, i):
            nonlocal ready
            ready, s["acc_free"] = yield from layer_norm(t, 0.5, s["down"], s["x"], rows_mark[0])
            s["b1_free"] = s["acc_free"]
            if t == 1:
                rows_users[:] = [ready[1]]
                i, layer = (i + 1, layer) if i < 2 else (0, layer + 1)
                if layer < DEPTH:
                    rows_mark[0] = load_rows(*(a[n][layer] for n in order[i]))
                else:
                    rows_mark[0] = load_rows(mods[2], a["norm_ffn"], ada["rows"][2])

        for layer in range(DEPTH):
            done = yield from transposed()
            yield from ffn(t, done)
            yield from norm(layer, 0)
            done = yield from transposed()
            yield from mix(t, layer, done)
            yield from norm(layer, 1)
            if t == 1:
                small_users[:] = [s["acc_free"]]
                if layer + 1 < DEPTH:
                    load_small(layer + 1)
                else:
                    load_second()
            done, added = yield from ple(t, transposed)
            yield from ffn(t, done, added)
            yield from norm(layer, 2)
        if t == 0:
            yield from region_end(0)
            users = [state[u]["gate_free"] for u in range(NT)]
            G.load(row2, GATE[0][:, :], rows(mods[1]), ada["rows"][1], *users)
            G.load(row2, GATE[1][:, :], rows(mods[0]), ada["rows"][0], *users)
            row = C[0]["big"][:, 0:1024]
            m = G.load(row2, row, rows(a["norm_mix"]), P.mark())
            yield m
            TT["rows"] = V.stt(GATE[0][:, :], GATE[0][:, :], 1.0, row, ALU.add, ALU.mult, m)
        h = yield from rms(t, GATE[0], GATE[1], MERGED[t], ready, TT["rows"], *s["act_free"])
        rows_free[t].set(h[1])
        done, s["h_turned"] = yield from xt_from(t, MERGED[t], h, s["xt_free"])
        yield from hybrid(t, done)
        yield s["down"]
        out = []
        for i in range(2):
            c = slice(512 * i, 512 * i + 512)
            y = V.stt(MERGED[t][:, c], ACC[t][i][:, :], 0.5, GAIN[:, c], ALU.mult, ALU.mult, s["down"], rows_mark[0],
                      s["merged_free"])
            s["acc_free"] = y
            out.append(V.tt(X[t][:, c], X[t][:, c], MERGED[t][:, c], ALU.add, y, *ready))
        if t == 0:
            A_f, B_f = C[0]["big"][:, 0:1024], C[0]["big"][:, 1024:2048]
            G.load(row2, A_f, rows(mods[4]), ada["rows"][4], s["merged_free"])
            m = G.load(row2, B_f, rows(mods[3]), ada["rows"][3], s["merged_free"])
            yield m
            TT["rows_f"] = V.stt(A_f, A_f, 1.0, BIAS[:, :], ALU.add, ALU.mult, m, rows_mark[0])
        h = yield from rms(t, C[0]["big"][:, 0:1024], C[0]["big"][:, 1024:2048], MERGED[t], out, TT["rows_f"])
        if t == 1:
            TT["gf"] = G.load(row2, BIAS[:, :], rows(mods[5]), ada["rows"][5], TT["rows_f"])
        yield from route(t, h)

    setup()
    plan.start(splitter())
    plan.start(setup_late())
    for t in range(NT):
        plan.start(tile(t))
    plan.run()

    over_marks = [q.mark() for q in (V, A, P, G)]
    RING_AFTER[:] = [over_marks] * NRING
    B_AFTER[:] = over_marks
    outs = experts()
    dumps = []
    out_slot = [[sem(f"out_done{t}"), 0] for t in range(NT)]
    for t in range(NT):
        dumps.append(S.load(out_slot[t], a["out"][128 * t:128 * t + 128], X[t][:, :], *outs))
    S.items.append((tuple(dumps), None, None, 0))

    with nc.Block() as block:
        @block.sync
        def _(e):
            S.replay(e)

        @block.tensor
        def _(e):
            P.replay(e)

        @block.vector
        def _(e):
            V.replay(e)

        @block.scalar
        def _(e):
            A.replay(e)

        @block.gpsimd
        def _(e):
            G.replay(e)

    top.close()


def chunked(w, groups, width, per):
    n = w.shape[0] // (128 * per)
    return w.reshape(n, per, 128, groups, width).transpose(3, 0, 2, 1, 4).reshape(groups * n, 128, per * width)


def wide(w):
    return w.reshape(w.shape[0] // 256, 2, 128, w.shape[1]).transpose(0, 2, 1, 3).reshape(w.shape[0] // 256, 128, -1)


def layout_up(w):
    k = w.shape[0]
    return chunked(w.reshape(k, 2, NG, 256).transpose(0, 2, 1, 3).reshape(k, -1), NG, 512, 4)


ORDER = (0, 2, 1, 3)


def layout_first(v):
    each = range(DEPTH)
    out = {}

    def stack(f):
        return np.ascontiguousarray(np.stack([f(i) for i in each]))

    out["x"] = v["x"].reshape(SEQ, D)
    out["pos"] = np.ascontiguousarray(v["positions"].reshape(NT, 128).T)
    for n in ("1", "2"):
        out["up" + n] = stack(lambda i: layout_up(v[f"ffn{n}_up"][i]))
        out["down" + n] = stack(lambda i: wide(v[f"ffn{n}_down"][i]))
    w = v["w_in"]
    out["w_in_a"] = stack(lambda i: chunked(w[i][:, 1792:2208], 1, 416, 4))
    out["w_in_b"] = stack(lambda i: np.concatenate([chunked(w[i][:, 512:1536], 2, 512, 4), chunked(w[i][:, 0:512], 1, 512, 4)]))
    out["w_in_c"] = stack(lambda i: chunked(w[i][:, 1536:1792], 1, 256, 8)[0])
    out["w_gate"] = stack(lambda i: np.concatenate(
        [chunked(w[i][:, 2208 + 1024 * n:3232 + 1024 * n], 2, 512, 4) for n in ORDER]))
    out["w_branch"] = stack(lambda i: np.concatenate([wide(v["w_branch"][i, n]) for n in ORDER]))
    out["w_out"] = stack(lambda i: wide(v["w_out"][i]))

    def ple(i):
        p = v["p"][i, 0].T.reshape(2, 128, SEQ).transpose(1, 0, 2).reshape(128, 2 * SEQ)
        w = v["w_ple"][i].reshape(2, 128, 2, 512).transpose(2, 1, 0, 3).reshape(2, 128, 1024)
        return np.stack([np.concatenate([p, w[h]], axis=1) for h in range(2)])

    out["w_ple"] = stack(ple)
    out["w_ple_gate"] = stack(lambda i: chunked(v["w_ple_gate"][i], 2, 512, 4))
    out["sgu_w"] = stack(lambda i: v["sgu_w"][i].transpose(2, 0, 1).reshape(128, 512))
    out["sgu_b"] = stack(lambda i: v["sgu_b"][i].T)

    def pool(i):
        w = np.zeros((2, 2, 64, 2, 64), np.float32)
        for g in range(4):
            w[g // 2, g % 2, :, g % 2, :] = v["pool_w"][i, g]
        return w.reshape(2, 128, 128).transpose(1, 0, 2).reshape(128, 256)

    out["pool_w"] = stack(pool)
    out["w_uq"] = stack(lambda i: v["mla_w_uq"][i].reshape(2, 128, 384).transpose(1, 0, 2).reshape(128, 768))
    out["w_ukv"] = v["mla_w_ukv"]
    for n in ("ln1_g", "ln1_b", "ln2_g", "ln2_b", "ln3_g", "ln3_b", "sgu_ln_g", "sgu_ln_b", "pool_scale", "mla_q_norm",
              "mla_kv_norm"):
        out[n] = v[n]
    return out


def layout_second(v):
    out = {}
    w = v["w_in_2"][0]
    cut = np.cumsum([0, 512, 512, 512, 512, 512, 512, 128, 128])
    xr, gr, dq, dk, dv, sq, sk, sv = (w[:, cut[i]:cut[i + 1]] for i in range(8))
    sq = sq.reshape(D, 2, 4, 64).transpose(0, 2, 1, 3).reshape(D, 512)
    out["w_in2"] = np.concatenate([chunked(x, 1, 512, 4) for x in (xr, gr, dq, dk, sq, dv)])
    out["w_in2_kv"] = chunked(np.concatenate([sk, sv], axis=1), 1, 256, 8)[0]
    out["w_gate2"] = chunked(w[:, 3328:], 6, 512, 4)
    wb = v["w_branch_2"][0]
    swa = wb[2].reshape(2, 4, 64, D).transpose(1, 0, 2, 3).reshape(512, D)
    out["w_branch2"] = np.concatenate([wide(x) for x in (wb[0], wb[1], swa)])
    out["w_out2"] = wide(v["w_out_2"][0])
    out["w_ada"] = v["w_ada_2"][0].reshape(4, 2, 128, 6, D).transpose(3, 0, 2, 1, 4).reshape(24, 128, 2 * D)
    out["b_ada"] = v["b_ada_2"].reshape(6, D)
    out["cond"] = v["c_2"].reshape(KD, 128).T
    out["norm_mix"], out["norm_ffn"] = v["norm_mix_2"][0], v["norm_ffn_2"][0]
    out["conv_w"] = v["conv_w_2"][0].reshape(4, 4, 128).transpose(2, 1, 0).reshape(128, 16)
    for n in ("conv_b", "lru_ba", "lru_bx", "lru_lambda"):
        out[n] = v[n + "_2"].reshape(4, 128).T
    for n, name in (("lru_a", "lru_wa_2"), ("lru_x", "lru_wx_2")):
        w = np.zeros((2, 64, 4, 2, 64), np.float32)
        for h in range(8):
            w[h % 2, :, h // 2, h % 2, :] = v[name][0, h]
        out[n] = w.reshape(128, 512)
    for n in ("diff_qnorm", "diff_knorm", "swa_qnorm", "swa_knorm", "diff_subln", "swa_sinks"):
        out[n] = v[n + "_2"][0]
    out["diff_lambda"] = v["diff_lambda_2"].reshape(256)
    rb = v["rel_bias_2"]
    out["rel_bias"] = np.concatenate([rb[:, 0:4], rb[:, 4:].reshape(32, 2, 4).transpose(0, 2, 1).reshape(32, 8)], axis=1)
    out["w_router"] = v["w_router_2"][0].reshape(KD, 128, N_EXP).transpose(1, 0, 2).reshape(128, KD * N_EXP)
    out["b_router"] = v["b_router_2"][0]
    out["w1"] = v["w1_2"][0].reshape(N_EXP, KD, 128, D, 2).transpose(0, 1, 2, 4, 3).reshape(N_EXP, KD, 128, 2 * D)
    out["b1"] = v["b1_2"][0].reshape(N_EXP, D, 2).transpose(0, 2, 1).reshape(N_EXP, 2 * D)
    out["w2"] = v["w2_2"][0].reshape(N_EXP, 4, 2, 128, D).transpose(0, 1, 3, 2, 4).reshape(N_EXP, 4, 128, 2 * D)
    out["b2"] = v["b2_2"][0]
    return out


def constants_second():
    out = {"ones": np.ones((128, 1), np.float32)}
    dist = 255 - np.arange(384)
    near = np.maximum(dist, 0)
    ratio = np.log(np.maximum(near, 1).astype(np.float32) / np.float32(16)) / np.float32(math.log(128 / 16))
    bucket = np.where(near < 16, near, np.minimum(16 + (ratio * np.float32(16)).astype(np.int32), 31))
    out["buckets"] = (np.arange(32)[:, None] == bucket[None, :]).astype(np.float32)
    future = np.where(dist < 0, MASKED, 0.0)[None, :].repeat(12, axis=0)
    future[4:, dist >= 128] = MASKED
    out["future"] = future.astype(np.float32)
    out["before"] = np.triu(np.ones((128, 128), np.float32), 1)
    out["iota"] = np.tile(np.arange(64, dtype=np.float32), (128, 2))
    return out


def constants_first():
    out = {"ident": np.eye(128, dtype=np.float32), "tril": np.triu(np.ones((128, 128), np.float32))}
    j, i = np.arange(128)[:, None], np.arange(128)[None, :]
    decay = np.zeros((128, 2, 2, 2, 128))
    for h in range(4):
        log_gamma = math.log1p(-2.0 ** (-5 - h))
        decay[:, h % 2, 0, h // 2] = np.exp(log_gamma * (128 + i - j))
        decay[:, h % 2, 1, h // 2] = np.where(j // 64 <= i // 64, np.exp(log_gamma * abs(i - j)), 0.0)
    out["decay"] = (decay * 0.125).astype(np.float32).reshape(128, 1024)
    band = np.zeros((128, 1088), np.float64)
    for g, window in enumerate((2, 4, 8, 16)):
        near = (j <= i) & (j > i - window)
        own = np.where(near, 1.0 / np.minimum(i + 1, window), 0.0) - (i == j)
        band[:, 128 * g:128 * g + 128] = own
        band[:, 512 + 128 * g:640 + 128 * g] = np.where(near, 1.0 / window, 0.0) - (i == j)
        t = np.arange(16)[None, :]
        band[:, 1024 + 16 * g:1040 + 16 * g] = np.where(j > 128 + t - window, 1.0 / window, 0.0)
    out["band"] = band.astype(np.float32)
    freq = [10000.0 ** (-(np.arange(0, n, 2, dtype=np.float32) / np.float32(n)).astype(np.float64)) for n in (64, 32)]
    out["freq"] = np.repeat(np.concatenate(freq).astype(np.float32)[None], 128, axis=0)
    return out


def kernel(**inputs):
    import concourse.bacc as _bacc
    from concourse.bass_utils import run_bass_kernel_spmd as _run

    arrays = {**layout_first(inputs), **layout_second(inputs), **constants_first(), **constants_second()}
    arrays = {name + "_dram": np.ascontiguousarray(x) for name, x in arrays.items()}
    nc = _bacc.Bacc("TRN2", target_bir_lowering=False, num_devices=1, dynamic_dma_scratch_size=4096)
    aps = {name[:-5]: nc.dram_tensor(name, x.shape, mybir.dt.from_np(x.dtype), kind="ExternalInput").ap()
           for name, x in arrays.items()}
    aps["out"] = nc.dram_tensor("out_dram", (SEQ, D), F32, kind="ExternalOutput").ap()
    program(nc, aps)
    r = _run(nc, [arrays], core_ids=[0])
    return r.results[0]["out_dram"].reshape(1, SEQ, D)
```

```python
import math
from contextlib import ExitStack

import numpy as np

import concourse.bass as bass
import concourse.mybir as mybir

ACT = mybir.ActivationFunctionType
ALU = mybir.AluOpType
AX = mybir.AxisListType
F32 = mybir.dt.float32
F32R = mybir.dt.float32r
I32 = mybir.dt.int32
U32 = mybir.dt.uint32

D = 1024
KD = D // 128
SEQ = 256
NT = SEQ // 128
DEPTH = 2
D_FF = 2816
NG = D_FF // 256
ALPHA = (2 * DEPTH) ** 0.25
LN_EPS = 1e-5
RMS_EPS = 1e-6
GN_EPS = 1e-5
MLA_SCALE = 96.0 ** -0.5
MASKED = -1e30
N_EXP = 32
N_EXTRA = 15
LIMIT = 7.0
SWIGLU = 1.702

N_SLOT = 10
AHEAD = 3
PENDING = 2
LEAD = 2
TARGET = 3
SPARE = 0
SLACK = 0.8
EARLY = 0.15


class Mark:

    def __init__(self, sem, count, time):
        self.sem, self.count, self.time = sem, count, time


class Later:

    def __init__(self, plan):
        self.plan, self.over, self.value, self.waiting = plan, False, None, []

    def set(self, value):
        self.over, self.value = True, value
        for work, result in self.waiting:
            self.plan.push(self.plan.now, work, result, value)


class Plan:

    def __init__(self):
        self.now, self.line, self.n, self.dma = 0.0, [], 0, 0.0

    def push(self, when, work, result, value=None):
        self.n += 1
        self.line.append((when, self.n, work, result, value))

    def later(self):
        return Later(self)

    def start(self, work, *marks):
        result = self.later()
        self.push(max([self.now] + [m.time - EARLY for m in marks if m]), work, result)
        return result

    def after(self, emit, *marks):
        def work():
            return emit()
            yield

        return self.start(work(), *marks)

    def run(self):
        while self.line:
            first = min(self.line, key=lambda x: x[:2])
            self.line.remove(first)
            when, _, work, result, value = first
            self.now = max(self.now, when)
            try:
                wait = work.send(value)
            except StopIteration as end:
                result.set(end.value)
                continue
            if isinstance(wait, Later):
                if wait.over:
                    self.push(self.now, work, result, wait.value)
                else:
                    wait.waiting.append((work, result))
            elif isinstance(wait, float):
                self.push(self.now + wait, work, result)
            else:
                marks = wait if isinstance(wait, list) else [wait]
                self.push(max([self.now] + [m.time - EARLY for m in marks if m]), work, result)


def size(ap):
    return math.prod(ap.shape[1:])


class Queue:

    LATER = 0.15

    def __init__(self, sem, plan):
        self.items, self.sem, self.count, self.plan = [], sem, 0, plan
        self.free = 0.0
        self.regs, self.outer = {}, []

    def read(self, name, src, low, high, *after):
        def emit(e):
            self.regs[name] = e.value_load(src, min_val=low, max_val=high)

        self.items.append((after, emit, None, 0))

    def only_if_more(self, name, than):
        self.items.append(("if", name, than, 0))

    def end(self):
        self.items.append(("end", None, None, 0))

    def enter(self, sem):
        self.outer.append((self.sem, self.count))
        self.sem, self.count = sem, 0

    def leave(self):
        self.sem, self.count = self.outer.pop()

    def mark(self):
        return Mark(self.sem, self.count, self.free + self.LATER)

    def put(self, emit, *after, busy=0.1):
        self.free = max([self.free, self.plan.now] + [m.time for m in after if m]) + busy
        self.count += 1
        self.items.append((after, emit, self.sem, 1))
        return self.mark()

    def replay(self, engine):
        reached, inside = {}, []
        for after, emit, sem, by in self.items:
            if after == "if":
                guard = engine.If(self.regs[emit] > sem)
                guard.__enter__()
                inside.append((guard, dict(reached)))
                continue
            if after == "end":
                guard, reached = inside.pop()
                guard.__exit__(None, None, None)
                continue
            for mark in after:
                if mark is not None and reached.get(id(mark.sem), 0) < mark.count:
                    engine.wait_ge(mark.sem, mark.count)
                    reached[id(mark.sem)] = mark.count
            if by:
                emit(engine).then_inc(sem, by)
            elif emit is not None:
                emit(engine)


class Vector(Queue):
    def takes(self, n):
        return 0.07 + n / 960

    def tt(self, out, a, b, op, *after):
        return self.put(lambda e: e.tensor_tensor(out, a, b, op=op), *after, busy=self.takes(size(out)))

    def ts(self, out, a, s1, s2, op0, op1, *after):
        busy = self.takes(size(out))
        if op1 is None:
            return self.put(lambda e: e.tensor_scalar(out, a, s1, None, op0=op0), *after, busy=busy)
        return self.put(lambda e: e.tensor_scalar(out, a, s1, s2, op0=op0, op1=op1), *after, busy=busy)

    def stt(self, out, a, s, b, op0, op1, *after):
        return self.put(lambda e: e.scalar_tensor_tensor(out, a, s, b, op0=op0, op1=op1), *after, busy=self.takes(size(out)))

    def copy(self, out, a, *after):
        return self.put(lambda e: e.tensor_copy(out, a), *after, busy=self.takes(size(out)))

    def memset(self, out, value, *after):
        return self.put(lambda e: e.memset(out, value), *after, busy=self.takes(size(out)))

    def reduce(self, out, a, op, *after):
        return self.put(lambda e: e.tensor_reduce(out, a, axis=AX.X, op=op), *after, busy=self.takes(size(a)))

    def recip(self, out, a, *after):
        return self.put(lambda e: e.reciprocal(out, a), *after, busy=0.07 + size(out) / 155)

    def stats(self, out, a, *after):
        return self.put(lambda e: e.bn_stats(out, a), *after, busy=self.takes(size(a)))

    def aggr(self, out, a, *after):
        return self.put(lambda e: e.bn_aggr(out, a), *after)


class Scalar(Queue):
    LATER = 0.2

    def copy(self, out, a, *after):
        return self.put(lambda e: e.copy(out, a), *after, busy=0.22 + size(out) / 1400)

    def act(self, out, a, func, *after, **more):
        return self.put(lambda e: e.activation(out, a, func, **more), *after, busy=0.22 + size(out) / 1400)


class Tensor(Queue):
    LATER = 0.25

    def mms(self, products, *after):
        def emit(e):
            for out, lhs, rhs, start, stop in products:
                last = e.matmul(out, lhs, rhs, start=start, stop=stop)
            return last

        return self.put(emit, *after, busy=sum(max(64, size(p[2])) * 4 / 2400 for p in products))

    def split(self, products, *after):
        def emit(e):
            for out, (xh, xl), (wh, wl), start, stop in products:
                e.matmul(out, xh, wh, start=start, stop=False)
                e.matmul(out, xh, wl, start=False, stop=False)
                last = e.matmul(out, xl, wh, start=False, stop=stop)
            return last

        return self.put(emit, *after, busy=sum(3 * (size(p[0]) + 6) / 2400 for p in products))

    def turn(self, pairs, ident, *after):
        def emit(e):
            for out, a in pairs:
                last = e.transpose(out, a, ident)
            return last

        return self.put(emit, *after, busy=0.065 * len(pairs))


class Loads(Queue):

    ISSUE = 0.06

    def load(self, slot, out, src, *after):
        slot[1] += 16
        self.items.append((after, lambda e: e.dma_start(out, src() if callable(src) else src), slot[0], 16))
        plan = self.plan
        self.free = max([self.free, plan.now] + [m.time for m in after if m]) + self.ISSUE
        plan.dma = max(plan.dma, self.free + 1.3) + out.shape[0] * size(out) * 4 / 360e3
        return Mark(slot[0], slot[1], plan.dma + 0.5)


class Pool(Vector, Loads):
    ISSUE = 1.0

    def takes(self, n):
        return 0.1 + n / 440


def rows(ap, n=128):
    return ap.unsqueeze(0).to_broadcast([n] + list(ap.shape))


def program(nc, a):
    top = ExitStack()

    def sem(name):
        return top.enter_context(nc.semaphore(name))

    def sb(name, cols, dt=F32, ctx=top):
        return ctx.enter_context(nc.sbuf_tensor("s_" + name, [128, cols], dt))

    bank = [top.enter_context(nc.psum_tensor(f"bank{i}", [128, 512], F32)) for i in range(8)]
    ACC = [[bank[0], bank[1]], [bank[2], bank[3]]]

    plan = Plan()
    V, A, P = Vector(sem("dve_a"), plan), Scalar(sem("act_a"), plan), Tensor(sem("pe_a"), plan)
    G, S = Pool(sem("pool_a"), plan), Loads(None, plan)

    ident = sb("ident", 128)
    X = [sb(f"x{t}", D) for t in range(NT)]
    MERGED = [sb(f"merged{t}", D) for t in range(NT)]
    GAIN, BIAS = sb("gain_row", D), sb("bias_row", D)
    ST = [sb(f"st{t}", 176) for t in range(NT)]
    RT = [sb(f"route{t}", 376) for t in range(NT)]
    RI = [top.enter_context(nc.sbuf_tensor(f"s_best{t}", [128, 8], U32)) for t in range(NT)]
    ones, cond_t, iota = sb("ones", 1), sb("cond", KD), sb("iota", 128)
    dense = ExitStack()

    def slots(n, name, ctx):
        loads = ExitStack()
        raw = [sb(f"{name}_raw{i}", 2048, ctx=loads) for i in range(n)]
        loads.close()
        return [(raw[i], sb(f"{name}_part{i}", 2048, F32R, ctx)) for i in range(n)]

    SLOTS = [(pair, 2) for pair in slots(N_SLOT, "w", dense)]
    XTH = [sb(f"xth{t}", D, F32R, dense) for t in range(NT)]
    XTL = [sb(f"xtl{t}", D, F32R, dense) for t in range(NT)]
    YTH = [sb(f"yth{t}", 512, F32R, dense) for t in range(NT)]
    YTL = [sb(f"ytl{t}", 512, F32R, dense) for t in range(NT)]
    GATE = [sb(f"gate{t}", D, ctx=dense) for t in range(NT)]

    spread = ExitStack()
    for t in range(NT):
        SLOTS += [(pair, t) for pair in slots(3, f"v{t}", spread)]
        sb(f"unused{t}", 384, ctx=spread)
    spread.close()
    first = ExitStack()
    sizes = dict(pr=1024, a2=1024, a3=512, a4=512, a5=256, kcat=384, q=384, ct=384, plt=256,
                 rqt=256, z=256, rv=256, rkt=256, mkt=512, mv=256)
    B = [{k: sb(f"{k}{t}", n, ctx=first) for k, n in sizes.items()} for t in range(NT)]
    RT1, RT2 = sb("rope1", 512, ctx=first), sb("rope2", 512, ctx=first)
    sgu_w, sgu_b = sb("sgu_w_t", 512, ctx=first), sb("sgu_b_t", 4, ctx=first)
    sgu_g, sgu_bb = sb("sgu_gain", 256, ctx=first), sb("sgu_bias", 256, ctx=first)
    pool_w, pool_s = sb("pool_w_t", 256, ctx=first), sb("pool_s", 256, ctx=first)
    q_gain, kv_gain = sb("q_gain", 256, ctx=first), sb("kv_gain", 128, ctx=first)
    w_uq, w_ukv = sb("w_uq_t", 768, ctx=first), sb("w_ukv_t", 512, ctx=first)
    decay = sb("decay", 1024, ctx=first)
    band = sb("band", 512 + 512 + 64, ctx=first)
    tril = sb("tril", 128, ctx=first)
    freq = sb("freq", 48, ctx=first)
    pos_i = first.enter_context(nc.sbuf_tensor("pos_i", [128, NT], I32))
    pos_f = sb("pos_f", NT, ctx=first)
    cos, sin = (sb(n, NT * 48, ctx=first) for n in ("cos_t", "sin_t"))
    ang, turns = RT1[:, :NT * 48], RT2[:, :NT * 48]

    first.close()
    second = ExitStack()
    sizes2 = dict(big=2048, aa=512, sq=512, dk=512, dq=512, dv=512, kt=512, sk=128, sv=128, skt=128, xrt=528, hl=8, rest=488)
    orders = [list(sizes2), ["xrt", "hl", "sk", "sv", "skt", "dq", "rest", "sq", "dk", "dv", "kt", "aa", "big"]]
    C = [{k: sb(f"{k}_{t}", sizes2[k], ctx=second) for k in order} for t, order in enumerate(orders)]
    bm = sb("bm", 12 * 256, ctx=second)
    gains = [sb(f"gain{i}", 64, ctx=second) for i in range(4)]
    subln, sinks, lamv, lam = (sb(n, w, ctx=second) for n, w in (("subln", 128), ("sinks", 8), ("lamv", 256), ("lam", 4)))
    conv_w, conv_b, sp, sp4, lt = (sb(n, w, ctx=second) for n, w in
                                   (("conv_w2", 16), ("conv_b2", 4), ("sp", 4), ("sp4", 8), ("lt", 12)))
    lru_a, lru_x, ba, bx = (sb(n, w, ctx=second) for n, w in (("lru_a2", 512), ("lru_x2", 512), ("ba", 4), ("bx", 4)))
    w_router, b_router = sb("w_router2", 256, ctx=second), sb("b_router2", N_EXP, ctx=second)
    rel, buckets, future = (sb(n, w, ctx=second) for n, w in (("rel", 12), ("buckets2", 384), ("future2", 384)))
    before = sb("before2", 128, ctx=second)
    second.close()
    dense.close()

    moe = ExitStack()
    NRING = N_SLOT + 8
    RING = [sb(f"ring{i}", 2048, ctx=moe) for i in range(NRING)]
    SEL = [sb(f"sel{i}", 128, ctx=moe) for i in range(2)]
    SELW = sb("selw", 256, ctx=moe)
    XE = [sb(f"xe{i}", 512, ctx=moe) for i in range(2)]
    SELT = [sb(f"selt{i}", 256, ctx=moe) for i in range(2)]
    GT, EX = sb("gt", 256, ctx=moe), sb("extra", 256, ctx=moe)
    EXI = moe.enter_context(nc.sbuf_tensor("s_extra_n", [128, 1 + N_EXTRA], I32))
    GLU = sb("glu", 512, ctx=moe)
    sb("unused", 752, ctx=moe)
    HALF = sb("half_row", 512, ctx=moe)
    sb("unused2", 512, ctx=moe)
    b1s, b2s = sb("b1s", 2048, ctx=moe), sb("b2s", 1024, ctx=moe)
    TH, LIN, ACTT = (sb(n, 512, ctx=moe) for n in ("th", "lin", "actt"))
    Y = [sb(f"y{i}", 512, ctx=moe) for i in range(2)]
    Y.append(b2s[:, 0:512])
    SELT.append(b2s[:, 512:768])
    moe.close()
    ring_slot = [[sem(f"ring_in{i}"), 0] for i in range(NRING)]
    b_slot = [sem("b_in"), 0]
    small2 = [sem("small2_in"), 0]
    toeplitz = nc.dram_tensor("toeplitz", [128, 12, 384], F32, kind="Internal").ap()


    spare = [(bank[i], None) for i in range(4, 8)]

    def take():
        while not spare:
            yield 0.1
        return spare.pop(0)

    def give(b, mark):
        spare.append((b, mark))

    FOREVER = 1 << 30
    chunks, stream, extra, at_stream = [], [], {}, {}
    slot_sem = [[sem(f"w_in{i}"), 0] for i in range(len(SLOTS))]
    unused = [(i, []) for i in range(len(SLOTS)) if SLOTS[i][1] == 2]
    away = [i for i in range(len(SLOTS)) if SLOTS[i][1] < 2]
    limit = [0, 0, FOREVER]
    loaded, lo_done, raw_of, hi_of = {}, {}, {}, {}
    at, n_loaded, n_split = [0, 0], [0], [0]
    wants = [None, None]
    urgent = [0]

    def urgent_until(*marks):
        def over():
            urgent[0] -= 1

        urgent[0] += 1
        plan.after(over, *marks)


    def chunk_add(*srcs):
        for src in srcs:
            at_stream[len(chunks)] = len(stream)
            stream.append((src, len(chunks)))
            chunks.append(src)

    def chunk_extra(src):
        extra.setdefault(len(chunks), []).append(len(stream))
        stream.append((src, len(chunks)))

    def open_to(i):
        return [x for x in unused if i < limit[SLOTS[x[0]][1]]]

    def slot_take(i):
        x = open_to(i)[0]
        unused.remove(x)
        return x

    def slot_give(i, mark):
        unused.append((i, [mark]))

    def region_open(region, until, *marks):
        limit[region] = until
        for i in list(away):
            if SLOTS[i][1] == region:
                away.remove(i)
                unused.append((i, list(marks)))

    def region_end(region):
        while True:
            for x in list(unused):
                if SLOTS[x[0]][1] == region:
                    unused.remove(x)
                    away.append(x[0])
            if sum(SLOTS[i][1] == region for i in away) == sum(r == region for _, r in SLOTS):
                return
            yield 0.3

    def load_ahead():
        if n_loaded[0] == len(stream):
            while len(unused) > len(stream) - n_split[0]:
                n, marks = unused.pop(0)
                ring_fill(n, *marks)
        while n_loaded[0] < len(stream):
            j = n_loaded[0]
            src, i = stream[j]
            pending = j - n_split[0]
            if pending >= PENDING or len(open_to(i)) < (2 if pending else 1):
                return
            n, marks = slot_take(i)
            raw_of[j] = n
            loaded[j] = [S.load(slot_sem[n], SLOTS[n][0][0][:, :src.shape[-1]], src, *marks)] * 2
            n_loaded[0] += 1

    def load_first():
        n, _ = slot_take(0)
        raw_of[0], n_loaded[0] = n, 1
        loaded[0], x_in = [], []
        for h in range(2):
            x_in.append(S.load([sem(f"x_in0{h}"), 0], X[0][:, 512 * h:512 * h + 512], a["x"][0:128, 512 * h:512 * h + 512]))
            c = slice(1024 * h, 1024 * h + 1024)
            loaded[0].append(S.load([sem(f"w_first{h}"), 0], SLOTS[n][0][0][:, c], chunks[0][:, c]))
        state[0]["x_in"] = x_in

    def splitter():
        for i in range(len(chunks)):
            for j in extra.get(i, []):
                while j >= n_loaded[0]:
                    yield 0.2
                yield loaded[j][0]
                slot_give(raw_of[j], (yield from ada_chunk(j)))
                n_split[0] = j + 1
                load_ahead()
            j = at_stream[i]
            while j >= n_loaded[0] or i > at[0] + AHEAD or not open_to(i):
                yield 0.2
                load_ahead()
            hi_of[i], marks = slot_take(i)
            w = chunks[i].shape[-1] // 2
            for part in range(2):
                c = slice(part * w, (part + 1) * w)
                raw, lo = (x[:, c] for x in SLOTS[raw_of[j]][0])
                hi = SLOTS[hi_of[i]][0][1][:, c]
                yield [loaded[j][part], *marks]
                m = A.copy(hi, raw, loaded[j][part], *marks)
                yield m
                while urgent[0] and i > at[0] + SPARE:
                    yield 0.1
                lo_done[i, part] = V.tt(lo, raw, hi.bitcast(F32), ALU.subtract, m)
            n_split[0] = j + 1
            load_ahead()

    def may_lead(i):
        return n_split[0] == len(stream) or i - at[1] < (sum(i < limit[r] for _, r in SLOTS) - PENDING) // 2 - 1

    def first():
        return int(at[0] - at[1] >= TARGET)

    def chunk_use(t, products, *after):
        i = at[t]
        marks = [m for m in after if m]

        def can(part):
            if (i, part) not in lo_done or (i >= at[0] if t else part == 0 and not may_lead(i)):
                return False
            return max([lo_done[i, part].time] + [m.time for m in marks]) <= plan.now + SLACK

        def turn(part):
            wants[t] = lambda: can(part)
            while P.free > plan.now + SLACK or not can(part) or first() != t and wants[1 - t] and wants[1 - t]():
                yield 0.1
            wants[t] = None

        halves, done = None, []
        for part in range(2):
            yield from turn(part)
            if halves is None:
                j = at_stream[i]
                halves = products(SLOTS[hi_of[i]][0][1], SLOTS[raw_of[j]][0][1])
            if halves[part]:
                done.append(P.split(halves[part], lo_done[i, part], *after))
        at[t] += 1
        if t == 1:
            slot_give(raw_of[j], done[-1])
            slot_give(hi_of[i], done[-1])
            load_ahead()
        return done

    ring_order, ring_in = [], {}

    def ring_load(n, *marks):
        e, k = divmod(n, 12)
        i = ring_order[n % NRING]
        ring_in[n] = S.load(ring_slot[i], RING[i][:, :], a["w1"][e, k] if k < 8 else a["w2"][e, k - 8], *marks)

    def ring_fill(i, *marks):
        ring_order.append(i)
        ring_load(len(ring_order) - 1, *marks)

    def rsqrt(x, y, u, mark, between=()):
        between = list(between)

        def other():
            if between:
                between.pop(0)()

        factor = -2.0 ** (-13 / 27)
        m = V.ts(y.bitcast(I32), x.bitcast(I32), -0.5, float(0x5EFFC000 - 2 ** 31), ALU.mult, ALU.add, mark)
        other()
        yield m
        for _ in range(3):
            if size(x) == 1:
                m = V.stt(u, y, x, y, ALU.mult, ALU.mult, m)
            else:
                m = V.tt(u, y, x, ALU.mult, m)
                yield m
                m = V.tt(u, u, y, ALU.mult, m)
            other()
            yield m
            m = V.stt(y, u, 3 * factor ** 2, y, ALU.subtract, ALU.mult, m)
            factor = -2 * factor ** 3
            yield m
        return m

    def split_into(th, tl, src, give_back, m, *free):
        h = A.copy(th, src, m, *free)
        yield h
        l = V.tt(tl, src, th.bitcast(F32), ALU.subtract, h)
        give_back(l)
        return l

    def xt_from(t, src, ready, xt_free):
        done = []
        for j in range(2):
            b, free = yield from take()
            yield [ready[j], free]
            m = P.turn([(b[:, 128 * k:128 * k + 128], src[:, 512 * j + 128 * k:512 * j + 128 * k + 128]) for k in range(4)],
                       ident[:, :], ready[j], free, CONST["ident"])
            c = slice(512 * j, 512 * j + 512)
            done.append(plan.start(split_into(XTH[t][:, c], XTL[t][:, c], b[:, :], lambda l, b=b: give(b, l), m, xt_free), m))
        return done, m

    def xk(t, k):
        return XTH[t][:, 128 * k:128 * k + 128], XTL[t][:, 128 * k:128 * k + 128]

    def group_products(t, b, w, part, nk=8):
        def products(hi, lo):
            out = []
            for j in range(nk):
                k = part * nk + j
                c = slice(j * w, j * w + w)
                out.append((b[:, :w], xk(t, k), (hi[:, c], lo[:, c]), k == 0, k == KD - 1))
            return out[:nk // 2], out[nk // 2:]
        return products

    def wide_products(lhs, outs, first_k, last_k, k0):
        def products(hi, lo):
            out = []
            for h in range(2):
                for j in range(2):
                    k, c = k0 + j, slice(1024 * h + 512 * j, 1024 * h + 512 * j + 512)
                    out.append((outs[h][:, :], lhs(k), (hi[:, c], lo[:, c]), k == first_k, k == last_k))
            return out[:2], out[2:]
        return products

    def layer_norm(t, scale, pe_marks, x_mark, rows_mark):
        x, st = X[t], ST[t]
        halves = [x[:, :512], x[:, 512:]]
        y, m = [], []
        for h in range(2):
            yield [pe_marks[h], x_mark]
            urgent[0] += 1 - h
            y.append(V.stt(halves[h], ACC[t][h][:, :], scale, halves[h], ALU.mult, ALU.add, pe_marks[h], x_mark))
            m.append(V.stats(st[:, 6 * h:6 * h + 6], halves[h], y[h]))
        yield m
        m = V.aggr(st[:, 12:14], st[:, 0:12], *m)
        yield m
        e = V.ts(st[:, 14:15], st[:, 13:14], LN_EPS, None, ALU.add, None, m)
        z = [None, None]

        def centre(h):
            def f():
                c = slice(512 * h, 512 * h + 512)
                z[h] = V.stt(halves[h], halves[h], st[:, 12:13], GAIN[:, c], ALU.subtract, ALU.mult, m, rows_mark)
            return f

        yield e
        r = yield from rsqrt(st[:, 14:15], st[:, 15:16], st[:, 16:17], e, [centre(0), centre(1)])
        out = []
        for h in range(2):
            c = slice(512 * h, 512 * h + 512)
            out.append(V.stt(halves[h], halves[h], st[:, 15:16], BIAS[:, c], ALU.mult, ALU.add, r, z[h]))
        urgent_until(out[1])
        urgent[0] -= 1
        return out, y[1]

    def scale_x(t, *after):
        return G.ts(X[t][:, :], X[t][:, :], ALPHA, 0.0, ALU.mult, ALU.add, *after)

    rows_slot = [sem("rows_in"), 0]
    rows_users = []

    def load_rows(g, b, *after):
        S.load(rows_slot, GAIN[:, :], rows(g), *rows_users, *after)
        return S.load(rows_slot, BIAS[:, :], rows(b), *rows_users, *after)

    CONST = {}

    state = [dict(xt_free=None, acc_free=None, b1_free=None, merged_free=None, gate_free=None, yt_free=[None, None],
                  act_free=[None, None], sel_known=plan.later()) for _ in range(NT)]

    def ffn(t, xt, first=()):
        s = state[t]
        acts, sil = [MERGED[t][:, 0:256], MERGED[t][:, 256:512]], MERGED[t][:, 512:768]
        x = [None, None]

        def activate(b, m, slot):
            silu = A.act(sil, b[:, 0:256], ACT.Silu, m, s["sil_free"])
            yield silu
            s["sil_free"] = V.tt(acts[slot], sil, b[:, 256:512], ALU.mult, silu, s["act_free"][slot])
            return s["sil_free"]

        pend = None
        for g in range(NG + 1):
            if g < NG:
                b, free = yield from take()
                x[0] = yield xt[0]
                yield from chunk_use(t, group_products(t, b, 512, 0, 4), free, x[0])
            if pend:
                pb, ready, slot, pg = pend
                urgent[0] += g == NG
                ready = yield ready
                yield ready
                m = P.turn([(pb[:, 128 * k:128 * k + 128], acts[slot][:, 128 * k:128 * k + 128]) for k in range(2)],
                           ident[:, :], ready)
                s["act_free"][slot] = m
                c = slice(256 * slot, 256 * slot + 256)
                yt = plan.start(split_into(YTH[t][:, c], YTL[t][:, c], pb[:, :256], lambda l, pb=pb: give(pb, l), m,
                                           s["yt_free"][slot]), m)
            if g < NG:
                x[1] = yield xt[1]
                _, m = yield from chunk_use(t, group_products(t, b, 512, 1, 4), x[1])
                if g == 0:
                    for f in first:
                        yield f
                    s["act_free"], s["sil_free"] = [s["merged_free"]] * 2, s["merged_free"]
                if g == NG - 1:
                    s["xt_free"] = m
                now = (b, plan.start(activate(b, m, g % 2), m), g % 2, g)
            if pend:
                def lhs(k, slot=slot):
                    c = slice(256 * slot + 128 * (k % 2), 256 * slot + 128 * (k % 2) + 128)
                    return YTH[t][:, c], YTL[t][:, c]

                y = yield yt
                urgent[0] -= g == NG
                down = yield from chunk_use(t, wide_products(lhs, ACC[t], 0, 2 * NG - 1, 2 * pg), y,
                                            s["acc_free"] if pg == 0 else None, s["b1_free"] if pg == 0 else None)
                s["yt_free"][slot] = down[1]
            pend = now if g < NG else None
        s["down"] = down

    def rope(src, dst, groups, half, c, s, done, *after):
        n = groups * 2 * half
        t1 = RT1[:, :n].rearrange("p (g w h) -> p g w h", g=groups, w=2)
        t2 = RT2[:, :n].rearrange("p (g w h) -> p g w h", g=groups, w=2)
        cb = c.unsqueeze(1).to_broadcast([128, groups, half])
        sb_ = s.unsqueeze(1).to_broadcast([128, groups, half])
        m = []
        for w in range(2):
            m.append(G.tt(t1[:, :, w], src[:, :, w], cb, ALU.mult, *after, *done))
            m.append(G.tt(t2[:, :, w], src[:, :, 1 - w], sb_, ALU.mult, *after, *done))
        lo = G.tt(dst[:, :, 0], t1[:, :, 0], t2[:, :, 0], ALU.subtract, *m)
        hi = G.tt(dst[:, :, 1], t1[:, :, 1], t2[:, :, 1], ALU.add, *m)
        return [lo, hi]

    rope_done = [[]]

    def branches(t, layer, ev, out, yt_used, prev_ev):
        buf, st, s = B[t], ST[t], state[t]
        b0, b1 = ACC[t]
        bf = [s["acc_free"], s["acc_free"]]
        prev = B[0]
        small = CONST["small"]
        cq = buf["a2"][:, 0:416]
        cn = buf["a2"][:, 416:800]
        c_ret, s_ret = cos[:, 48 * t:48 * t + 32], sin[:, 48 * t:48 * t + 32]
        c_mla, s_mla = cos[:, 48 * t + 32:48 * t + 48], sin[:, 48 * t + 32:48 * t + 48]

        def turned(src, ready, n):
            yt_free = (yield yt_used[n - 2]) if n > 1 else s["yt_free"][n % 2]
            b, f = yield from take()
            yield [f, *ready]
            c = slice(256 * (n % 2), 256 * (n % 2) + 256)
            m = P.turn([(b[:, 128 * k:128 * k + 128], src[:, 128 * k:128 * k + 128]) for k in range(2)], ident[:, :],
                       *ready, f)
            yield m
            l = yield from split_into(YTH[t][:, c], YTL[t][:, c], b[:, 0:256], lambda l: give(b, l), m, yt_free)
            out[n].set(l)

        ssq, cq_in = yield ev["cq"]
        yield ssq
        e0 = V.ts(st[:, 22:23], st[:, 20:21], 1.0 / 256, RMS_EPS, ALU.mult, ALU.add, ssq)
        e1 = V.ts(st[:, 23:24], st[:, 21:22], 1.0 / 128, RMS_EPS, ALU.mult, ALU.add, ssq, e0)
        r = yield from rsqrt(st[:, 22:24], st[:, 24:26], st[:, 26:28], e1)
        n0 = V.stt(cn[:, 0:256], cq[:, 0:256], st[:, 24:25], q_gain[:, :], ALU.mult, ALU.mult, r, cq_in, small)
        n1 = V.stt(cn[:, 256:384], cq[:, 256:384], st[:, 25:26], kv_gain[:, :], ALU.mult, ALU.mult, r)
        kpe = st[:, 32:64].rearrange("p (g w h) -> p g w h", g=1, w=2)
        rope_done[0] = rope(cq[:, 384:416].rearrange("p (g w h) -> p g w h", g=1, w=2), kpe, 1, 16, c_mla, s_mla,
                            rope_done[0], cq_in, s.get("kpe_free"), CONST["rope"])
        kpe_done = rope_done[0]
        yield [n0, n1, bf[0]]
        m = P.turn([(b0[:, 128 * k:128 * k + 128], cn[:, 128 * k:128 * k + 128]) for k in range(3)], ident[:, :],
                   n0, n1, bf[0])
        yield m
        ct = A.copy(buf["ct"][:, :], b0[:, 0:384], m)
        bf[0] = ct
        rqk = buf["pr"][:, 0:512].rearrange("p (g w h) -> p g w h", g=8, w=2)
        roped = buf["a3"][:, :].rearrange("p (g w h) -> p g w h", g=8, w=2)
        qk_in = yield ev["qk"]
        yield [qk_in, ct]
        rope_done[0] = rope(rqk, roped, 8, 32, c_ret, s_ret, rope_done[0], qk_in)
        ret_roped = rope_done[0]
        m = P.mms([(b1[:, 0:384], buf["ct"][:, 128 * k:128 * k + 128], w_uq[:, 384 * k:384 * k + 384], k == 0, k == 1)
                   for k in range(2)], ct, bf[1], small)
        mk = P.mms([(b0[:, :], buf["ct"][:, 256:384], w_ukv[:, :], True, True)], ct, bf[0])
        yield m
        qc = A.copy(buf["q"][:, :], b1[:, 0:384], m, s.get("q_free"))
        bf[1] = qc
        yield mk
        kv4 = b0[:, :].rearrange("p (h w) -> p h w", h=4)
        kc4 = buf["kcat"][:, :].rearrange("p (h w) -> p h w", h=4)
        k_nope = A.copy(kc4[:, :, 0:64], kv4[:, :, 0:64], mk)
        mv = A.copy(buf["mv"][:, :].rearrange("p (h w) -> p h w", h=4), kv4[:, :, 64:128], mk)
        bf[0] = mv
        q4 = buf["q"][:, :].rearrange("p (h w) -> p h w", h=4)[:, :, 64:96].rearrange("p h (w x) -> p h w x", w=2)
        rope_done[0] = rope(q4, q4, 4, 16, c_mla, s_mla, rope_done[0], qc)
        q_roped = rope_done[0]
        k_pe = G.copy(kc4[:, :, 64:96], st[:, 32:64].unsqueeze(1).to_broadcast([128, 4, 32]), *kpe_done, k_nope)
        s["kpe_free"] = k_pe
        yield [*ret_roped, bf[1]]
        m = P.turn([(b1[:, 128 * k:128 * k + 128], buf["a3"][:, 128 * k:128 * k + 128]) for k in range(4)], ident[:, :],
                   *ret_roped, bf[1])
        yield m
        rq = A.copy(buf["rqt"][:, :], b1[:, 0:256], m)
        rk = A.copy(buf["rkt"][:, :], b1[:, 256:512], m, s.get("rkt_free"))
        bf[1] = rk
        ev["rkt"].set(rk)
        ev["mv"].set(mv)
        rk0, mv0 = (yield prev_ev["rkt"]), (yield prev_ev["mv"])
        yield [q_roped[1], k_pe, bf[0]]
        m = P.turn([(b0[0:96, 128 * h:128 * h + 128], buf["q"][:, 96 * h:96 * h + 96]) for h in range(4)], ident[:, :],
                   *q_roped, bf[0])
        s["q_free"] = m
        yield m
        qt = A.copy(buf["a3"][0:96, :], b0[0:96, :], m)
        bf[0] = qt
        yield [rk, rk0, qt]
        sb_ = [b0, b1]
        m = []
        for par in range(2):
            ps = []
            for kt in range(t + 1):
                for h2 in range(2):
                    lo = 64 * par
                    c = (kt * 2 + h2) * 128
                    ps.append((sb_[par][:, c:c + 128], B[kt]["rkt"][lo:lo + 64, 128 * h2:128 * h2 + 128],
                               buf["rqt"][lo:lo + 64, 128 * h2:128 * h2 + 128], True, True))
            m.append(P.mms(ps, rq, rk, rk0, bf[par]))
        yield m
        w = 256 * (t + 1)
        d4 = decay[:, :].rearrange("p (a b) -> p a b", a=2)
        rs4 = buf["a2"][:, :].rearrange("p (a b) -> p a b", a=2)
        rs = []
        for par in range(2):
            rs.append(V.tt(rs4[:, par, 0:w], sb_[par][:, 0:w], d4[:, par, 512 - w:512], ALU.mult, m[par], CONST["all"],
                           *kpe_done))
            bf[par] = rs[par]
        yield [bf[1], k_nope, k_pe]
        m = P.turn([(b1[0:96, 128 * h:128 * h + 128], buf["kcat"][:, 96 * h:96 * h + 96]) for h in range(4)], ident[:, :],
                   k_nope, k_pe, bf[1])
        yield m
        kt_ = A.copy(buf["mkt"][0:96, :], b1[0:96, :], m, s.get("mkt_free"))
        bf[1] = kt_
        ev["mkt"].set(kt_)
        uv_in = yield ev["uv"]
        yield uv_in
        gv = buf["a4"][:, 256:512]
        s0 = V.stats(st[:, 0:6], gv, uv_in)
        yield s0
        s0 = V.aggr(st[:, 12:14], st[:, 0:6], s0)
        yield s0
        e = V.ts(st[:, 14:15], st[:, 13:14], LN_EPS, None, ALU.add, None, s0)
        zz = []
        r = yield from rsqrt(st[:, 14:15], st[:, 15:16], st[:, 16:17], e,
                             [lambda: zz.append(V.stt(gv, gv, st[:, 12:13], sgu_g[:, :], ALU.subtract, ALU.mult, s0, small))])
        gvn = V.stt(gv, gv, st[:, 15:16], sgu_bb[:, :], ALU.mult, ALU.add, r, zz[0])
        z_in, vg_in, z0, vg0 = (yield ev["z"]), (yield ev["vg"]), (yield prev_ev["z"]), (yield prev_ev["vg"])
        yield [z_in, bf[0]]
        ps = []
        for g in range(4):
            o = b0[64 * (g % 2):64 * (g % 2) + 64, 128 * (g // 2):128 * (g // 2) + 128]
            ps.append((o, buf["z"][:, 64 * g:64 * g + 64], band[:, 512 * t + 128 * g:512 * t + 128 * g + 128], True, t == 0))
            if t:
                ps.append((o[:, 0:16], prev["z"][96:128, 64 * g:64 * g + 64],
                           band[96:128, 1024 + 16 * g:1024 + 16 * g + 16], False, True))
        mp = P.mms(ps, z_in, z0, bf[0], CONST["all"])
        yield mp
        plt = A.copy(buf["plt"][:, :], b0[:, 0:256], mp)
        bf[0] = plt
        yield [*rs, gvn, bf[1], vg_in]
        ps = []
        for h in range(4):
            for kt in range(t + 1):
                c = (kt * 2 + h // 2) * 128
                ps.append((b1[:, 64 * h:64 * h + 64], rs4[:, h % 2, c:c + 128], B[kt]["rv"][:, 64 * h:64 * h + 64],
                           kt == 0, kt == t))
        for g in range(4):
            ps.append((b1[:, 256 + 64 * g:320 + 64 * g], sgu_w[:, 128 * g:128 * g + 128], gv[:, 64 * g:64 * g + 64],
                       True, True))
        mr = P.mms(ps, *rs, gvn, bf[1], vg_in, vg0, CONST["tril"])
        s["rkt_free"] = mr
        yield [mr]
        us = []
        for g in range(4):
            c = slice(64 * g, 64 * g + 64)
            us.append(V.stt(buf["a4"][:, c], b1[:, 256 + 64 * g:320 + 64 * g], sgu_b[:, g:g + 1], buf["a4"][:, c],
                            ALU.add, ALU.mult, mr, uv_in))
        plan.start(turned(buf["a4"], us, 0), *us)
        ss = [V.stats(st[:, 6 * h:6 * h + 6], b1[:, 64 * h:64 * h + 64], mr, r) for h in range(4)]
        yield ss
        mv_ = [V.aggr(st[:, 24 + 2 * h:26 + 2 * h], st[:, 6 * h:6 * h + 6], *ss, n1) for h in range(4)]
        yield mv_
        var = st[:, 24:32].rearrange("p (h w) -> p h w", w=2)
        e = V.ts(st[:, 0:4], var[:, :, 1], GN_EPS, None, ALU.add, None, *mv_)
        yield e
        r = yield from rsqrt(st[:, 0:4], st[:, 4:8], st[:, 8:12], e)
        ry = []
        for h in range(4):
            ry.append(V.ts(buf["q"][:, 64 * h:64 * h + 64], b1[:, 64 * h:64 * h + 64], var[:, h, 0:1], st[:, 4 + h:5 + h],
                           ALU.subtract, ALU.mult, r, s["q_free"]))
        bf[1] = ry[3]
        g_in = yield ev["g"]
        yield ry
        yr = V.tt(buf["a5"][:, :], buf["a5"][:, :], buf["q"][:, 0:256], ALU.mult, *ry, g_in)
        s["q_free"] = yr
        plan.start(turned(buf["a5"], [yr], 2), yr)
        yield [plt, bf[0]]
        m = P.mms([(b0[:, 128 * g:128 * g + 128], buf["plt"][:, 128 * g:128 * g + 128], pool_w[:, 128 * g:128 * g + 128],
                    True, True) for g in range(2)], plt, bf[0], small)
        yield m
        yp = V.tt(buf["plt"][:, :], b0[:, 0:256], pool_s[:, :], ALU.mult, m)
        bf[0] = yp
        plan.start(turned(buf["plt"], [yp], 1), yp)
        kt0 = yield prev_ev["mkt"]
        yield [qt, kt_, kt0, *bf]
        n_k = 128 * (t + 1)
        sc = [b0[:, :].rearrange("p (h k) -> p h k", k=n_k), b1[:, :].rearrange("p (h k) -> p h k", k=n_k)]
        per = 4 if t == 0 else 2
        m = []
        for j in range(4 // per):
            ps = []
            for h in range(per):
                for kt in range(t + 1):
                    hh = per * j + h
                    ps.append((sc[j][:, h, 128 * kt:128 * kt + 128], buf["a3"][0:96, 128 * hh:128 * hh + 128],
                               B[kt]["mkt"][0:96, 128 * hh:128 * hh + 128], True, True))
            m.append(P.mms(ps, qt, kt_, kt0, bf[j]))
        s["mkt_free"] = m[-1]
        mx = st[:, 0:4]
        pm = buf["pr"][:, 0:4 * n_k].rearrange("p (h k) -> p h k", k=n_k)
        exps = []
        for j in range(4 // per):
            yield m[j]
            cut = V.memset(sc[j][0:64, 0:per, n_k - 64:n_k], MASKED, m[j])
            top_ = V.reduce(mx[:, per * j:per * j + per], sc[j][:, 0:per, :], ALU.max, cut, *ry)
            yield top_
            neg = V.ts(st[:, 4 + per * j:4 + per * j + per], mx[:, per * j:per * j + per], -MLA_SCALE, None, ALU.mult, None, top_)
            yield neg
            for h in range(per):
                hh = per * j + h
                ex = A.act(pm[:, hh, :], sc[j][:, h, :], ACT.Exp, neg, *ret_roped, bias=st[:, 4 + hh:5 + hh],
                           scale=MLA_SCALE, accum_out=st[:, 8 + hh:9 + hh])
                exps.append(ex)
            bf[j] = ex
        yield exps
        rsum = V.recip(st[:, 16:20], st[:, 8:12], *exps)
        pt = buf["a2"][:, 0:4 * n_k]
        ready = []
        for j in range(4 // per):
            m = P.turn([([b0, b1][j][:, 128 * i:128 * i + 128], buf["pr"][:, 512 * j + 128 * i:512 * j + 128 * i + 128])
                        for i in range(4)], ident[:, :], *exps, bf[j])
            ready.append(m)
        for j in range(4 // per):
            yield ready[j]
            ready[j] = bf[j] = A.copy(pt[:, 512 * j:512 * j + 512], [b0, b1][j][:, :], ready[j], mr)
        yield ready
        ps = []
        for h in range(4):
            for kt in range(t + 1):
                c = h * n_k + kt * 128
                ps.append((b0[:, 64 * h:64 * h + 64], pt[:, c:c + 128], B[kt]["mv"][:, 64 * h:64 * h + 64], kt == 0, kt == t))
        m = P.mms(ps, *ready, mv, mv0, bf[0])
        yield [m, rsum]
        ym = V.tt(buf["q"][:, 0:256].rearrange("p (h e) -> p h e", h=4), b0[:, 0:256].rearrange("p (h e) -> p h e", h=4),
                  st[:, 16:20].unsqueeze(2).to_broadcast([128, 4, 64]), ALU.mult, m, rsum, s["q_free"])
        s["acc_free"] = ym
        s["b1_free"] = bf[1]
        yield from turned(buf["q"], [ym], 3)
        if t == 1:
            for r in range(2):
                region_open(r, region_until(r, layer + 1), *(q.mark() for q in (V, A, P, G)))
            load_ahead()

    def group_of(t, xt):
        s = state[t]

        def group(w, nk, *parts):
            b, free = yield from take()
            for i, part in enumerate(parts):
                x = [(yield xt[0])]
                if nk == 8 or part:
                    x.append((yield xt[1]))
                _, m = yield from chunk_use(t, group_products(t, b, w, part, nk), free if i == 0 else None, *x)
            s["xt_free"] = m
            return b, m

        return group

    def evacuate(b, m, ev, emit):
        def work():
            marks = emit()
            last = marks[-1] if isinstance(marks, tuple) else marks
            give(b, last)
            ev.set(marks)

        plan.after(work, m)

    def known(marks):
        out = []
        for m in marks:
            if isinstance(m, Later):
                m = yield m
            out.append(m[0] if isinstance(m, list) else m)
        return out

    def gated_sum(t, lhs_of, n_branch, n_chunk, out, yt_used, gate_free, merged_free):
        s = state[t]
        gate, merged = GATE[t], MERGED[t]
        group = s["group"]
        total = [None, None]
        for n in range(n_branch):
            th = [plan.later(), plan.later()]
            for h in range(2):
                c = slice(512 * h, 512 * h + 512)
                b, m = yield from group(512, 4, 0, 1)

                def squash(b=b, m=m, c=c, before=total[h], th=th[h]):
                    free = yield from known([before] if before else gate_free)
                    yield free
                    y = A.act(gate[:, c], b[:, :], ACT.Tanh, m, *free, scale=0.5)
                    give(b, y)
                    th.set(y)

                plan.start(squash(), m)
            ready = yield out[n]
            yield ready
            bs = []
            for h in range(2):
                bs.append((yield from take()))
            for i in range(n_chunk):
                m = yield from chunk_use(t, wide_products(lhs_of(n), [bs[0][0], bs[1][0]], 0, 2 * n_chunk - 1, 2 * i),
                                         ready, bs[0][1], bs[1][1])
            yt_used[n].set(m[1])

            def gather(h, m, n=n, bs=bs, th=th, before=total):
                c = slice(512 * h, 512 * h + 512)
                x = yield th[h]
                yield x
                if n == 0:
                    free = yield from known(merged_free)
                    y = V.stt(merged[:, c], gate[:, c], 1.0, bs[h][0][:, :], ALU.add, ALU.mult, m, x, *free)
                    give(bs[h][0], y)
                    return y
                y = V.stt(gate[:, c], gate[:, c], 1.0, bs[h][0][:, :], ALU.add, ALU.mult, m, x)
                give(bs[h][0], y)
                so_far = yield before[h]
                yield [y, so_far]
                return (V if n == n_branch - 1 else G).tt(merged[:, c], merged[:, c], gate[:, c], ALU.add, y, so_far)

            total = [plan.start(gather(h, m[h]), m[h]) for h in range(2)]
        total = yield from known(total)
        s["gate_free"] = total[1]
        done, s["merged_free"] = yield from xt_from(t, merged, total, s["xt_free"])
        return done

    def through_w_out(t, done):
        s = state[t]
        for i in range(4):
            x = yield done[i // 2]
            s["down"] = yield from chunk_use(t, wide_products(lambda k: xk(t, k), ACC[t], 0, KD - 1, 2 * i), x,
                                             s["acc_free"], s["b1_free"])
        s["xt_free"] = s["down"][1]

    mix_ev = {}

    def mix(t, layer, xt):
        s, buf, st = state[t], B[t], ST[t]
        ev = mix_ev[t, layer] = {n: plan.later() for n in ("cq", "qk", "vg", "g", "uv", "z", "rkt", "mkt", "mv")}
        out, yt_used = [plan.later() for _ in range(4)], [plan.later() for _ in range(4)]
        group = s["group"] = group_of(t, xt)
        side = plan.start(branches(t, layer, ev, out, yt_used, mix_ev[0, layer]))
        act_free = s["act_free"]

        b, m = yield from group(416, 4, 0, 1)
        yield from region_end(t)

        def evacuated(b, m, name, emit):
            evacuate(b, m, ev[name], lambda: emit(b, m))

        def cq(b, m):
            A.act(buf["kcat"][:, 0:256], b[:, 0:256], ACT.Square, m, accum_out=st[:, 20:21])
            q = A.act(buf["kcat"][:, 256:384], b[:, 256:384], ACT.Square, m, accum_out=st[:, 21:22])
            return q, A.copy(buf["a2"][:, 0:416], b[:, 0:416], m)

        evacuated(b, m, "cq", cq)
        b, m = yield from group(512, 4, 0, 1)
        evacuated(b, m, "qk", lambda b, m: A.copy(buf["pr"][:, 0:512], b[:, :], m))
        b, m = yield from group(512, 4, 0, 1)

        def vg(b, m):
            ev["g"].set(A.act(buf["a5"][:, :], b[:, 256:512], ACT.Silu, m))
            return A.copy(buf["rv"][:, :], b[:, 0:256], m, s.get("rv_free"))

        evacuated(b, m, "vg", vg)
        b, m = yield from group(512, 4, 0, 1)
        evacuated(b, m, "uv", lambda b, m: A.act(buf["a4"][:, :], b[:, :], ACT.Gelu_apprx_tanh, m))
        b, m = yield from group(256, 8, 0)
        evacuated(b, m, "z", lambda b, m: A.copy(buf["z"][:, :], b[:, 0:256], m, s.get("z_free")))

        def lhs_of(n):
            def lhs(k):
                c = slice(256 * (n % 2) + 128 * k, 256 * (n % 2) + 128 * k + 128)
                return YTH[t][:, c], YTL[t][:, c]
            return lhs

        done = yield from gated_sum(t, lhs_of, 4, 1, out, yt_used, [s["gate_free"]], act_free)
        s["yt_free"] = [(yield yt_used[2]), (yield yt_used[3])]
        yield side
        yield from through_w_out(t, done)

    def ple(t, xt):
        s = state[t]
        kept = []
        for h in range(2):
            b, free = yield from take()

            def products(hi, lo, b=b):
                out = []
                for k in range(2):
                    o, c = 256 * k + 128 * t, slice(512 + 512 * k, 1024 + 512 * k)
                    out.append((b[:, :], (hi[:, o:o + 128], lo[:, o:o + 128]), (hi[:, c], lo[:, c]), k == 0, k == 1))
                return [], out

            m, = yield from chunk_use(t, products, free)
            kept.append(plan.later())
            evacuate(b, m, kept[h], lambda h=h, b=b, m=m: A.copy(MERGED[t][:, 512 * h:512 * h + 512], b[:, :], m,
                                                                s["merged_free"]))
        xt = yield from xt()
        group = group_of(t, xt)
        added = []
        for h in range(2):
            b, m = yield from group(512, 4, 0, 1)

            def add(h=h, b=b, m=m):
                c = slice(512 * h, 512 * h + 512)
                th = A.act(GATE[t][:, c], b[:, :], ACT.Tanh, m, s["gate_free"], scale=0.5)
                give(b, th)
                k = yield kept[h]
                yield [th, k]
                y = V.stt(MERGED[t][:, c], GATE[t][:, c], 1.0, MERGED[t][:, c], ALU.add, ALU.mult, th, k)
                yield y
                s["gate_free"] = s["merged_free"] = s["x"] = V.stt(X[t][:, c], MERGED[t][:, c], 0.5, X[t][:, c], ALU.mult, ALU.add, y, s["x"])

            added.append(plan.start(add(), m))
        return xt, added

    mods = nc.dram_tensor("mods", [6, D], F32, kind="Internal").ap()
    ada = dict(block=0, part=0, rows=[], last=None)
    mod_slot = [[sem(f"mod_out{i}"), 0] for i in range(6)]
    b_ada, norms, col, row = (RT[0][:, c:c + n] for c, n in ((0, 48), (48, 16), (64, 8), (72, 128)))

    def ada_row(j, m):
        acc = GATE[j % 2]
        b, free = yield from take()
        yield [m, free]
        pm = P.mms([(b[:, k:k + 1], acc[:, 128 * k:128 * k + 128], ones[:, 0:1], True, True) for k in range(KD)], m, free,
                   CONST["all"])
        yield pm
        y = V.tt(col, b[:, 0:KD], b_ada[:, KD * j:KD * j + KD], ALU.add, pm, *ada["rows"][-1:])
        give(b, y)
        if j in (1, 4):
            n = KD * (j // 4)
            y = V.stt(col, col, 1.0, norms[:, n:n + KD], ALU.add, ALU.mult, y)
        if j == 5:
            y = V.ts(col, col, 0.5, None, ALU.mult, None, y)
        b, free = yield from take()
        yield [y, free]
        m = P.turn([(b[0:KD, 0:128], col)], ident[:, :], y, free)
        yield m
        r = V.copy(row[0:KD, :], b[0:KD, 0:128], m)
        give(b, r)
        ada["rows"].append(G.load(mod_slot[j], mods[j].rearrange("(k c) -> k c", c=128), row[0:KD, :], r))
        return [pm]

    ada_made = []

    def ada_chunk(i):
        j, part = ada["block"], ada["part"]
        acc = GATE[j % 2]
        raw = SLOTS[raw_of[i]][0][0]
        m = ada["last"]
        free = (yield ada_made[j - 2]) if part == 0 and j > 1 else ()
        for w in range(2):
            k = 2 * part + w
            cond = cond_t[:, k:k + 1]
            src = raw[:, 1024 * w:1024 * w + 1024]
            if k == 0:
                m = V.ts(acc[:, :], src, cond, None, ALU.mult, None, loaded[i][0], *free, ada["cond"])
            else:
                m = V.stt(acc[:, :], src, cond, acc[:, :], ALU.mult, ALU.add, loaded[i][0], m)
            yield m
        ada["last"] = m
        ada["part"] = part + 1
        if part == 3:
            ada["block"], ada["part"] = j + 1, 0
            ada_made.append(plan.start(ada_row(j, m), m))
        return m

    TT = {}

    def load_second():
        after = small_users
        for out, name in ((before, "before"), (conv_w, "conv_w"), (conv_b, "conv_b"), (lru_a, "lru_a"), (lru_x, "lru_x"),
                          (ba, "lru_ba"), (bx, "lru_bx"), (sp, "lru_lambda"), (w_router, "w_router")):
            G.load(small2, out[:, :], a[name], *after)
        for out, name in ((gains[0], "diff_qnorm"), (gains[1], "diff_knorm"), (gains[2], "swa_qnorm"),
                          (gains[3], "swa_knorm"), (subln, "diff_subln"), (sinks, "swa_sinks"), (lamv, "diff_lambda"),
                          (b_router, "b_router")):
            G.load(small2, out[:, :], rows(a[name]), *after)
        G.load(small2, rel[0:32, :], a["rel_bias"], *after)
        G.load(small2, buckets[0:32, :], a["buckets"], *after)
        m = TT["m"] = G.load(small2, future[0:12, :], a["future"], *after)
        plan.start(parameters(m), m)

    def parameters(m):
        yield 20.0
        b, free = yield from take()
        pm = P.mms([(b[0:12, 0:384], rel[0:32, :], buckets[0:32, :], True, True)], m, free)
        yield pm
        y = V.tt(future[0:12, :], b[0:12, 0:384], future[0:12, :], ALU.add, pm)
        give(b, y)
        w = G.load([sem("toeplitz_out"), 0], toeplitz.rearrange("c h j -> h c j"),
                   future[0:12, :].unsqueeze(1).to_broadcast([12, 128, 384]), y)
        src = bass.AP(tensor=toeplitz.tensor, offset=127, ap=[[12 * 384 - 1, 128], [384, 12], [1, 256]])
        TT["bias"] = G.load([sem("toeplitz_in"), 0], bm[:, :].rearrange("p (h k) -> p h k", h=12), src, w)
        TT["dg"] = V.tt(gains[1][:, :], gains[0][:, :], gains[1][:, :], ALU.mult, m)
        TT["sg"] = V.tt(gains[3][:, :], gains[2][:, :], gains[3][:, :], ALU.mult, m)
        TT["sub"] = V.ts(subln[:, :], subln[:, :], 0.8, None, ALU.mult, None, m)
        l1 = V.tt(lamv[:, 0:64], lamv[:, 0:64], lamv[:, 64:128], ALU.mult, m)
        l2 = V.tt(lamv[:, 128:192], lamv[:, 128:192], lamv[:, 192:256], ALU.mult, m)
        yield [l1, l2]
        l3 = V.reduce(lam[:, 0:2], lamv[:, :].rearrange("p (a b) -> p a b", a=2)[:, :, 0:64], ALU.add, l1, l2)
        yield l3
        l4 = A.act(lam[:, 0:2], lam[:, 0:2], ACT.Exp, l3)
        yield l4
        l5 = V.tt(lam[:, 2:3], lam[:, 1:2], lam[:, 0:1], ALU.subtract, l4)
        yield l5
        TT["lam"] = V.ts(lam[:, 2:3], lam[:, 2:3], -0.2, None, ALU.add, None, l5)
        n1 = V.stt(lt[:, 0:4], sp[:, :], -1.0, sp[:, :], ALU.mult, ALU.max, m)
        yield n1
        n2 = A.act(lt[:, 0:4], lt[:, 0:4], ACT.Exp, n1, scale=-1.0)
        yield n2
        n3 = V.ts(lt[:, 4:8], lt[:, 0:4], 2.0, None, ALU.add, None, n2)
        yield n3
        n3 = V.recip(lt[:, 4:8], lt[:, 4:8], n3)
        yield n3
        n3 = V.tt(lt[:, 0:4], lt[:, 0:4], lt[:, 4:8], ALU.mult, n3)
        yield n3
        n4 = V.tt(lt[:, 4:8], lt[:, 0:4], lt[:, 0:4], ALU.mult, n3)
        yield n4
        p = V.ts(lt[:, 8:12], lt[:, 4:8], 1.0 / 19, None, ALU.mult, None, n4)
        for k in range(8, 0, -1):
            yield p
            p = V.stt(lt[:, 8:12], lt[:, 8:12], 1.0 / (2 * k + 1), lt[:, 4:8], ALU.add, ALU.mult, p)
        yield p
        p = V.stt(lt[:, 8:12], lt[:, 8:12], 1.0, lt[:, 0:4], ALU.add, ALU.mult, p)
        yield p
        q = V.ts(sp[:, :], sp[:, :], -4.0, 0.0, ALU.mult, ALU.max, p)
        yield q
        q = V.stt(sp4[:, 0:4], lt[:, 8:12], 8.0, sp[:, :], ALU.mult, ALU.add, q)
        yield q
        q = V.ts(sp4[:, 4:8], sp4[:, 0:4], -1.0, None, ALU.mult, None, q)
        q = V.ts(ba[:, :], ba[:, :], 0.5, None, ALU.mult, None, q)
        TT["lru"] = V.ts(bx[:, :], bx[:, :], 0.5, None, ALU.mult, None, q)

    def rms(t, row, shift, dst, ready, scratch, free, *after):
        x, st = X[t], ST[t]
        halves = [slice(0, 512), slice(512, 1024)]
        q = []
        for h, c in enumerate(halves):
            yield ready[h]
            urgent[0] += 1 - h
            q.append(A.act(scratch[h][:, :], x[:, c], ACT.Square, ready[h], free, scale=D ** -0.5, accum_out=st[:, 12 + h:13 + h]))
        yield [*q, *after]
        z = [None, None]

        def gained(h):
            def f():
                c = halves[h]
                z[h] = V.tt(dst[:, c], x[:, c], row[:, c], ALU.mult, *ready, *after)
            return f

        e = V.ts(st[:, 14:15], st[:, 12:13], st[:, 13:14], RMS_EPS, ALU.add, ALU.add, *q)
        yield e
        r = yield from rsqrt(st[:, 14:15], st[:, 15:16], st[:, 16:17], e, [gained(0), gained(1)])
        out = [V.stt(dst[:, c], dst[:, c], st[:, 15:16], shift[:, c], ALU.mult, ALU.add, r, z[h])
               for h, c in enumerate(halves)]
        urgent_until(out[1])
        urgent[0] -= 1
        return out, q[1]

    def second_branches(t, ev, out, yt_used, prev):
        c, st, s = C[t], ST[t], state[t]
        b0, b1 = ACC[t]
        both = [b0, b1]
        bf = [s["acc_free"], s["acc_free"]]
        n_k = 128 * (t + 1)

        def cc4(ap):
            return ap.rearrange("p (c n) -> p c n", c=4)

        xrt = cc4(c["xrt"][:, 0:524])
        big = c["big"]
        xc, grt, tp, ig = (big[:, 512 * i:512 * i + 512] for i in range(4))
        xr_in = yield ev["xr"]
        yield [xr_in, bf[0]]
        m = P.turn([(b0[:, 128 * k:128 * k + 128], tp[:, 128 * k:128 * k + 128]) for k in range(4)], ident[:, :], xr_in, bf[0])
        yield m
        x1 = A.copy(xrt[:, :, 3:131], cc4(b0[:, :]), m)
        bf[0] = x1
        if t == 0:
            x0 = V.memset(xrt[:, :, 0:3], 0.0, x1)
        else:
            x0 = yield prev["xrt"]
            yield x0
            x0 = V.copy(xrt[:, :, 0:3], cc4(C[0]["xrt"][:, 0:524])[:, :, 128:131], x0, x1)
        ev["xrt"].set(x1)
        gr_in = yield ev["gr"]
        yield [gr_in, bf[1]]
        mg = P.turn([(b1[:, 128 * k:128 * k + 128], ig[:, 128 * k:128 * k + 128]) for k in range(4)], ident[:, :], gr_in, bf[1])
        yield mg
        gr = A.copy(grt, b1[:, :], mg)
        bf[1] = gr
        cw = conv_w[:, :].rearrange("p (c n) -> p c n", c=4)
        x4 = cc4(xc)
        yield [x0, x1]
        m = [V.ts(x4[:, i, :], xrt[:, i, 0:128], cw[:, i, 0:1], conv_b[:, i:i + 1], ALU.mult, ALU.add, x0, x1, TT["m"])
             for i in range(4)]
        for tap in range(1, 4):
            yield m
            m = [V.stt(x4[:, i, :], xrt[:, i, tap:tap + 128], cw[:, i, tap:tap + 1], x4[:, i, :], ALU.mult, ALU.add, m[i])
                 for i in range(4)]
        yield [*m, *bf]
        ga = P.mms([(b0[:, 128 * i:128 * i + 128], lru_a[:, 128 * i:128 * i + 128], x4[:, i, :], True, True) for i in range(4)],
                   *m, bf[0], TT["m"])
        gx = P.mms([(b1[:, 128 * i:128 * i + 128], lru_x[:, 128 * i:128 * i + 128], x4[:, i, :], True, True) for i in range(4)],
                   bf[1])
        yield ga
        ra = [A.act(cc4(tp)[:, i, :], b0[:, 128 * i:128 * i + 128], ACT.Tanh, ga, TT["lru"], bias=ba[:, i:i + 1], scale=0.5)
              for i in range(4)]
        bf[0] = ra[3]
        yield [gx, ra[0]]
        rx = [A.act(cc4(ig)[:, i, :], b1[:, 128 * i:128 * i + 128], ACT.Tanh, gx, mg, bias=bx[:, i:i + 1], scale=0.5)
              for i in range(4)]
        bf[1] = rx[3]
        aa = c["aa"]
        yield [ra[3], rx[0]]
        ea = [A.act(cc4(aa[:, :])[:, i, :], cc4(tp)[:, i, :], ACT.Exp, ra[i], bias=sp4[:, 4 + i:5 + i],
                    scale=sp4[:, 4 + i:5 + i]) for i in range(4)]
        yield [rx[3], ea[0]]
        ta = [A.act(cc4(tp)[:, i, :], cc4(tp)[:, i, :], ACT.Tanh, ea[i], bias=sp4[:, i:i + 1], scale=sp4[:, i:i + 1])
              for i in range(4)]
        bb = V.stt(ig, ig, 1.0, xc, ALU.add, ALU.mult, *rx)
        yield ea
        sq = xrt[:, :, 0:128]
        u = V.tt(sq, cc4(aa[:, :]), cc4(aa[:, :]), ALU.mult, *ea)
        yield [u, *ta]
        u = V.stt(cc4(tp), sq, 1.0, cc4(tp), ALU.add, ALU.mult, u, *ta)
        yield u
        rt = A.act(tp, tp, ACT.Sqrt, u, scale=0.25)
        yield [rt, bb]
        bb = V.tt(ig, ig, tp, ALU.mult, rt, bb)
        init_in = None if t == 0 else (yield prev["hl"])
        yield [bb, init_in]
        hs = []
        for i in range(4):
            init = 0.0 if t == 0 else C[0]["hl"][:, i:i + 1]
            hs.append(V.put(lambda e, i=i, init=init: e.tensor_tensor_scan(
                x4[:, i, :], cc4(aa[:, :])[:, i, :], cc4(ig)[:, i, :], init, op0=ALU.mult, op1=ALU.add),
                bb, *ea, init_in, busy=0.2))
        hl = V.copy(c["hl"][:, 0:4].unsqueeze(2), x4[:, :, 127:128], *hs)
        ev["hl"].set(hl)
        o = V.tt(xc, xc, grt, ALU.mult, *hs, gr, hl)
        yield o
        hi = A.copy(YTH[t][:, :], xc, o, *s["yt_free"])
        yield hi
        lo = V.tt(YTL[t][:, :], xc, YTH[t][:, :].bitcast(F32), ALU.subtract, hi)
        out[0].set(lo)
        big_free = lo
        def heads(ap):
            return ap.rearrange("p (h d) -> p h d", d=64)

        in_ = []
        for n in ("dq", "dk", "sk", "sq"):
            in_ += yield ev[n]
        yield in_
        ms = V.ts(st[:, 64:90], st[:, 64:90], 1.0 / 64, RMS_EPS, ALU.mult, ALU.add, *in_)
        yield ms
        r = yield from rsqrt(st[:, 64:90], st[:, 90:116], st[:, 116:142], ms)

        def normed(buf, n, first):
            return V.tt(heads(buf), heads(buf), st[:, first:first + n].unsqueeze(2).to_broadcast([128, n, 64]), ALU.mult, r)

        dk = normed(c["dk"][:, :], 8, 98)
        dq = normed(c["dq"][:, :], 8, 90)
        dk = G.tt(heads(c["dk"][:, :]), heads(c["dk"][:, :]), gains[1][:, :].unsqueeze(1).to_broadcast([128, 8, 64]),
                  ALU.mult, dk, TT["dg"])

        def turn4(dst, src, b, n, *after):
            yield [*after, bf[b]]
            m = P.turn([(both[b][:, 128 * k:128 * k + 128], src[:, 128 * k:128 * k + 128]) for k in range(n)], ident[:, :],
                       *after, bf[b])
            yield m
            bf[b] = A.copy(dst, both[b][:, 0:128 * n], m)
            return bf[b]

        qt = yield from turn4(c["dq"][:, :], c["dq"], 0, 4, dq)
        sk = normed(c["sk"][:, :], 2, 114)
        sk = G.tt(heads(c["sk"][:, :]), heads(c["sk"][:, :]), gains[3][:, :].unsqueeze(1).to_broadcast([128, 2, 64]),
                  ALU.mult, sk, TT["sg"])
        sq_ = normed(c["sq"][:, :], 8, 106)
        kt = yield from turn4(c["kt"][:, :], c["dk"], 1, 4, dk)
        ev["kt"].set(kt)
        sqt = yield from turn4(c["sq"][:, :], c["sq"], 0, 4, sq_)
        skt = yield from turn4(c["skt"][:, :], c["sk"], 1, 1, sk)
        ev["skt"].set(skt)
        S_, PT = big[:, 0:1024], big[:, 1024:2048]
        O = c["dk"]
        per = 4 if t == 0 else 2
        rounds = 4 // per
        o_free = kt
        s_free, pt_free = big_free, big_free
        kt0, skt0 = (yield prev["kt"]), (yield prev["skt"])
        sv_in, sv0 = (yield ev["skv"]), (yield prev["skv"])
        dv_in, dv0 = (yield ev["dv"]), (yield prev["dv"])
        for kind in range(2):
            q, k_, rowk = (c["dq"], "kt", kt0) if kind == 0 else (c["sq"], "skt", skt0)
            kmark = kt if kind == 0 else skt
            qmark = qt if kind == 0 else sqt
            done = []
            for rd in range(rounds):
                sv = S_.rearrange("p (u j k) -> p u j k", u=2, j=per)
                bias = bm[:, :].rearrange("p (h k) -> p h k", h=12)[:, :, 256 - n_k:256]
                yield [qmark, kmark, rowk, s_free, *bf]
                ms = []
                for u in range(2):
                    ps = []
                    for j in range(per):
                        blk = rd * per + j
                        for kk in range(t + 1):
                            col = 128 * blk if kind == 0 else 0
                            ps.append((both[u][:, j * n_k + 128 * kk:j * n_k + 128 * kk + 128],
                                       q[64 * u:64 * u + 64, 128 * blk:128 * blk + 128],
                                       C[kk][k_][64 * u:64 * u + 64, col:col + 128], True, True))
                    qt_used = m = P.mms(ps, qmark, kmark, rowk, bf[u])
                    ms.append(m)
                sm = []
                for u in range(2):
                    if kind == 0:
                        bv = bias[:, rd * per:rd * per + per, :]
                    else:
                        bv = bias[:, 4:12, :].rearrange("p (g u) k -> p g u k", u=2)[:, rd * per:rd * per + per, u, :]
                    yield ms[u]
                    bf[u] = V.stt(sv[:, u], both[u][:, 0:per * n_k].rearrange("p (j k) -> p j k", j=per), 0.125, bv,
                                  ALU.mult, ALU.add, ms[u], TT["bias"], s_free)
                    sm.append(bf[u])
                n = 2 * per
                yield sm
                mx = V.reduce(st[:, 0:n], S_[:, 0:n * n_k].rearrange("p (x k) -> p x k", k=n_k), ALU.max, *sm)
                yield mx
                if kind == 1:
                    sk_v = sinks[:, :].rearrange("p (u g) -> p u g", u=2)[:, :, rd * per:rd * per + per]
                    mx = V.tt(st[:, 0:n].rearrange("p (u j) -> p u j", u=2), st[:, 0:n].rearrange("p (u j) -> p u j", u=2),
                              sk_v, ALU.max, mx, TT["m"])
                    yield mx
                neg = V.ts(st[:, 8:8 + n], st[:, 0:n], -1.0, None, ALU.mult, None, mx)
                yield neg
                ex = [A.act(S_[:, x * n_k:x * n_k + n_k], S_[:, x * n_k:x * n_k + n_k], ACT.Exp, neg,
                            bias=st[:, 8 + x:9 + x], accum_out=st[:, 16 + x:17 + x]) for x in range(n)]
                if kind == 1:
                    es = V.tt(st[:, 24:24 + n].rearrange("p (u j) -> p u j", u=2), sk_v,
                              st[:, 0:n].rearrange("p (u j) -> p u j", u=2), ALU.subtract, mx)
                    es = A.act(st[:, 24:24 + n], st[:, 24:24 + n], ACT.Exp, es)
                    yield [es, *ex]
                    su = V.tt(st[:, 16:16 + n], st[:, 16:16 + n], st[:, 24:24 + n], ALU.add, es, *ex)
                    yield su
                    rs = V.recip(st[:, 32:32 + n], st[:, 16:16 + n], su)
                    pts = []
                    for u in range(2):
                        pts.append(P.turn([(both[u][:, 128 * i:128 * i + 128], S_[:, 512 * u + 128 * i:512 * u + 128 * i + 128])
                                           for i in range(4)], ident[:, :], *ex, bf[u]))
                    s_free = pts[1]
                    for u in range(2):
                        yield pts[u]
                        pts[u] = bf[u] = A.copy(PT[:, 512 * u:512 * u + 512], both[u][:, :], pts[u], pt_free)
                    yield pts
                    ps = []
                    for j in range(per):
                        for u in range(2):
                            for kk in range(t + 1):
                                i = 512 * u + j * n_k + 128 * kk
                                ps.append((b0[:, 64 * (2 * j + u):64 * (2 * j + u) + 64], PT[:, i:i + 128],
                                           C[kk]["sv"][:, 64 * u:64 * u + 64], kk == 0, kk == t))
                    m = P.mms(ps, *pts, sv_in, sv0, bf[0])
                    pt_free = m
                    yield [m, rs, o_free]
                    ov = O[:, 128 * per * rd:128 * per * rd + 128 * per].rearrange("p (j u e) -> p j u e", j=per, u=2)
                    rv = st[:, 32:32 + n].rearrange("p (u j) -> p j u", u=2).unsqueeze(3).to_broadcast([128, per, 2, 64])
                    bf[0] = V.tt(ov, b0[:, 0:128 * per].rearrange("p (j u e) -> p j u e", j=per, u=2), rv, ALU.mult, m, rs, o_free)
                    done.append(bf[0])
                else:
                    yield ex
                    rs = V.recip(st[:, 32:32 + n], st[:, 16:16 + n], *ex)
                    yield rs
                    rs = V.ts(st[:, 32 + per:32 + n], st[:, 32 + per:32 + n], lam[:, 2:3], None, ALU.mult, None, rs, TT["lam"])
                    yield rs
                    p1 = [A.act(sv[:, 1, j], sv[:, 1, j], ACT.Copy, rs, scale=st[:, 32 + per + j:33 + per + j])
                          for j in range(per)]
                    at_ = []
                    for j in range(per):
                        yield p1[j]
                        at_.append(V.stt(sv[:, 0, j], sv[:, 0, j], st[:, 32 + j:33 + j], sv[:, 1, j], ALU.mult, ALU.add, p1[j]))
                    yield [*at_, bf[0]]
                    m = P.turn([(b0[:, 128 * i:128 * i + 128], S_[:, 128 * i:128 * i + 128]) for i in range(4)],
                               ident[:, :], *at_, bf[0])
                    s_free = m
                    yield m
                    bf[0] = A.copy(PT[:, 0:512], b0[:, :], m, pt_free)
                    yield [bf[0], bf[1]]
                    ps = []
                    for j in range(per):
                        for kk in range(t + 1):
                            i = j * n_k + 128 * kk
                            blk = rd * per + j
                            ps.append((b1[:, 128 * j:128 * j + 128], PT[:, i:i + 128],
                                       C[kk]["dv"][:, 128 * blk:128 * blk + 128], kk == 0, kk == t))
                    m = P.mms(ps, bf[0], dv_in, dv0, bf[1])
                    pt_free = m
                    yield m
                    bf[1] = A.copy(O[:, 128 * per * rd:128 * per * rd + 128 * per], b1[:, 0:128 * per], m, o_free)
                    done.append(bf[1])
            if kind == 0:
                yield done
                q2 = A.act(PT[:, 0:512], O[:, :], ACT.Square, *done, pt_free)
                yield q2
                v = V.reduce(st[:, 0:4], PT[:, 0:512].rearrange("p (h e) -> p h e", h=4), ALU.add, q2)
                pt_free = v
                yield v
                v = V.ts(st[:, 0:4], st[:, 0:4], 1.0 / 128, RMS_EPS, ALU.mult, ALU.add, v)
                yield v
                r = yield from rsqrt(st[:, 0:4], st[:, 4:8], st[:, 8:12], v)
                o4 = O[:, :].rearrange("p (h e) -> p h e", h=4)
                y = V.tt(o4, o4, st[:, 4:8].unsqueeze(2).to_broadcast([128, 4, 128]), ALU.mult, r)
                yield y
                y = G.tt(o4, o4, subln[:, :].unsqueeze(1).to_broadcast([128, 4, 128]), ALU.mult, y, TT["sub"])
                done = [y]

            def turned(done, O, n):
                free = yield yt_used[n - 1]
                b, f = yield from take()
                yield [f, *done]
                m = P.turn([(b[:, 128 * k:128 * k + 128], O[:, 128 * k:128 * k + 128]) for k in range(4)], ident[:, :], *done, f)
                yield m
                l = yield from split_into(YTH[t][:, :], YTL[t][:, :], b[:, :], lambda l: give(b, l), m, free)
                out[n].set(l)

            if kind == 0:
                plan.start(turned(done, O, 1), *done)
                O, o_free = c["dq"], qt_used
            else:
                s["acc_free"], s["b1_free"] = bf
                yield from turned(done, O, 2)

    hybrid_ev = []

    def hybrid(t, xt):
        s, st, c = state[t], ST[t], C[t]
        names = ("xr", "gr", "dq", "dk", "sk", "skv", "sq", "dv", "xrt", "hl", "kt", "skt")
        ev = {n: plan.later() for n in names}
        hybrid_ev.append(ev)
        out, yt_used = [plan.later() for _ in range(3)], [plan.later() for _ in range(3)]
        group = s["group"] = group_of(t, xt)
        side = plan.start(second_branches(t, ev, out, yt_used, hybrid_ev[0]))
        plan.start(mixers_over(side) if t else first_mixers_over(side))
        tmp = MERGED[t]
        big = c["big"]

        def heads_of(name, b, m, w, first, half, before=None, more=None):
            def work():
                sq = tmp[:, 512 * half:512 * half + w]
                free = (yield ev[before])[0] if before else s["h_turned"]
                q = A.act(sq, b[:, 0:w], ACT.Square, m, free)
                e = A.copy(c[name][:, :], b[:, 0:w], m)
                last = e
                if more:
                    last = A.copy(c[more][:, :], b[:, w:2 * w], m)
                    ev["skv"].set(last)
                give(b, last)
                yield q
                r = V.reduce(st[:, first:first + w // 64], sq.rearrange("p (h d) -> p h d", d=64), ALU.add, q)
                ev[name].set([r, e])

            plan.start(work(), m)

        b, m = yield from group(512, 4, 0, 1)
        yield from region_end(t)
        evacuate(b, m, ev["xr"], lambda b=b, m=m: A.copy(big[:, 1024:1536], b[:, :], m))
        b, m = yield from group(512, 4, 0, 1)
        evacuate(b, m, ev["gr"], lambda b=b, m=m: A.act(big[:, 1536:2048], b[:, :], ACT.Gelu_apprx_tanh, m))
        b, m = yield from group(512, 4, 0, 1)
        heads_of("dq", b, m, 512, 64, 0)
        b, m = yield from group(512, 4, 0, 1)
        heads_of("dk", b, m, 512, 72, 1)
        b, m = yield from group(256, 8, 0)
        heads_of("sk", b, m, 128, 88, 0, "dq", "sv")
        b, m = yield from group(512, 4, 0, 1)
        heads_of("sq", b, m, 512, 80, 1, "dk")
        b, m = yield from group(512, 4, 0, 1)
        evacuate(b, m, ev["dv"], lambda b=b, m=m: A.copy(c["dv"][:, :], b[:, :], m))
        squares = [ev["sk"], ev["sq"]]

        def lhs_of(n):
            return lambda k: (YTH[t][:, 128 * k:128 * k + 128], YTL[t][:, 128 * k:128 * k + 128])

        done = yield from gated_sum(t, lhs_of, 3, 2, out, yt_used, rows_free, squares)
        yield side
        yield from through_w_out(t, done)

    def select(x, t, pos, weight, sel_free, selw_free, *after):
        return (V.ts(SEL[x][:, 64 * t:64 * t + 64], iota[:, 0:64], pos, None, ALU.is_equal, None, *after, sel_free),
                V.ts(SELW[:, 128 * t:128 * t + 128], iota[:, :], pos, weight, ALU.is_equal, ALU.mult, *after, selw_free))

    def select_expert(e, t, *after):
        return select(e % 2, t, RT[t][:, 64 + e:65 + e], RT[t][:, 248 + e:249 + e], *after)

    def add_x(t):
        P.mms([(ACC[t][g][:, :], ident[:, :], X[t][:, 512 * g:512 * g + 512], True, False) for g in range(2)],
              state[t]["acc_free"], *state[t]["x_done"])

    def add_bias(e, *after):
        return bias_products(ident[0:32, e:e + 1].to_broadcast([32, 64]), b1s[0:32, :], *after)

    def bias_products(lhs, bias, *after):
        halves = [(b[64 * g:64 * g + 64, :], slice(1024 * j + 512 * g, 1024 * j + 512 * g + 512))
                  for j, (b, _) in enumerate(layer_banks) for g in range(2)]
        return P.mms([(o, lhs, bias[:, c], True, False) for o, c in halves], *after)

    def route(t, ready):
        s, r, ht = state[t], RT[t], HT[t]
        lg, sel, pos, gp = r[:, 0:32], r[:, 32:64], r[:, 64:96], r[:, 248:376]
        m8, ex, su, rc, ng = r[:, 96:104], r[:, 104:108], r[:, 108:109], r[:, 109:110], r[:, 110:111]
        z = V.memset(gp, 0.0)
        turned = []
        for j in range(2):
            b, free = yield from take()
            yield [ready[j], free]
            m = P.turn([(b[:, 128 * k:128 * k + 128], MERGED[t][:, 512 * j + 128 * k:512 * j + 128 * k + 128]) for k in range(4)],
                       ident[:, :], ready[j], free)
            turned.append((b, m))
        for j, (b, m) in enumerate(turned):
            yield m
            turned[j] = A.copy(ht[j][:, :], b[:, :], m)
            give(b, turned[j])
        b, free = yield from take()
        for j in range(2):
            yield turned[j]
            m = P.mms([(b[:, 0:32], ht[j][:, 128 * k:128 * k + 128], w_router[:, 128 * j + 32 * k:128 * j + 32 * k + 32],
                        j + k == 0, j * k == 3) for k in range(4)], turned[j], free, TT["m"])
        yield m
        m = V.tt(lg, b[:, 0:32], b_router[:, :], ALU.add, m)
        give(b, m)
        yield m
        mx = V.put(lambda e: e.max(m8, lg), m)
        yield mx
        ix = V.put(lambda e: e.max_index(RI[t][:, :], m8, lg), mx)
        ng_ = V.ts(ng, m8[:, 0:1], -1.0, None, ALU.mult, None, mx)
        yield [ix, ng_]
        ix = V.copy(r[:, 244:248], RI[t][:, 0:4], ix)
        e = A.act(ex, m8[:, 0:4], ACT.Exp, ng_, bias=ng, accum_out=su)
        yield ix
        m = V.ts(sel, iota[:, 0:32], r[:, 244:245], None, ALU.is_equal, None, ix, CONST["all"])
        for k in range(1, 4):
            yield m
            m = V.stt(sel, iota[:, 0:32], r[:, 244 + k:245 + k], sel, ALU.is_equal, ALU.add, m)
        s["sel"] = m
        s["sel_known"].set(m)
        yield e
        rc_ = V.recip(rc, su, e)
        yield rc_
        w = V.ts(ex, ex, rc, None, ALU.mult, None, rc_)
        sel0 = yield state[0]["sel_known"]
        yield [m, sel0]
        b, free = yield from take()
        ps = [(b[:, 0:32], before[:, :], sel, True, t == 0)]
        if t:
            ps.append((b[:, 0:32], ones[:, 0:1].to_broadcast([128, 128]), RT[0][:, 32:64], False, True))
        pm = P.mms(ps, m, sel0, free, CONST["all"], TT["m"])
        g = z
        for k in range(4):
            yield [g, w]
            one = V.ts(r[:, 116:148], iota[:, 0:32], r[:, 244 + k:245 + k], ex[:, k:k + 1], ALU.is_equal, ALU.mult, g, w)
            yield one
            g = V.tt(gp[:, 0:32], gp[:, 0:32], r[:, 116:148], ALU.add, one)
        yield pm
        p = V.stt(pos, b[:, 0:32], -999.0, sel, ALU.add, ALU.mult, pm)
        give(b, p)
        yield p
        p = V.ts(pos, pos, 999.0, None, ALU.add, None, p)
        s["gp"] = g
        s["selected"] = select_expert(0, t, None, None, p, g)

    def experts(b_in):
        PA, PB = (b for b, _ in layer_banks)
        (PC, c_free), (PM, m_free) = spare
        free = dict(A=None, B=None, C=c_free, M=m_free)
        ring_used, extra_in, extra_used = {}, {}, {}
        sel_free, xe_free = [None, None], [None, None]
        selt_free, y_free = [None, None, None], [None, None, None]
        last = dict(selw=None, act=None, actt=None, bias=None)
        sel, xe, selt, ymark = {}, {}, {}, {}

        def ring(e, k):
            if e < N_EXP:
                n = 12 * e + k
                return RING[ring_order[n % NRING]], ring_in[n]
            n = 12 * (e - N_EXP) + k
            return RING[extra_slot(n)], extra_in[n]

        def extra_slot(n):
            return ring_order[(12 * N_EXP + n % 4) % NRING]

        def extra_load(n):
            k = n % 12
            src = a["w1" if k < 8 else "w2"]
            extra_in[n] = S.load(extra_sem[n % 4], RING[extra_slot(n)][:, :],
                                 lambda: src[bass.ds(S.regs["e"], 1), k % 8].rearrange("a p c -> (a p) c"),
                                 extra_used[n - 4] if n >= 4 else ring_used[12 * N_EXP - NRING + n])

        def ring_over(e, k, mark):
            if e < N_EXP:
                ring_used[12 * e + k] = mark
                if 12 * e + k + NRING < 12 * N_EXP:
                    ring_load(12 * e + k + NRING, mark)
            else:
                extra_used[12 * (e - N_EXP) + k] = mark
                if k < 8:
                    extra_load(12 * (e - N_EXP) + k + 4)

        def gathering(b, x, tiles):
            return [(b[:, 64 * k:64 * k + 64], MERGED[t][:, 128 * k:128 * k + 128], SEL[x][:, 64 * t:64 * t + 64],
                     t == tiles[0], t == tiles[-1]) for k in range(KD) for t in tiles]

        def gather(i, x):
            m = P.mms(gathering(PM, x, range(NT)), *(p for p, _ in sel[i]), free["M"])
            sel_free[x] = m
            free["M"] = xe[i] = A.copy(XE[x][:, :], PM[:, :], m, xe_free[x])

        def gather_first():
            m = P.mms(gathering(PM, 0, [0]), sel[0][0][0], free["M"])
            free["M"] = x = A.copy(XE[0][:, :], PM[:, :], m, sel[0][0][1])
            sel_free[0] = m = P.mms(gathering(PC, 0, [1]), sel[0][1][0], free["C"])
            free["C"] = xe[0] = V.tt(XE[0][:, :], PC[:, :], XE[0][:, :], ALU.add, m, x)

        def turn_weights(i, x):
            m = P.turn([(PM[:, 128 * t:128 * t + 128], SELW[:, 128 * t:128 * t + 128]) for t in range(NT)], ident[:, :],
                       *(w for _, w in sel[i]), free["M"])
            last["selw"] = m
            free["M"] = selt[i] = A.copy(SELT[x][:, :], PM[:, 0:256], m, selt_free[x])

        def scatter(i, x, stop, banks=[(t, g) for t in range(NT) for g in range(2)]):
            m = P.mms([(ACC[t][g][:, :], SELT[x][64 * g:64 * g + 64, 128 * t:128 * t + 128], Y[x][64 * g:64 * g + 64, :],
                        False, stop) for t, g in banks], selt[i], *(ymark[i][g] for _, g in banks))
            selt_free[x] = y_free[x] = m
            return m

        def first_layer(i, x, bias):
            halves = [(pb[64 * g:64 * g + 64, :], slice(1024 * j + 512 * g, 1024 * j + 512 * g + 512))
                      for j, pb in enumerate((PA, PB)) for g in range(2)]
            last["bias"] = bias
            for k in range(KD):
                w, w_in = ring(i, k)
                m = P.mms([(o, XE[x][:, 64 * k:64 * k + 64], w[:, c], False, k == KD - 1) for o, c in halves], w_in, xe[i])
                ring_over(i, k, m)
            xe_free[x] = m
            free["A"] = glu = V.ts(GLU[:, :], PA[:, :], LIMIT, None, ALU.min, None, m, last["act"])
            th = A.act(TH[:, :], GLU[:, :], ACT.Tanh, glu, last["act"], scale=0.5 * SWIGLU)
            free["B"] = lin = V.ts(LIN[:, :], PB[:, :], -LIMIT, LIMIT, ALU.max, ALU.min, m, last["act"])
            glu = V.stt(GLU[:, :], TH[:, :], 1.0, GLU[:, :], ALU.add, ALU.mult, th)
            return V.stt(GLU[:, :], LIN[:, :], 1.0, GLU[:, :], ALU.add, ALU.mult, glu, lin)

        def turn_act(glu):
            m = P.turn([(PC[:, 128 * j:128 * j + 128], GLU[:, 128 * j:128 * j + 128]) for j in range(4)], ident[:, :],
                       glu, free["C"])
            last["act"] = m
            return A.copy(ACTT[:, :], PC[:, :], m, last["actt"])

        def second_layer(i, x, act):
            for q in range(4):
                w, w_in = ring(i, 8 + q)
                m = []
                for g in range(2):
                    ps = []
                    for j in range(2):
                        c = 2 * q + j
                        lhs = ACTT[:, 128 * (c % 4) + 64 * (c // 4):128 * (c % 4) + 64 * (c // 4) + 64]
                        ps.append((PC[64 * g:64 * g + 64, :], lhs, w[:, 1024 * j + 512 * g:1024 * j + 512 * g + 512],
                                   c == 0, c == KD - 1))
                    m.append(P.mms(ps, w_in, act))
                ring_over(i, 8 + q, m[1])
            last["actt"] = m[1]
            if i == N_EXP - 1:
                halves = [slice(0, 64), slice(64, 128)]
                ymark[i] = [V.tt(Y[x][h, :], PC[h, :], HALF[h, :], ALU.mult, m[g], y_free[x], TT["half"])
                            for g, h in enumerate(halves)]
            else:
                y = V.tt(Y[x][:, :], PC[:, :], HALF[:, :], ALU.mult, m[1], y_free[x], TT["half"])
                ymark[i], free["C"] = [y, y], y

        def biases():
            b2_in = G.tt(b2s[0:32, :], b2s[0:32, :], GAIN[0:32, :], ALU.mult, b_in, TT["gf"])
            m = P.turn([(PC[:, 128 * t:128 * t + 128], RT[t][:, 248:376]) for t in range(NT)], ident[:, :],
                       *(state[t]["gp"] for t in range(NT)), free["C"])
            free["C"] = gt = A.act(GT[0:32, :], PC[0:32, 0:256], ACT.Copy, m, scale=2.0)
            P.mms([(ACC[t][g][:, :], GT[0:32, 128 * t:128 * t + 128], b2s[0:32, 512 * g:512 * g + 512], False, False)
                   for t in range(NT) for g in range(2)], gt, b2_in)

        own, before_, with_, one_ = (EX[:, 32 * i:32 * i + 32] for i in range(4))

        def count_extra():
            m = P.mms([(PM[:, 0:32], ones[:, 0:1].to_broadcast([128, 128]), RT[t][:, 32:64], t == 0, t == NT - 1)
                       for t in range(NT)], state[0]["sel"], state[1]["sel"], free["M"])
            v = V.ts(own, PM[:, 0:32], 64.0, None, ALU.is_gt, None, m)
            for bound in (128.0, 192.0):
                v = V.stt(own, PM[:, 0:32], bound, own, ALU.is_gt, ALU.add, v)
            free["M"] = v
            o = V.memset(one_, 1.0)
            v = V.put(lambda e: e.tensor_tensor_scan(with_, one_, own, 0.0, op0=ALU.mult, op1=ALU.add), v, o)
            return V.tt(before_, with_, own, ALU.subtract, v), V.copy(EXI[:, 0:1], with_[:, 31:32], v)

        def extra_items(summed, n_extra):
            engines = (S, V, A, P)
            kept = dict(free), dict(last), list(sel_free), list(selt_free), list(xe_free), list(y_free)
            for name, q in zip(("sp", "dve", "act", "pe"), engines):
                q.read("n", EXI[0:1, 0:1], 0, N_EXTRA, n_extra)
                q.only_if_more("n", 0)
                q.enter(sem(f"{name}_extra"))
            bias_slot = [sem("extra_b_in"), 0]
            num, pos, weight, tmp = EX[:, 128:129], EX[:, 129:131], EX[:, 131:133], EX[:, 224:256]
            pos_of = [EX[:, 160 + 32 * t:192 + 32 * t] for t in range(NT)]
            v = V.ts(tmp, before_, 64.0, -64.0, ALU.mult, ALU.add, summed)
            for t in range(NT):
                v = V.tt(pos_of[t], RT[t][:, 64:96], tmp, ALU.add, v)
            for i in range(N_EXTRA):
                e = N_EXP + i
                if i:
                    for q in engines:
                        q.only_if_more("n", i)
                v = V.ts(tmp, with_, float(i), None, ALU.is_le, None, v)
                v = V.reduce(num, tmp, ALU.add, v)
                number = V.copy(EXI[:, 1 + i:2 + i], num, v)
                v = V.stt(one_, before_, float(i), tmp, ALU.is_le, ALU.subtract, v)
                for t in range(NT):
                    for out, src in ((pos, pos_of[t]), (weight, RT[t][:, 248:280])):
                        v = V.tt(tmp, src, one_, ALU.mult, v)
                        v = V.reduce(out[:, t:t + 1], tmp, ALU.add, v)
                v = V.ts(pos, pos, -64.0 * i, None, ALU.add, None, v)
                S.read("e", EXI[0:1, 1 + i:2 + i], 0, N_EXP - 1, number)
                bias_in = S.load(bias_slot, b1s[32:33, :], lambda: a["b1"][bass.ds(S.regs["e"], 1)], last["bias"])
                for k in range(4):
                    extra_load(12 * i + k)
                sel[e] = [select(0, t, pos[:, t:t + 1], weight[:, t:t + 1], sel_free[0], last["selw"], v) for t in range(NT)]
                v = sel[e][1][1]
                gather(e, 0)
                turn_weights(e, 2)
                bias = bias_products(ones[32:33, 0:1].to_broadcast([1, 64]), b1s[32:33, :], bias_in, free["A"], free["B"])
                act = turn_act(first_layer(e, 0, bias))
                second_layer(e, 2, act)
                scatter(e, 2, False)
            for q in engines:
                for i in range(N_EXTRA):
                    q.end()
                q.leave()
            free.update(kept[0])
            last.update(kept[1])
            for now, then in zip((sel_free, selt_free, xe_free, y_free), kept[2:]):
                now[:] = then

        extra_sem = [[sem(f"extra_in{i}"), 0] for i in range(4)]
        sel[0] = [state[t]["selected"] for t in range(NT)]
        gather_first()
        turn_weights(0, 0)
        for e in range(N_EXP):
            x = e % 2
            if e + 1 < N_EXP:
                sel[e + 1] = [select_expert(e + 1, t, sel_free[1 - x], last["selw"]) for t in range(NT)]
            if e == N_EXP - 1:
                extra_items(*counted)
            glu = first_layer(e, x, add_bias(e, b_in, free["A"], free["B"]) if e else None)
            if e:
                scatter(e - 1, 1 - x, False)
            if e == 4:
                biases()
            if e + 1 < N_EXP:
                gather(e + 1, 1 - x)
            act = turn_act(glu)
            if e + 1 < N_EXP:
                turn_weights(e + 1, 1 - x)
            second_layer(e, x, act)
            if e == 4:
                counted = count_extra()
        outs = []
        for g in range(2):
            for t in range(NT):
                m = scatter(N_EXP - 1, x, True, [(t, g)])
                outs.append((t, g, (A if t else V).copy(X[t][:, 512 * g:512 * g + 512], ACC[t][g][:, :], m)))
        return outs

    mix_start = []

    def region_until(region, layer):
        return mix_start[layer] + (2 if region else -LEAD)

    for layer in range(DEPTH):
        def ffn_chunks(up, down, more=()):
            for g in range(NG + 1):
                if g < NG:
                    chunk_add(up[layer, 2 * g], up[layer, 2 * g + 1])
                if g:
                    chunk_add(down[layer, g - 1])
                for src in more[g - 1:g] if 0 < g < NG else more[NG - 1:] if g == NG else ():
                    chunk_extra(src)

        ffn_chunks(a["up1"], a["down1"], [a["w_ada"][12 + i] for i in range(12 * layer)])
        mix_start.append(len(chunks))
        chunk_add(*(a["w_in_a"][layer, i] for i in range(2)))
        chunk_add(*(a["w_in_b"][layer, i] for i in range(6)))
        chunk_add(a["w_in_c"][layer])
        for n in range(4):
            chunk_add(*(a["w_gate"][layer, 4 * n + i] for i in range(4)))
            chunk_add(a["w_branch"][layer, n])
        chunk_add(*(a["w_out"][layer, i] for i in range(4)))
        chunk_add(*(a["w_ple"][layer, i] for i in range(2)))
        chunk_add(*(a["w_ple_gate"][layer, i] for i in range(4)))
        ffn_chunks(a["up2"], a["down2"], [a["w_ada"][i] for i in range(12 - 12 * layer)])
    mix_start.append(len(chunks))
    chunk_add(*(a["w_in2"][i] for i in range(8)))
    chunk_add(a["w_in2_kv"])
    chunk_add(*(a["w_in2"][i] for i in range(8, 12)))
    for n in range(3):
        chunk_add(*(a["w_gate2"][4 * n + i] for i in range(4)))
        chunk_add(*(a["w_branch2"][2 * n + i] for i in range(2)))
    chunk_add(*(a["w_out2"][i] for i in range(4)))

    b_in, layer_banks = [], []
    row2 = [sem("rows2_in"), 0]
    one = [sem("const_in"), 0]
    small_slot = [sem("small_in"), 0]
    small_users = []
    rows_mark = [None]
    rows_free = [plan.later() for _ in range(NT)]
    rows_mix, rows_ffn = plan.later(), plan.later()
    HT = [[C[1][n] for n in names] for names in (("aa", "dk"), ("kt", "dv"))]
    shift_f = C[1]["big"][:, 0:1024]

    def load_small(layer):
        for out, name in ((sgu_w, "sgu_w"), (sgu_b, "sgu_b"), (pool_w, "pool_w"), (w_uq, "w_uq"), (w_ukv, "w_ukv")):
            G.load(small_slot, out[:, :], a[name][layer], *small_users)
        for out, name in ((sgu_g, "sgu_ln_g"), (sgu_bb, "sgu_ln_b"), (pool_s, "pool_scale"), (q_gain, "mla_q_norm"),
                          (kv_gain, "mla_kv_norm")):
            m = G.load(small_slot, out[:, :], rows(a[name][layer]), *small_users)
        CONST["small"] = m

        def mask():
            yield 20.0
            w = sgu_w[:, :].rearrange("p (g t) -> p g t", g=4)
            CONST["tril"] = V.tt(w, w, tril[:, :].unsqueeze(1).to_broadcast([128, 4, 128]), ALU.mult, m, CONST["all"])

        plan.start(mask(), m)

    def setup():
        CONST["ident"] = S.load([sem("ident_in"), 0], ident[:, :], a["ident"])
        for r in range(2):
            region_open(r, region_until(r, 0))
        load_first()
        load_ahead()
        state[1]["x_in"] = [S.load([sem("x_in1"), 0], X[1][:, :], a["x"][128:256])] * 2

    def setup_late():
        while at[0] < 10:
            yield 0.5
        rows_mark[0] = load_rows(a["ln1_g"][0], a["ln1_b"][0])
        for out, name in ((cond_t, "cond"), (b_ada, "b_ada"), (norms, "norms"), (ones, "ones"), (iota, "iota"), (freq, "freq"),
                          (pos_i, "pos"), (tril, "tril"), (decay, "decay"), (band, "band")):
            m = G.load(one, out[:, :], a[name], P.mark())
        CONST["all"] = m
        load_small(0)
        while at[0] < 12:
            yield 0.5
        yield m
        yield 15.0
        ada["cond"] = A.act(cond_t[:, :], cond_t[:, :], ACT.Silu, m)
        yield from setup_rope()

    def setup_rope():
        m = CONST["all"]
        m = V.copy(pos_f[:, :], pos_i[:, :], m)
        for t in range(NT):
            yield m
            m = V.ts(ang[:, 48 * t:48 * t + 48], freq[:, :], pos_f[:, t:t + 1], None, ALU.mult, None, m)
        big = 12582912.0
        yield m
        m = V.ts(turns, ang, float(np.float32(1 / (2 * math.pi))), big, ALU.mult, ALU.add, m)
        yield m
        m = V.ts(turns, turns, big, None, ALU.subtract, None, m)
        rest = 2 * math.pi
        for bits in (9, 11, 24):
            unit = 2.0 ** (bits - 2 - math.floor(math.log2(rest)))
            part = float(np.float32(rest)) if bits == 24 else math.floor(rest * unit) / unit
            rest -= part
            yield m
            m = V.stt(ang, turns, -part, ang, ALU.mult, ALU.add, m)
        lim = 3.1415925
        yield m
        c0 = V.ts(sin[:, :], ang, -lim, lim, ALU.max, ALU.min, m)
        m = V.ts(cos[:, :], ang, math.pi / 2, None, ALU.add, None, m)
        yield m
        m = V.ts(turns, cos[:, :], math.pi, -2 * math.pi, ALU.is_gt, ALU.mult, m)
        yield m
        m = V.tt(cos[:, :], cos[:, :], turns, ALU.add, m)
        yield m
        m = V.ts(cos[:, :], cos[:, :], -lim, lim, ALU.max, ALU.min, m)
        yield m
        A.act(sin[:, :], sin[:, :], ACT.Sin, c0, m)
        CONST["rope"] = A.act(cos[:, :], cos[:, :], ACT.Sin, m)

    def mix_rows():
        for u in range(NT):
            for f in state[u]["added"]:
                yield f
        users = [state[u]["gate_free"] for u in range(NT)]
        G.load(row2, GATE[0][:, :], rows(mods[1]), ada["rows"][1], *users)
        rows_mix.set(G.load(row2, GATE[1][:, :], rows(mods[0]), ada["rows"][0], *users))

    def first_mixers_over(side):
        yield side
        marks = [q.mark() for q in (P, V, A, G)]
        for i in range(N_SLOT + 4, N_SLOT + 6):
            ring_fill(i, *marks)

    def mixers_over(side):
        yield side
        marks = [q.mark() for q in (P, V, A, G)]
        m = G.load(row2, shift_f, rows(mods[3]), ada["rows"][3], *marks)
        rows_ffn.set(m)
        half_slot = [sem("half_in"), 0]
        for h in range(2):
            TT["half"] = G.load(half_slot, HALF[64 * h:64 * h + 64, :], rows(mods[5, 512 * h:512 * h + 512], 64),
                                ada["rows"][5], *marks)
        G.load(b_slot, b1s[0:32, :], a["b1"], *marks)
        b_in.append(G.load(b_slot, b2s[0:32, :], a["b2"], *marks))
        while n_loaded[0] < len(stream):
            yield 0.5
        for i in range(N_SLOT + 6, NRING):
            ring_fill(i, *marks)

    def tile(t):
        s = state[t]
        ready = s["x_in"]
        order = [("ln1_g", "ln1_b"), ("ln2_g", "ln2_b"), ("ln3_g", "ln3_b")]

        def transposed():
            done, m = yield from xt_from(t, X[t], ready, s["xt_free"])
            s["x"] = scale_x(t, m, *ready)
            return done

        def norm(layer, i):
            nonlocal ready
            ready, s["acc_free"] = yield from layer_norm(t, 0.5, s["down"], s["x"], rows_mark[0])
            s["b1_free"] = s["acc_free"]
            if t == 1:
                rows_users[:] = [ready[1]]
                i, layer = (i + 1, layer) if i < 2 else (0, layer + 1)
                if layer < DEPTH:
                    rows_mark[0] = load_rows(*(a[n][layer] for n in order[i]))
                else:
                    rows_mark[0] = load_rows(mods[2], mods[4], ada["rows"][2], ada["rows"][4])

        for layer in range(DEPTH):
            done = yield from transposed()
            yield from ffn(t, done)
            yield from norm(layer, 0)
            done = yield from transposed()
            yield from mix(t, layer, done)
            yield from norm(layer, 1)
            if t == 1:
                small_users[:] = [s["acc_free"]]
                if layer + 1 < DEPTH:
                    load_small(layer + 1)
                else:
                    load_second()
            done, s["added"] = yield from ple(t, transposed)
            if t == 1 and layer == DEPTH - 1:
                plan.start(mix_rows())
            yield from ffn(t, done, s["added"])
            yield from norm(layer, 2)
        m = yield rows_mix
        h, q = yield from rms(t, GATE[0], GATE[1], MERGED[t], ready, ACC[t], s["acc_free"], m, *s["act_free"])
        s["acc_free"] = s["b1_free"] = q
        rows_free[t].set(h[1])
        done, s["h_turned"] = yield from xt_from(t, MERGED[t], h, s["xt_free"])
        yield from hybrid(t, done)
        if t == 1:
            marks = [q.mark() for q in (P, V, A, G)]
            for i in range(N_SLOT, N_SLOT + 4):
                ring_fill(i, *marks)
            for _ in range(2):
                layer_banks.append((yield from take()))
        out = []
        for i in range(2):
            c = slice(512 * i, 512 * i + 512)
            yield s["down"][i]
            y = V.stt(MERGED[t][:, c], ACC[t][i][:, :], 0.5, GAIN[:, c], ALU.mult, ALU.mult, s["down"][i], rows_mark[0],
                      s["merged_free"])
            out.append(V.tt(X[t][:, c], X[t][:, c], MERGED[t][:, c], ALU.add, y, *ready))
        s["acc_free"], s["x_done"] = y, out
        if t == 1:
            yield out
            TT["gf"] = G.load([sem("gf_in"), 0], GAIN[0:32, :], rows(mods[5], 32), *out)
            add_bias(0, b_in[0], *(m for _, m in layer_banks))
            for u in range(NT):
                add_x(u)
        m = yield rows_ffn
        h, _ = yield from rms(t, BIAS, shift_f, MERGED[t], out, HT[t], m, rows_mark[0])
        yield from route(t, h)

    setup()
    plan.start(splitter())
    plan.start(setup_late())
    for t in range(NT):
        plan.start(tile(t))
    plan.run()

    written = []
    for t, g, m in experts(b_in[0]):
        c = slice(512 * g, 512 * g + 512)
        written.append(S.load([sem(f"out_done{t}{g}"), 0], a["out"][128 * t:128 * t + 128, c], X[t][:, c], m))
    S.items.append((tuple(written), None, None, 0))

    with nc.Block() as block:
        @block.sync
        def _(e):
            S.replay(e)

        @block.tensor
        def _(e):
            P.replay(e)

        @block.vector
        def _(e):
            V.replay(e)

        @block.scalar
        def _(e):
            A.replay(e)

        @block.gpsimd
        def _(e):
            G.replay(e)

    top.close()


def chunked(w, groups, width, per):
    n = w.shape[0] // (128 * per)
    return w.reshape(n, per, 128, groups, width).transpose(3, 0, 2, 1, 4).reshape(groups * n, 128, per * width)


def wide(w):
    n = w.shape[0] // 256
    return w.reshape(n, 2, 128, 2, D // 2).transpose(0, 2, 3, 1, 4).reshape(n, 128, 2 * D)


def layout_up(w):
    k = w.shape[0]
    return chunked(w.reshape(k, 2, NG, 256).transpose(0, 2, 1, 3).reshape(k, -1), NG, 512, 4)


ORDER = (0, 2, 1, 3)


def layout_first(v):
    each = range(DEPTH)
    out = {}

    def stack(f):
        return np.ascontiguousarray(np.stack([f(i) for i in each]))

    out["x"] = v["x"].reshape(SEQ, D)
    out["pos"] = np.ascontiguousarray(v["positions"].reshape(NT, 128).T)
    for n in ("1", "2"):
        out["up" + n] = stack(lambda i: layout_up(v[f"ffn{n}_up"][i]))
        out["down" + n] = stack(lambda i: wide(v[f"ffn{n}_down"][i]))
    w = v["w_in"]
    out["w_in_a"] = stack(lambda i: chunked(w[i][:, 1792:2208], 1, 416, 4))
    out["w_in_b"] = stack(lambda i: np.concatenate([chunked(w[i][:, 512:1536], 2, 512, 4), chunked(w[i][:, 0:512], 1, 512, 4)]))
    out["w_in_c"] = stack(lambda i: chunked(w[i][:, 1536:1792], 1, 256, 8)[0])
    out["w_gate"] = stack(lambda i: np.concatenate(
        [chunked(w[i][:, 2208 + 1024 * n:3232 + 1024 * n], 2, 512, 4) for n in ORDER]))
    out["w_branch"] = stack(lambda i: np.concatenate([wide(v["w_branch"][i, n]) for n in ORDER]))
    out["w_out"] = stack(lambda i: wide(v["w_out"][i]))

    def ple(i):
        p = v["p"][i, 0].T.reshape(2, 128, SEQ).transpose(1, 0, 2).reshape(128, 2 * SEQ)
        w = v["w_ple"][i].reshape(2, 128, 2, 512).transpose(2, 1, 0, 3).reshape(2, 128, 1024)
        return np.stack([np.concatenate([p, w[h]], axis=1) for h in range(2)])

    out["w_ple"] = stack(ple)
    out["w_ple_gate"] = stack(lambda i: chunked(v["w_ple_gate"][i], 2, 512, 4))
    out["sgu_w"] = stack(lambda i: v["sgu_w"][i].transpose(2, 0, 1).reshape(128, 512))
    out["sgu_b"] = stack(lambda i: v["sgu_b"][i].T)

    def pool(i):
        w = np.zeros((2, 2, 64, 2, 64), np.float32)
        for g in range(4):
            w[g // 2, g % 2, :, g % 2, :] = v["pool_w"][i, g]
        return w.reshape(2, 128, 128).transpose(1, 0, 2).reshape(128, 256)

    out["pool_w"] = stack(pool)
    out["w_uq"] = stack(lambda i: v["mla_w_uq"][i].reshape(2, 128, 384).transpose(1, 0, 2).reshape(128, 768))
    out["w_ukv"] = v["mla_w_ukv"]
    for n in ("ln1_g", "ln1_b", "ln2_g", "ln2_b", "ln3_g", "ln3_b", "sgu_ln_g", "sgu_ln_b", "pool_scale", "mla_q_norm",
              "mla_kv_norm"):
        out[n] = v[n]
    return out


def layout_second(v):
    out = {}
    w = v["w_in_2"][0]
    cut = np.cumsum([0, 512, 512, 512, 512, 512, 512, 128, 128])
    xr, gr, dq, dk, dv, sq, sk, sv = (w[:, cut[i]:cut[i + 1]] for i in range(8))
    sq = sq.reshape(D, 2, 4, 64).transpose(0, 2, 1, 3).reshape(D, 512)
    out["w_in2"] = np.concatenate([chunked(x, 1, 512, 4) for x in (xr, gr, dq, dk, sq, dv)])
    out["w_in2_kv"] = chunked(np.concatenate([sk, sv], axis=1), 1, 256, 8)[0]
    out["w_gate2"] = chunked(w[:, 3328:], 6, 512, 4)
    wb = v["w_branch_2"][0]
    swa = wb[2].reshape(2, 4, 64, D).transpose(1, 0, 2, 3).reshape(512, D)
    out["w_branch2"] = np.concatenate([wide(x) for x in (wb[0], wb[1], swa)])
    out["w_out2"] = wide(v["w_out_2"][0])
    out["w_ada"] = v["w_ada_2"][0].reshape(4, 2, 128, 6, D).transpose(3, 0, 2, 1, 4).reshape(24, 128, 2 * D)
    out["b_ada"] = v["b_ada_2"].reshape(6, KD, 128).transpose(2, 0, 1).reshape(128, 6 * KD)
    out["cond"] = v["c_2"].reshape(KD, 128).T
    out["norms"] = np.stack([v["norm_mix_2"][0], v["norm_ffn_2"][0]]).reshape(2, KD, 128).transpose(2, 0, 1).reshape(128, 2 * KD)
    out["conv_w"] = v["conv_w_2"][0].reshape(4, 4, 128).transpose(2, 1, 0).reshape(128, 16)
    for n in ("conv_b", "lru_ba", "lru_bx", "lru_lambda"):
        out[n] = v[n + "_2"].reshape(4, 128).T
    for n, name in (("lru_a", "lru_wa_2"), ("lru_x", "lru_wx_2")):
        w = np.zeros((2, 64, 4, 2, 64), np.float32)
        for h in range(8):
            w[h % 2, :, h // 2, h % 2, :] = v[name][0, h]
        out[n] = w.reshape(128, 512)
    for n in ("diff_qnorm", "diff_knorm", "swa_qnorm", "swa_knorm", "diff_subln", "swa_sinks"):
        out[n] = v[n + "_2"][0]
    out["diff_lambda"] = v["diff_lambda_2"].reshape(256)
    rb = v["rel_bias_2"]
    out["rel_bias"] = np.concatenate([rb[:, 0:4], rb[:, 4:].reshape(32, 2, 4).transpose(0, 2, 1).reshape(32, 8)], axis=1)
    out["w_router"] = v["w_router_2"][0].reshape(KD, 128, N_EXP).transpose(1, 0, 2).reshape(128, KD * N_EXP)
    out["b_router"] = v["b_router_2"][0]
    out["w1"] = v["w1_2"][0].reshape(N_EXP, KD, 128, D, 2).transpose(0, 1, 2, 4, 3).reshape(N_EXP, KD, 128, 2 * D)
    out["b1"] = v["b1_2"][0].reshape(N_EXP, D, 2).transpose(0, 2, 1).reshape(N_EXP, 2 * D)
    out["w2"] = v["w2_2"][0].reshape(N_EXP, 4, 2, 128, D).transpose(0, 1, 3, 2, 4).reshape(N_EXP, 4, 128, 2 * D)
    out["b2"] = v["b2_2"][0]
    return out


def constants_second():
    out = {"ones": np.ones((128, 1), np.float32)}
    dist = 255 - np.arange(384)
    near = np.maximum(dist, 0)
    ratio = np.log(np.maximum(near, 1).astype(np.float32) / np.float32(16)) / np.float32(math.log(128 / 16))
    bucket = np.where(near < 16, near, np.minimum(16 + (ratio * np.float32(16)).astype(np.int32), 31))
    out["buckets"] = (np.arange(32)[:, None] == bucket[None, :]).astype(np.float32)
    future = np.where(dist < 0, MASKED, 0.0)[None, :].repeat(12, axis=0)
    future[4:, dist >= 128] = MASKED
    out["future"] = future.astype(np.float32)
    out["before"] = np.triu(np.ones((128, 128), np.float32), 1)
    out["iota"] = np.tile(np.arange(64, dtype=np.float32), (128, 2))
    return out


def constants_first():
    out = {"ident": np.eye(128, dtype=np.float32), "tril": np.triu(np.ones((128, 128), np.float32))}
    j, i = np.arange(128)[:, None], np.arange(128)[None, :]
    decay = np.zeros((128, 2, 2, 2, 128))
    for h in range(4):
        log_gamma = math.log1p(-2.0 ** (-5 - h))
        decay[:, h % 2, 0, h // 2] = np.exp(log_gamma * (128 + i - j))
        decay[:, h % 2, 1, h // 2] = np.where(j // 64 <= i // 64, np.exp(log_gamma * abs(i - j)), 0.0)
    out["decay"] = (decay * 0.125).astype(np.float32).reshape(128, 1024)
    band = np.zeros((128, 1088), np.float64)
    for g, window in enumerate((2, 4, 8, 16)):
        near = (j <= i) & (j > i - window)
        own = np.where(near, 1.0 / np.minimum(i + 1, window), 0.0) - (i == j)
        band[:, 128 * g:128 * g + 128] = own
        band[:, 512 + 128 * g:640 + 128 * g] = np.where(near, 1.0 / window, 0.0) - (i == j)
        t = np.arange(16)[None, :]
        band[:, 1024 + 16 * g:1040 + 16 * g] = np.where(j > 128 + t - window, 1.0 / window, 0.0)
    out["band"] = band.astype(np.float32)
    freq = [10000.0 ** (-(np.arange(0, n, 2, dtype=np.float32) / np.float32(n)).astype(np.float64)) for n in (64, 32)]
    out["freq"] = np.repeat(np.concatenate(freq).astype(np.float32)[None], 128, axis=0)
    return out


def kernel(**inputs):
    import concourse.bacc as _bacc
    from concourse.bass_utils import run_bass_kernel_spmd as _run

    arrays = {**layout_first(inputs), **layout_second(inputs), **constants_first(), **constants_second()}
    arrays = {name + "_dram": np.ascontiguousarray(x) for name, x in arrays.items()}
    nc = _bacc.Bacc("TRN2", target_bir_lowering=False, num_devices=1, dynamic_dma_scratch_size=4096)
    aps = {name[:-5]: nc.dram_tensor(name, x.shape, mybir.dt.from_np(x.dtype), kind="ExternalInput").ap()
           for name, x in arrays.items()}
    aps["out"] = nc.dram_tensor("out_dram", (SEQ, D), F32, kind="ExternalOutput").ap()
    program(nc, aps)
    r = _run(nc, [arrays], core_ids=[0])
    return r.results[0]["out_dram"].reshape(1, SEQ, D)
```
